# Optimizing a Trainium2 kernel written in Bass

```python
import math
import jax, jax.numpy as jnp
from jax import lax
import numpy as np

D_MODEL = 1024
BATCH = 1
SEQ = 256
DEPTH = 1

SSD_EXPAND = 2
SSD_D_INNER = SSD_EXPAND * D_MODEL
SSD_HEAD_DIM = 64
SSD_HEADS = SSD_D_INNER // SSD_HEAD_DIM
SSD_GROUPS = 4
SSD_HEADS_PER_GROUP = SSD_HEADS // SSD_GROUPS
SSD_STATE = 128
SSD_CONV = 4
SSD_CHUNK = 128
SSD_CONV_CH = SSD_D_INNER + 2 * SSD_GROUPS * SSD_STATE
SSD_DT_MIN = 0.001
SSD_DT_MAX = 0.1

DA_HEAD_DIM = 64
DA_HEADS = D_MODEL // (2 * DA_HEAD_DIM)
DA_V_DIM = 2 * DA_HEAD_DIM
DA_WIDTH = DA_HEADS * 2 * DA_HEAD_DIM
Q_BLOCK = 128

N_BRANCH = 2
D_FF = 2816
EPS = 1e-6

IN_SIZES = [SSD_D_INNER, SSD_CONV_CH, SSD_HEADS, DA_WIDTH, DA_WIDTH, DA_WIDTH, N_BRANCH * D_MODEL]
D_IN_PROJ = sum(IN_SIZES)
IN_SPLITS = np.cumsum(IN_SIZES)[:-1].tolist()


def rmsnorm(x, g):
    xf = x.astype(jnp.float32)
    y = xf * lax.rsqrt(jnp.mean(xf * xf, axis=-1, keepdims=True) + EPS)
    return y.astype(x.dtype) * g

def swiglu(x, w_gate, w_up, w_down):
    return (jax.nn.silu(x @ w_gate) * (x @ w_up)) @ w_down

def alibi_slopes(n_heads):
    return jnp.asarray(2.0 ** (-8.0 * np.arange(1, n_heads + 1) / n_heads), dtype=jnp.float32)

def causal_dwconv(x, w, b):
    k = w.shape[0]
    y = lax.conv_general_dilated(x, w[:, None, :], window_strides=(1,), padding=[(k - 1, 0)],
                                 dimension_numbers=("NWC", "WIO", "NWC"),
                                 feature_group_count=x.shape[-1])
    return y + b

def ssd_chunked(x, dt, a_head, bm, cm):
    b, L, H, P = x.shape
    G, N, E, Q = SSD_GROUPS, SSD_STATE, SSD_HEADS_PER_GROUP, SSD_CHUNK
    nc = L // Q
    X = (x.astype(jnp.float32) * dt[..., None]).reshape(b, nc, Q, G, E, P)
    a = (dt * a_head).reshape(b, nc, Q, G, E).transpose(0, 3, 4, 1, 2)
    Bc = bm.astype(jnp.float32).reshape(b, nc, Q, G, N)
    Cc = cm.astype(jnp.float32).reshape(b, nc, Q, G, N)
    a_cum = jnp.cumsum(a, axis=-1)
    seg = a_cum[..., :, None] - a_cum[..., None, :]
    causal = jnp.tril(jnp.ones((Q, Q), dtype=bool))
    Lmat = jnp.exp(jnp.where(causal, seg, -jnp.inf))
    CB = jnp.einsum('bclgn,bcsgn->bgcls', Cc, Bc)
    y_diag = jnp.einsum('bgcls,bgecls,bcsgep->bclgep', CB, Lmat, X)
    decay_states = jnp.exp(a_cum[..., -1:] - a_cum)
    states = jnp.einsum('bclgn,bgecl,bclgep->bcgepn', Bc, decay_states, X)
    chunk_decay = jnp.exp(a_cum[..., -1])

    def step(h, inp):
        s, d = inp
        return h * d[..., None, None] + s, h

    _, prev = lax.scan(step, jnp.zeros(states.shape[:1] + states.shape[2:], jnp.float32),
                       (jnp.moveaxis(states, 1, 0), jnp.moveaxis(chunk_decay, 3, 0)))
    prev = jnp.moveaxis(prev, 0, 1)
    y_off = jnp.einsum('bclgn,bcgepn,bgecl->bclgep', Cc, prev, jnp.exp(a_cum))
    return (y_diag + y_off).reshape(b, L, H, P)

def ssd_branch(z, xbc, dt_raw, conv_w, conv_b, dt_bias, a_log, d_skip, norm_g, w_branch):
    b, L, _ = z.shape
    xbc = jax.nn.silu(causal_dwconv(xbc, conv_w, conv_b))
    xs, bm, cm = jnp.split(xbc, [SSD_D_INNER, SSD_D_INNER + SSD_GROUPS * SSD_STATE], axis=-1)
    dt = jax.nn.softplus(dt_raw.astype(jnp.float32) + dt_bias.astype(jnp.float32))
    a_head = -jnp.exp(a_log.astype(jnp.float32))
    xh = xs.reshape(b, L, SSD_HEADS, SSD_HEAD_DIM)
    y = ssd_chunked(xh, dt, a_head,
                    bm.reshape(b, L, SSD_GROUPS, SSD_STATE), cm.reshape(b, L, SSD_GROUPS, SSD_STATE))
    y = (y + d_skip.astype(jnp.float32)[:, None] * xh.astype(jnp.float32)).astype(z.dtype)
    y = y.reshape(b, L, SSD_D_INNER) * jax.nn.silu(z)
    y = rmsnorm(y.reshape(b, L, SSD_GROUPS, SSD_D_INNER // SSD_GROUPS), 1.0).reshape(b, L, SSD_D_INNER) * norm_g
    return y @ w_branch

def diff_attn_branch(q, k, v, lq1, lk1, lq2, lk2, subln_g, w_branch, lam_init):
    b, L, _ = q.shape
    H, d = DA_HEADS, DA_HEAD_DIM
    q = q.reshape(b, L, H, 2, d)
    k = k.reshape(b, L, H, 2, d)
    v = v.reshape(b, L, H, DA_V_DIM)
    lam = (jnp.exp(jnp.sum(lq1.astype(jnp.float32) * lk1.astype(jnp.float32)))
           - jnp.exp(jnp.sum(lq2.astype(jnp.float32) * lk2.astype(jnp.float32))) + lam_init)
    slopes = alibi_slopes(H)
    scale = 1.0 / math.sqrt(d)
    nb = L // Q_BLOCK
    qb = q.reshape(b, nb, Q_BLOCK, H, 2, d).transpose(1, 0, 2, 3, 4, 5)
    key_pos = jnp.arange(L)

    def one_block(args):
        q_blk, i = args
        q_pos = i * Q_BLOCK + jnp.arange(Q_BLOCK)
        s = jnp.einsum('bqhmd,bkhmd->bhmqk', q_blk, k).astype(jnp.float32) * scale
        dist = (q_pos[:, None] - key_pos[None, :]).astype(jnp.float32)
        s = s - slopes[None, :, None, None, None] * dist
        s = jnp.where(dist >= 0, s, -jnp.inf)
        p = jax.nn.softmax(s, axis=-1)
        attn = p[:, :, 0] - lam * p[:, :, 1]
        return jnp.einsum('bhqk,bkhe->bqhe', attn.astype(v.dtype), v)

    out = lax.map(one_block, (qb, jnp.arange(nb)))
    out = out.transpose(1, 0, 2, 3, 4).reshape(b, L, H, DA_V_DIM)
    out = rmsnorm(out, subln_g) * (1.0 - lam_init)
    return out.reshape(b, L, DA_WIDTH) @ w_branch

def first_inputs(seed: int = 0) -> dict:
    key = jax.random.key(seed)
    ks = iter(jax.random.split(key, 40))
    f32 = jnp.float32

    def nrm(shape, fan_in):
        return jax.random.normal(next(ks), (DEPTH,) + shape, f32) * fan_in ** -0.5

    def gain(n):
        return 1.0 + 0.05 * jax.random.normal(next(ks), (DEPTH, n), f32)

    x = jax.random.normal(next(ks), (BATCH, SEQ, D_MODEL), f32)
    dt0 = jnp.exp(jax.random.uniform(next(ks), (DEPTH, SSD_HEADS), f32)
                  * (math.log(SSD_DT_MAX) - math.log(SSD_DT_MIN)) + math.log(SSD_DT_MIN))
    dt0 = jnp.maximum(dt0, 1e-4)
    return {
        "x": x,
        "ffn1_pre_g": gain(D_MODEL),
        "ffn1_w_gate": nrm((D_MODEL, D_FF), D_MODEL),
        "ffn1_w_up": nrm((D_MODEL, D_FF), D_MODEL),
        "ffn1_w_down": nrm((D_FF, D_MODEL), D_FF),
        "ffn1_post_g": gain(D_MODEL),
        "mix_pre_g": gain(D_MODEL),
        "w_in": nrm((D_MODEL, D_IN_PROJ), D_MODEL),
        "gate_b": 0.02 * jax.random.normal(next(ks), (DEPTH, N_BRANCH * D_MODEL), f32),
        "ssd_conv_w": nrm((SSD_CONV, SSD_CONV_CH), SSD_CONV),
        "ssd_conv_b": 0.02 * jax.random.normal(next(ks), (DEPTH, SSD_CONV_CH), f32),
        "ssd_dt_bias": dt0 + jnp.log(-jnp.expm1(-dt0)),
        "ssd_A_log": jnp.log(jax.random.uniform(next(ks), (DEPTH, SSD_HEADS), f32, 1.0, 16.0)),
        "ssd_D": gain(SSD_HEADS),
        "ssd_norm_g": gain(SSD_D_INNER),
        "ssd_w_branch": nrm((SSD_D_INNER, D_MODEL), SSD_D_INNER),
        "da_lambda_q1": 0.1 * jax.random.normal(next(ks), (DEPTH, DA_HEAD_DIM), f32),
        "da_lambda_k1": 0.1 * jax.random.normal(next(ks), (DEPTH, DA_HEAD_DIM), f32),
        "da_lambda_q2": 0.1 * jax.random.normal(next(ks), (DEPTH, DA_HEAD_DIM), f32),
        "da_lambda_k2": 0.1 * jax.random.normal(next(ks), (DEPTH, DA_HEAD_DIM), f32),
        "da_subln_g": gain(DA_V_DIM),
        "da_w_branch": nrm((DA_WIDTH, D_MODEL), DA_WIDTH),
        "w_out": nrm((D_MODEL, D_MODEL), D_MODEL),
        "mix_post_g": gain(D_MODEL),
        "ffn2_pre_g": gain(D_MODEL),
        "ffn2_w_gate": nrm((D_MODEL, D_FF), D_MODEL),
        "ffn2_w_up": nrm((D_MODEL, D_FF), D_MODEL),
        "ffn2_w_down": nrm((D_FF, D_MODEL), D_FF),
        "ffn2_post_g": gain(D_MODEL),
    }

def first_block(x, ffn1_pre_g, ffn1_w_gate, ffn1_w_up, ffn1_w_down, ffn1_post_g,
              mix_pre_g, w_in, gate_b,
              ssd_conv_w, ssd_conv_b, ssd_dt_bias, ssd_A_log, ssd_D, ssd_norm_g, ssd_w_branch,
              da_lambda_q1, da_lambda_k1, da_lambda_q2, da_lambda_k2, da_subln_g, da_w_branch,
              w_out, mix_post_g,
              ffn2_pre_g, ffn2_w_gate, ffn2_w_up, ffn2_w_down, ffn2_post_g):
    h = x
    b, L, _ = x.shape
    for l in range(DEPTH):
        lam_init = 0.8 - 0.6 * math.exp(-0.3 * l)
        h = h + 0.5 * rmsnorm(swiglu(rmsnorm(h, ffn1_pre_g[l]), ffn1_w_gate[l], ffn1_w_up[l], ffn1_w_down[l]),
                              ffn1_post_g[l])
        u = rmsnorm(h, mix_pre_g[l])
        z, xbc, dt_raw, q, k, v, gate_logits = jnp.split(u @ w_in[l], IN_SPLITS, axis=-1)
        y_ssd = ssd_branch(z, xbc, dt_raw, ssd_conv_w[l], ssd_conv_b[l], ssd_dt_bias[l], ssd_A_log[l],
                           ssd_D[l], ssd_norm_g[l], ssd_w_branch[l])
        y_att = diff_attn_branch(q, k, v, da_lambda_q1[l], da_lambda_k1[l], da_lambda_q2[l], da_lambda_k2[l],
                                 da_subln_g[l], da_w_branch[l], lam_init)
        gates = jax.nn.sigmoid(gate_logits + gate_b[l]).reshape(b, L, N_BRANCH, D_MODEL)
        merged = gates[:, :, 0] * y_ssd + gates[:, :, 1] * y_att
        h = h + rmsnorm(merged @ w_out[l], mix_post_g[l])
        h = h + 0.5 * rmsnorm(swiglu(rmsnorm(h, ffn2_pre_g[l]), ffn2_w_gate[l], ffn2_w_up[l], ffn2_w_down[l]),
                              ffn2_post_g[l])
    return h


ROPE_THETA = 10000.0
BLOCK = 128

HEAD_DIM = 64
SWA_HEADS = 8
SWA_KV_HEADS = 2
SWA_GROUP = SWA_HEADS // SWA_KV_HEADS
WINDOW = 128

MLA_HEADS = 8
MLA_NOPE_DIM = 64
MLA_ROPE_DIM = 32
MLA_V_DIM = 64
MLA_QK_DIM = MLA_NOPE_DIM + MLA_ROPE_DIM
Q_LORA_RANK = 384
KV_LORA_RANK = 256

D_FF_2 = -(-8 * D_MODEL // (3 * 256)) * 256

IN_SIZES_2 = [
    SWA_HEADS * HEAD_DIM,
    SWA_KV_HEADS * HEAD_DIM,
    SWA_KV_HEADS * HEAD_DIM,
    Q_LORA_RANK,
    KV_LORA_RANK,
    MLA_ROPE_DIM,
    D_MODEL,
    D_MODEL,
]
IN_WIDTH = int(sum(IN_SIZES_2))
IN_OFFSETS = [int(v) for v in np.cumsum(IN_SIZES_2)[:-1]]


def rmsnorm_2(x, g):
    xf = x.astype(jnp.float32)
    xf = xf * lax.rsqrt(jnp.mean(xf * xf, axis=-1, keepdims=True) + EPS)
    return (xf * g.astype(jnp.float32)).astype(x.dtype)

def rope_tables(seq, dim):
    inv = ROPE_THETA ** (-jnp.arange(0, dim, 2, dtype=jnp.float32) / dim)
    ang = jnp.arange(seq, dtype=jnp.float32)[:, None] * inv[None, :]
    return jnp.cos(ang)[:, None, :], jnp.sin(ang)[:, None, :]

def apply_rope(x, cos, sin):
    xf = x.astype(jnp.float32)
    x1, x2 = jnp.split(xf, 2, axis=-1)
    out = jnp.concatenate([x1 * cos - x2 * sin, x2 * cos + x1 * sin], axis=-1)
    return out.astype(x.dtype)

def swa_sink_attention(q, k, v, sinks):
    B, S = q.shape[0], q.shape[1]
    nb = S // BLOCK
    qb = q.reshape(B, nb, BLOCK, SWA_KV_HEADS, SWA_GROUP, HEAD_DIM)

    def band(t):
        tp = jnp.pad(t, ((0, 0), (BLOCK, 0), (0, 0), (0, 0)))
        tb = tp.reshape(B, nb + 1, BLOCK, SWA_KV_HEADS, HEAD_DIM)
        return jnp.concatenate([tb[:, :-1], tb[:, 1:]], axis=2)

    kw, vw = band(k), band(v)
    s = jnp.einsum('bnqhgd,bnkhd->bnhgqk', qb, kw,
                   preferred_element_type=jnp.float32) * (HEAD_DIM ** -0.5)
    qi = jnp.arange(BLOCK)[:, None]
    kj = jnp.arange(2 * BLOCK)[None, :]
    diff = qi - kj + BLOCK
    band_ok = (diff >= 0) & (diff < WINDOW)
    kpos = jnp.arange(nb)[:, None] * BLOCK + kj - BLOCK
    mask = band_ok[None] & (kpos >= 0)[:, None, :]
    s = jnp.where(mask[None, :, None, None], s, -jnp.inf)
    sink = sinks.astype(jnp.float32).reshape(1, 1, SWA_KV_HEADS, SWA_GROUP, 1, 1)
    m = jnp.maximum(jnp.max(s, axis=-1, keepdims=True), sink)
    p = jnp.exp(s - m)
    denom = jnp.sum(p, axis=-1, keepdims=True) + jnp.exp(sink - m)
    p = (p / denom).astype(v.dtype)
    o = jnp.einsum('bnhgqk,bnkhd->bnqhgd', p, vw)
    return o.reshape(B, S, SWA_HEADS * HEAD_DIM)

def mla_attention(q_nope, q_rope, k_nope, k_rope, v):
    B, S = q_nope.shape[0], q_nope.shape[1]
    nb = S // BLOCK
    scale = MLA_QK_DIM ** -0.5
    kpos = jnp.arange(S)

    def to_blocks(t):
        return jnp.moveaxis(t.reshape(B, nb, BLOCK, *t.shape[2:]), 1, 0)

    def one_block(args):
        qn, qr, n = args
        s = (jnp.einsum('bqhd,bkhd->bhqk', qn, k_nope, preferred_element_type=jnp.float32)
             + jnp.einsum('bqhr,bkr->bhqk', qr, k_rope, preferred_element_type=jnp.float32)) * scale
        qpos = n * BLOCK + jnp.arange(BLOCK)
        causal = kpos[None, :] <= qpos[:, None]
        s = jnp.where(causal[None, None], s, -jnp.inf)
        p = jax.nn.softmax(s, axis=-1).astype(v.dtype)
        return jnp.einsum('bhqk,bkhd->bqhd', p, v)

    o = lax.map(one_block, (to_blocks(q_nope), to_blocks(q_rope), jnp.arange(nb)))
    return jnp.moveaxis(o, 0, 1).reshape(B, S, MLA_HEADS * MLA_V_DIM)

def second_inputs(seed: int = 0) -> dict:
    key = jax.random.key(seed)
    ks = jax.random.split(key, 17)
    f32 = jnp.float32

    def w(k, shape, fan_in):
        return jax.random.normal(k, shape, f32) * (fan_in ** -0.5)

    def gain(k, shape):
        return 1.0 + 0.02 * jax.random.normal(k, shape, f32)

    L = DEPTH
    return {
        "x": jax.random.normal(ks[0], (BATCH, SEQ, D_MODEL), f32),
        "mix_norm_g": gain(ks[1], (L, D_MODEL)),
        "w_in": w(ks[2], (L, D_MODEL, IN_WIDTH), D_MODEL),
        "swa_sinks": 0.5 * jax.random.normal(ks[3], (L, SWA_HEADS), f32),
        "q_norm_g": gain(ks[4], (L, Q_LORA_RANK)),
        "w_uq": w(ks[5], (L, Q_LORA_RANK, MLA_HEADS * MLA_QK_DIM), Q_LORA_RANK),
        "kv_norm_g": gain(ks[6], (L, KV_LORA_RANK)),
        "w_ukv": w(ks[7], (L, KV_LORA_RANK, MLA_HEADS * (MLA_NOPE_DIM + MLA_V_DIM)), KV_LORA_RANK),
        "w_o_swa": w(ks[8], (L, SWA_HEADS * HEAD_DIM, D_MODEL), SWA_HEADS * HEAD_DIM),
        "w_o_mla": w(ks[9], (L, MLA_HEADS * MLA_V_DIM, D_MODEL), MLA_HEADS * MLA_V_DIM),
        "w_out": w(ks[10], (L, D_MODEL, D_MODEL), D_MODEL),
        "ffn_norm_g": gain(ks[11], (L, D_MODEL)),
        "w_gate": w(ks[12], (L, D_MODEL, D_FF_2), D_MODEL),
        "w_up": w(ks[13], (L, D_MODEL, D_FF_2), D_MODEL),
        "w_down": w(ks[14], (L, D_FF_2, D_MODEL), D_FF_2),
        "final_norm_g": gain(ks[15], (D_MODEL,)),
    }

def second_block(x, mix_norm_g, w_in, swa_sinks, q_norm_g, w_uq, kv_norm_g, w_ukv,
              w_o_swa, w_o_mla, w_out, ffn_norm_g, w_gate, w_up, w_down, final_norm_g):
    B, S = x.shape[0], x.shape[1]
    cos_a, sin_a = rope_tables(S, HEAD_DIM)
    cos_b, sin_b = rope_tables(S, MLA_ROPE_DIM)

    for l in range(DEPTH):
        h = rmsnorm_2(x, mix_norm_g[l])
        proj = h @ w_in[l]
        qa, ka, va, q_lat, kv_lat, k_r, g_a, g_b = jnp.split(proj, IN_OFFSETS, axis=-1)

        qa = apply_rope(qa.reshape(B, S, SWA_HEADS, HEAD_DIM), cos_a, sin_a)
        ka = apply_rope(ka.reshape(B, S, SWA_KV_HEADS, HEAD_DIM), cos_a, sin_a)
        va = va.reshape(B, S, SWA_KV_HEADS, HEAD_DIM)
        o_a = swa_sink_attention(qa, ka, va, swa_sinks[l])

        cq = rmsnorm_2(q_lat, q_norm_g[l])
        qb = (cq @ w_uq[l]).reshape(B, S, MLA_HEADS, MLA_QK_DIM)
        q_nope, q_rope = jnp.split(qb, [MLA_NOPE_DIM], axis=-1)
        q_rope = apply_rope(q_rope, cos_b, sin_b)
        ckv = rmsnorm_2(kv_lat, kv_norm_g[l])
        kvb = (ckv @ w_ukv[l]).reshape(B, S, MLA_HEADS, MLA_NOPE_DIM + MLA_V_DIM)
        k_nope, vb = jnp.split(kvb, [MLA_NOPE_DIM], axis=-1)
        k_rope = apply_rope(k_r[:, :, None, :], cos_b, sin_b)[:, :, 0, :]
        o_b = mla_attention(q_nope, q_rope, k_nope, k_rope, vb)

        y = jax.nn.sigmoid(g_a) * (o_a @ w_o_swa[l]) + jax.nn.sigmoid(g_b) * (o_b @ w_o_mla[l])
        x = x + y @ w_out[l]

        h = rmsnorm_2(x, ffn_norm_g[l])
        x = x + (jax.nn.silu(h @ w_gate[l]) * (h @ w_up[l])) @ w_down[l]

    return rmsnorm_2(x, final_norm_g)


def setup_inputs(seed=0):
    out = dict(first_inputs(seed))
    for name, value in second_inputs(seed + 1).items():
        if name != "x":
            out[name + "_2"] = value
    return out


def reference(
    x, ffn1_pre_g, ffn1_w_gate, ffn1_w_up, ffn1_w_down, ffn1_post_g, mix_pre_g, w_in, gate_b,
    ssd_conv_w, ssd_conv_b, ssd_dt_bias, ssd_A_log, ssd_D, ssd_norm_g, ssd_w_branch,
    da_lambda_q1, da_lambda_k1, da_lambda_q2, da_lambda_k2, da_subln_g, da_w_branch, w_out,
    mix_post_g, ffn2_pre_g, ffn2_w_gate, ffn2_w_up, ffn2_w_down, ffn2_post_g, mix_norm_g_2,
    w_in_2, swa_sinks_2, q_norm_g_2, w_uq_2, kv_norm_g_2, w_ukv_2, w_o_swa_2, w_o_mla_2,
    w_out_2, ffn_norm_g_2, w_gate_2, w_up_2, w_down_2, final_norm_g_2,
):
    x = first_block(
        x, ffn1_pre_g, ffn1_w_gate, ffn1_w_up, ffn1_w_down, ffn1_post_g, mix_pre_g, w_in,
        gate_b, ssd_conv_w, ssd_conv_b, ssd_dt_bias, ssd_A_log, ssd_D, ssd_norm_g, ssd_w_branch,
        da_lambda_q1, da_lambda_k1, da_lambda_q2, da_lambda_k2, da_subln_g, da_w_branch, w_out,
        mix_post_g, ffn2_pre_g, ffn2_w_gate, ffn2_w_up, ffn2_w_down, ffn2_post_g,
    )
    return second_block(
        x, mix_norm_g_2, w_in_2, swa_sinks_2, q_norm_g_2, w_uq_2, kv_norm_g_2, w_ukv_2,
        w_o_swa_2, w_o_mla_2, w_out_2, ffn_norm_g_2, w_gate_2, w_up_2, w_down_2, final_norm_g_2,
    )


_drawn_inputs = setup_inputs


def setup_inputs(seed=0):
    import zlib

    import numpy as np

    out = dict(_drawn_inputs(seed))
    spreads = {}
    factors = {'gate_b': 8.0,
     'ssd_conv_b': 3.617,
     'ffn2_post_g': 3.24,
     'mix_norm_g_2': 8.0,
     'swa_sinks_2': 61.656,
     'q_norm_g_2': 8.0,
     'kv_norm_g_2': 8.0,
     'ffn_norm_g_2': 5.275,
     'final_norm_g_2': 8.237}
    for name, (base, spread) in spreads.items():
        noise = np.random.default_rng([zlib.crc32(name.encode()), seed]).standard_normal(out[name].shape)
        drawn = base * np.exp(spread * noise) if base else spread * noise
        out[name] = __import__('jax').numpy.asarray(drawn.astype(out[name].dtype))
    for name, factor in factors.items():
        out[name] = (out[name] * factor).astype(out[name].dtype)
    return out
```

```python
import math
from contextlib import ExitStack

import numpy as np
import concourse.bass as bass
from concourse import mybir

ALU = mybir.AluOpType
ACT = mybir.ActivationFunctionType
AX = mybir.AxisListType
F32 = mybir.dt.float32
F32R = mybir.dt.float32r
BF16 = mybir.dt.bfloat16

P = 128
D = 1024
KD = D // P
NT = 2
TOK = NT * P
D_FF = 2816
FF_STEPS = D_FF // 256
EPS = 1e-6
HIDE = -1e30
SSD_INNER, SSD_GROUPS, SSD_HEADS, SSD_P, SSD_N = 2048, 4, 32, 64, 128
HPG = SSD_HEADS // SSD_GROUPS
GW = HPG * SSD_P
CONV_K = 4
XBC_TILES = (SSD_INNER + 2 * SSD_GROUPS * SSD_N) // P
DA_HEADS = 8
LAM_INIT = 0.8 - 0.6 * math.exp(0.0)
SWA_HEADS, SWA_KV, HD = 8, 2, 64
MLA_HEADS, NOPE, ROPE, MLA_V = 8, 64, 32, 64
MLA_QK = NOPE + ROPE
Q_RANK, KV_RANK = 384, 256

RING = 3
UNIT = 2048
U_FFN1 = 0
U_XBC = U_FFN1 + 3 * FF_STEPS
U_DT = U_XBC + XBC_TILES // 2
U_Z = U_DT + 1
U_QKV = U_Z + 8
U_SSDW = U_QKV + 12
U_GATE = U_SSDW + 8
U_DAW = U_GATE + 8
U_WOUT = U_DAW + 4
U_FFN2 = U_WOUT + 4
U_IN2 = U_FFN2 + 3 * FF_STEPS
U_GATE2A = U_IN2 + 6
U_UQ = U_GATE2A + 2
U_UKV = U_UQ + 2
U_GATE2B = U_UKV + 1
U_OSWA = U_GATE2B + 6
U_OMLA = U_OSWA + 2
U_OUT2 = U_OMLA + 2
U_FFN3 = U_OUT2 + 4
U_END = U_FFN3 + 3 * FF_STEPS

C_XBC = SSD_INNER
C_DT = C_XBC + XBC_TILES * P
C_Q = C_DT + SSD_HEADS
C_GATE = C_Q + 3 * D
LAT0 = SWA_HEADS * HD + 2 * SWA_KV * HD
KR0 = LAT0 + Q_RANK + KV_RANK
PJ = KR0 + ROPE

GC = {}
_n = 0
for _name, _tiles in (("ffn1", KD), ("mix", KD), ("ffn2", KD), ("mix2", KD), ("ffn3", KD), ("q_lat", 3),
                      ("kv_lat", 2), ("subln", 1), ("conv_b", XBC_TILES), ("conv_w", CONV_K * XBC_TILES)):
    GC[_name] = _n
    _n += _tiles
N_COLS = _n
ROW = dict(dt_bias=0, a_log=32, skip=64, lam=96, sinks=96 + 4 * 64)
N_ROWS = ROW["sinks"] + SWA_HEADS


def tables():
    r, c = np.arange(P)[:, None], np.arange(P)[None, :]
    hide = lambda keep: np.where(keep, 0.0, HIDE)
    causal = hide(r >= c)
    near = np.where(r >= c, r - c, -HIDE)
    cols = dict(
        ident=np.eye(P), upto=r <= c, after=r > c,
        swa=np.concatenate([causal, hide(c > r), causal], 1),
        mla=np.concatenate([causal, np.zeros((P, P)), causal], 1),
        dist=np.concatenate([near, P + r - c, near], 1),
        causal_t=hide(r <= c),
    )
    for name, dim in (("a", HD), ("b", ROPE)):
        inv = np.float32(10000.0) ** (-np.arange(0, dim, 2, dtype=np.float32) / np.float32(dim))
        ang = (np.arange(TOK, dtype=np.float32)[:, None] * inv[None, :].astype(np.float32)).astype(np.float32)
        for f, fn in (("cos", np.cos), ("sin", np.sin)):
            t = fn(ang.astype(np.float64)).astype(np.float32)
            cols[f"{f}_{name}"] = t.reshape(NT, P, dim // 2).transpose(1, 0, 2).reshape(P, -1)
    at, n = {}, 0
    for k, v in cols.items():
        at[k] = (n, n + v.shape[1])
        n += v.shape[1]
    return np.concatenate([np.asarray(v, np.float32) for v in cols.values()], 1), at, n


TABLES, T_AT, N_TABLES = tables()


class Steps:

    def __init__(self, eng, sem):
        self.eng, self.sem, self.n = eng, sem, 0

    def inc(self, ins):
        self.n += 1
        ins.then_inc(self.sem, 1)
        return self.n

    def wait(self):
        self.eng.wait_ge(self.sem, self.n)

    def link(self, ins):
        self.inc(ins)
        self.wait()


def program(nc, w, out):
    with ExitStack() as ctx:
        def sb(name, shape, dt=F32):
            return ctx.enter_context(nc.sbuf_tensor(name, shape, dt))

        def sem(name):
            return ctx.enter_context(nc.semaphore(name))

        RAW = sb("RAW", [P, RING, UNIT])
        WH = sb("WH", [P, RING, UNIT], F32R)
        WL = sb("WL", [P, RING, UNIT], F32R)
        H = sb("H", [P, NT, D])
        XN = sb("XN", [P, NT, D])
        XTH = sb("XTH", [P, KD, TOK], F32R)
        XTL = sb("XTL", [P, KD, TOK], F32R)
        KTH = sb("KTH", [P, 768], F32R)
        KTL = sb("KTL", [P, 768], F32R)
        BUF1 = sb("BUF1", [P, NT, 2048])
        BUF2 = sb("BUF2", [P, NT, 2048])
        QK = sb("QK", [P, 8, 2, TOK])
        V = sb("V", [P, NT, D])
        GAIN = sb("GAIN", [P, 2048])
        SCR = sb("SCR", [P, 5120])
        COLS = sb("COLS", [P, N_COLS])
        ROWS = sb("ROWS", [P, N_ROWS])
        TAB = sb("TAB", [P, N_TABLES])
        ID16 = sb("ID16", [P, P], BF16)
        MASK16 = sb("MASK16", [P, 4, P], BF16)
        SS = sb("SS", [P, 16])
        RS = sb("RS", [P, 16])
        DT = sb("DT", [P, 6, 64])
        EX = sb("EX", [P, 2, NT, SSD_HEADS])
        SM = sb("SM", [P, 40])
        PS = [ctx.enter_context(nc.psum_tensor(f"PS{i}", [P, 512], F32)) for i in range(8)]

        def tab(name):
            return TAB[:, T_AT[name][0]:T_AT[name][1]]

        SUBLN = COLS[:, GC["subln"]:GC["subln"] + 1]
        IDENT, UPTO, AFTER = tab("ident"), tab("upto"), tab("after")
        BT = XN[:, 0, :].rearrange("p (g t) -> p g t", g=SSD_GROUPS)
        CT = XN[:, 1, :].rearrange("p (g t) -> p g t", g=SSD_GROUPS)
        CONV = SCR[:, 0:512]
        XSIL = SCR[:, 512:1024]
        E = SCR[:, 0:1024].rearrange("p (h l) -> p h l", h=HPG)
        AB = SCR[:, 1024:2048].rearrange("p (h l) -> p h l", h=HPG)
        XDT, XDEC, STATE, Y, T1, B0 = (SCR[:, 2048 + 512 * n:2560 + 512 * n] for n in range(6))
        SG = SCR[:, 0:512]
        HS = SCR[:, 512:1024]
        TB = SCR[:, 1024:3072].rearrange("p (b c) -> p b c", b=4)
        SMAP = SCR[:, 0:768].rearrange("p (m k) -> p m k", m=2)
        ATT = SCR[:, 768:1152]
        PT = SCR[:, 1152:1536]
        SQJ = SCR[:, 1536:1792]
        PROJ = BUF1[:].rearrange("p t c -> p (t c)")[:, 0:NT * PJ].rearrange("p (t c) -> p t c", t=NT)
        QM = SCR[:, 0:1536].rearrange("p (t h c) -> p t h c", t=NT, h=MLA_HEADS)
        KM = SCR[:, 1536:3072].rearrange("p (t h c) -> p t h c", t=NT, h=MLA_HEADS)
        SC = [SCR[:, 3072:3456], SCR[:, 3456:3840]]
        PT2 = [SCR[:, 3840:4224], SCR[:, 4224:4608]]
        KDUP = SCR[:, 4608:5120].rearrange("p (t j u c) -> p t j u c", t=NT, j=SWA_KV, u=2)
        REST = BUF1[:].rearrange("p t c -> p (t c)")[:, NT * PJ:4096]
        BC = XN[:].rearrange("p t c -> p (t c)")
        SQT = GAIN[:, 0:1024].rearrange("p (j t) -> p j t", j=4)
        SKT = GAIN[:, 1024:1536].rearrange("p (j t) -> p j t", j=2)

        raw = [sem(f"weights_loaded{i}") for i in range(RING)]
        w_hi, w_lo, w_used = sem("weights_hi"), sem("weights_lo"), sem("weights_used")
        loaded, gain_loaded, stored = sem("loaded"), sem("gain_loaded"), sem("stored")
        act_steps, dve_steps, pool_steps = sem("act_steps"), sem("dve_steps"), sem("pool_steps")
        rstd_ok, xn_ok, xn_turned, xt_hi, xt_lo = map(sem, ("rstd_ok", "xn_ok", "xn_turned", "xt_hi", "xt_lo"))
        gate_ok, h_ready, hT_hi, hT_lo = map(sem, ("gate_ok", "hidden_ready", "hidden_hi", "hidden_lo"))
        y_sq, y_ss, y_rs, h_done = map(sem, ("y_squares", "y_sums", "y_rstd", "h_done"))
        out_ok = sem("out_ok")
        conv_1, conv_done, conv_silu, x_turned, x_kept = map(
            sem, ("conv_first_tap", "conv_done", "conv_silu", "x_turned", "x_kept"))
        consts16, dt_raw, z_kept, qkv_kept = map(sem, ("consts16", "dt_raw", "z_kept", "qkv_kept"))
        dt_abs, dt_exp, a_ok, cums, cums_exp, cums_neg = map(
            sem, ("dt_abs", "dt_exp", "a_ok", "cums", "cums_exp", "cums_neg"))
        ab_ok, ssd_mm, ssd_cb, ssd_e, ssd_m, xdec_ok, ssd_y, ssd_st = map(
            sem, ("a_spread", "ssd_sums", "ssd_cb", "ssd_decay", "ssd_mix", "ssd_xdec", "ssd_y", "ssd_state"))
        state_ok, skip_ok, y_read, y_gated, y_rms, ys_ok = map(
            sem, ("state_ok", "skip_ok", "y_read", "y_gated", "y_rms", "ys_ok"))
        k_turned, k_hi, k_lo = map(sem, ("k_turned", "k_hi", "k_lo"))
        lam_dot, lam_exp, lam_ok = map(sem, ("lam_dot", "lam_exp", "lam_ok"))
        scores, s_ready, p_exp, attn_ok, p_turned, p_kept, pv, o_kept, o_sq, o_rs, o_ok = map(
            sem, ("scores", "scores_masked", "probs", "attn_ok", "probs_turned", "probs_kept", "pv", "o_kept",
                  "o_squares", "o_rstd", "o_ok"))
        g_logit, gates_ok, merged, acc_read = map(sem, ("gate_logits", "gates_ok", "merged", "acc_read"))
        proj_kept, lat_rs, lat_ok, lat_turned, lat_hi, lat_lo, q_kept, kv_kept = map(
            sem, ("proj_kept", "lat_rstd", "lat_ok", "lat_turned", "lat_hi", "lat_lo", "q_kept", "kv_kept"))
        swa_roped, kdup_ok, swa_turned, swa_kept, mla_roped, kcat_ok, g2_kept, mla_turned, mla_kept = map(
            sem, ("swa_roped", "kdup_ok", "swa_turned", "swa_kept", "mla_roped", "kcat_ok", "gate2_kept",
                  "mla_turned", "mla_kept"))
        sc2, s2_ready, p2_exp, p2_turned, p2_kept, pv2, o2_kept, gates2 = map(
            sem, ("scores2", "scores2_masked", "probs2", "probs2_turned", "probs2_kept", "pv2", "o2_kept", "gates2"))

        def slot(c):
            return c % RING

        block = ctx.enter_context(nc.Block())

        @block.sync
        def _(sp):
            def load(c, src, wide, i=0):
                s = slot(c)
                rows = src.shape[0] // P
                if c >= RING or not isinstance(i, int):
                    sp.wait_ge(w_lo, c + RING * i - RING + 1)
                sp.dma_start(RAW[:, s, 0:rows * wide].rearrange("p (k c) -> p k c", c=wide),
                             src.rearrange("(k p) c -> p k c", p=P)).then_inc(raw[s], 16)

            def ffn_loads(u0, gate, up, down):
                def g(c, j, i=0):
                    load(c, gate[:, bass.ds(j * 256, 256)], 256, i)

                def u(c, j, i=0):
                    load(c, up[:, bass.ds(j * 256, 256)], 256, i)

                def d(c, j, i=0):
                    load(c, down[bass.ds(j * 256, 256), :], D, i)
                g(u0, 0)
                u(u0 + 1, 0)
                with sp.Fori(1, FF_STEPS) as i:
                    g(u0 - 1, i, i)
                    u(u0, i, i)
                    d(u0 + 1, i - 1, i)
                d(u0 + 3 * FF_STEPS - 1, FF_STEPS - 1)

            def cols_units(u0, src, c0, n, wide=256):
                for j in range(n):
                    load(u0 + j, src[:, c0 + wide * j:c0 + wide * (j + 1)], wide)

            def rows_units(u0, src, n):
                for j in range(n):
                    load(u0 + j, src[256 * j:256 * (j + 1), :], D)

            sp.dma_start(H[:], w["x"].rearrange("o (t p) d -> p (o t) d", p=P)).then_inc(loaded, 16)
            sp.dma_start(COLS[:], w["cols"]).then_inc(loaded, 16)
            sp.dma_start(TAB[:], w["tables"]).then_inc(loaded, 16)
            sp.dma_start(ROWS[:], w["rows"].partition_broadcast(P)).then_inc(loaded, 16)
            sp.dma_start(GAIN[:, 0:D], w["ffn1_post_g"].partition_broadcast(P)).then_inc(gain_loaded, 16)
            ffn_loads(U_FFN1, w["ffn1_w_gate"], w["ffn1_w_up"], w["ffn1_w_down"])
            cols_units(U_XBC, w["w_in"], C_XBC, XBC_TILES // 2)
            cols_units(U_DT, w["w_in"], C_DT, 1, SSD_HEADS)
            cols_units(U_Z, w["w_in"], 0, 8)
            sp.wait_ge(h_done, 4)
            sp.dma_start(GAIN[:], w["ssd_norm_g"].partition_broadcast(P)).then_inc(gain_loaded, 16)
            cols_units(U_QKV, w["w_in"], C_Q, 12)
            rows_units(U_SSDW, w["ssd_w_branch"], 4)
            sp.wait_ge(ys_ok, 8)
            sp.dma_start(GAIN[:], w["gate_b"].partition_broadcast(P)).then_inc(gain_loaded, 16)
            for j in range(4, 8):
                load(U_SSDW + j, w["ssd_w_branch"][256 * j:256 * (j + 1), :], D)
            cols_units(U_GATE, w["w_in"], C_GATE, 8)
            rows_units(U_DAW, w["da_w_branch"], 4)
            sp.wait_ge(g_logit, 8)
            sp.dma_start(GAIN[:, 0:D], w["mix_post_g"].partition_broadcast(P)).then_inc(gain_loaded, 16)
            rows_units(U_WOUT, w["w_out"], 4)
            ffn_loads(U_FFN2, w["ffn2_w_gate"], w["ffn2_w_up"], w["ffn2_w_down"])
            sp.wait_ge(h_done, 8)
            sp.dma_start(GAIN[:, 0:D], w["ffn2_post_g"].partition_broadcast(P)).then_inc(gain_loaded, 16)
            cols_units(U_IN2, w["w_in_2"], 0, 5)
            load(U_IN2 + 5, w["w_in_2"][:, 1280:PJ], PJ - 1280)
            cols_units(U_GATE2A, w["w_in_2"], PJ, 2)
            cols_units(U_UQ, w["w_uq_2"], 0, 2, 384)
            load(U_UKV, w["w_ukv_2"], D)
            cols_units(U_GATE2B, w["w_in_2"], PJ + 512, 6)
            rows_units(U_OSWA, w["w_o_swa_2"], 2)
            rows_units(U_OMLA, w["w_o_mla_2"], 2)
            rows_units(U_OUT2, w["w_out_2"], 4)
            sp.wait_ge(sc2, 2 * SWA_HEADS)
            sp.dma_start(GAIN[:, 0:D], w["final_norm_g_2"].partition_broadcast(P)).then_inc(gain_loaded, 16)
            ffn_loads(U_FFN3, w["w_gate_2"], w["w_up_2"], w["w_down_2"])
            sp.wait_ge(out_ok, NT)
            sp.dma_start(out.rearrange("o (t p) d -> p (o t) d", p=P), XN[:]).then_inc(stored, 16)
            sp.wait_ge(stored, 16)

        @block.scalar
        def _(act):
            own = Steps(act, act_steps)

            def split_hi(c, i=0):
                if isinstance(i, int) and c >= U_END:
                    return
                s = slot(c)
                act.wait_ge(raw[s], 16 * (c // RING + i + 1))
                if c >= RING or not isinstance(i, int):
                    act.wait_ge(w_used, c + RING * i - RING + 1)
                nc.scalar.activation(WH[:, s, :], RAW[:, s, :], ACT.Copy).then_inc(w_hi, 1)

            def rsqrt(dst, src, n, signal, eps_scale=1.0 / D):
                own.wait()
                own.link(nc.scalar.activation(dst, src, ACT.Ln, scale=eps_scale, bias=EPS))
                nc.scalar.activation(dst, dst, ACT.Exp, scale=-0.5).then_inc(signal, 1)
                act.wait_ge(signal, n)

            def norm(n, gain):
                act.wait_ge(h_done, 4 * n) if n else act.wait_ge(loaded, 64)
                own.wait() if own.n else None
                for t in range(NT):
                    own.inc(nc.scalar.activation(TB[:, 2 * t:2 * t + 2, :].rearrange("p a b -> p (a b)"), H[:, t, :],
                                                 ACT.Square, accum_out=SS[:, t:t + 1]))
                rsqrt(RS[:, 0:NT], SS[:, 0:NT], n + 1, rstd_ok)
                if n == 0:
                    for c in range(RING):
                        split_hi(c)
                if gain is None:
                    return
                for r in range(4):
                    act.wait_ge(xn_turned, 4 * n + r + 1)
                    for k in range(2):
                        j = 2 * r + k
                        ins = nc.scalar.activation(XTH[:, j, :], PS[6 + r % 2][:, k * TOK:(k + 1) * TOK], ACT.Copy,
                                                   scale=COLS[:, GC[gain] + j:GC[gain] + j + 1])
                    ins.then_inc(xt_hi, 1)

            def ffn(f, u0, last):
                n0 = FF_STEPS * f

                def g_part(c, j, i=0):
                    split_hi(c + 3, i)
                    act.wait_ge(w_used, c + 3 * i + 1)
                    if not isinstance(j, int) or j:
                        act.wait_ge(h_ready, j + n0)
                    nc.scalar.activation(SG, PS[4][:], ACT.Silu).then_inc(gate_ok, 1)

                def hidden_hi(j):
                    act.wait_ge(h_ready, j + n0 + 1)
                    nc.scalar.activation(KTH[:, 0:512], HS, ACT.Copy).then_inc(hT_hi, 1)
                g_part(u0, 0)
                split_hi(u0 + 4)
                hidden_hi(0)

                def step(c, j, i=0):
                    g_part(c, j, i)
                    split_hi(c + 4, i)
                    split_hi(c + 5, i)
                    act.wait_ge(w_used, c + 3 * i + 3)
                    hidden_hi(j)
                end = FF_STEPS - last
                with act.Fori(1, end) as i:
                    step(u0 - 1, i, i)
                if last:
                    step(u0 + 3 * FF_STEPS - 4, FF_STEPS - 1)
                split_hi(u0 + 3 * FF_STEPS - 1 + 3)

            def post(m, unit, half):
                act.wait_ge(w_used, unit + 1)
                own.wait()
                for b in range(4):
                    ins = nc.scalar.activation(TB[:, b, :], PS[b][:], ACT.Square, accum_out=SS[:, b:b + 1])
                    ins.then_inc(y_sq, 1)
                act.wait_ge(y_ss, m + 1)
                own.link(nc.scalar.activation(RS[:, 0:NT], RS[:, 0:NT], ACT.Ln, scale=1.0 / D, bias=EPS))
                nc.scalar.activation(RS[:, 0:NT], RS[:, 0:NT], ACT.Exp, scale=-0.5,
                                     bias=math.log(0.5) if half else 0.0).then_inc(y_rs, 1)

            def kt_hi(n, prev_unit, scale=1.0):
                act.wait_ge(k_turned, n + 1)
                act.wait_ge(w_used, prev_unit + 1)
                nc.scalar.activation(KTH[:, 0:512], PS[7][:], ACT.Copy, scale=scale).then_inc(k_hi, 1)

            def products(n0, u0, n, scale=1.0):
                for j in range(n):
                    kt_hi(n0 + j, u0 + j - 1, scale)
                    if j:
                        split_hi(u0 + j - 1 + 3)

            norm(0, "ffn1")
            ffn(0, U_FFN1, 0)
            post(0, U_FFN1 + 3 * FF_STEPS - 1, True)
            norm(1, "mix")

            for n in range(XBC_TILES // 2):
                split_hi(U_XBC + n + 3)
                act.wait_ge(w_used, U_XBC + n + 1)
                if n:
                    act.wait_ge(conv_silu, n)
                for f in range(2):
                    j = 2 * n + f
                    ins = nc.scalar.activation(CONV[:, f * TOK:(f + 1) * TOK], PS[4 + n % 2][:, f * TOK:(f + 1) * TOK],
                                               ACT.Identity,
                                               scale=COLS[:, GC["conv_w"] + 3 * XBC_TILES + j:GC["conv_w"] + 3 * XBC_TILES + j + 1],
                                               bias=COLS[:, GC["conv_b"] + j:GC["conv_b"] + j + 1])
                ins.then_inc(conv_1, 1)
                act.wait_ge(conv_done, n + 1)
                if n < 8:
                    if n:
                        act.wait_ge(x_turned, n)
                    nc.scalar.activation(XSIL, CONV, ACT.Silu).then_inc(conv_silu, 1)
                else:
                    nc.scalar.activation(BC[:, (n - 8) * 512:(n - 7) * 512], CONV, ACT.Silu).then_inc(conv_silu, 1)
            split_hi(U_DT + 3)
            for n in range(8):
                split_hi(U_Z + n + 3)
                act.wait_ge(w_used, U_Z + n + 1)
                nc.scalar.activation(BUF2[:, :, n * 256:(n + 1) * 256],
                                     PS[5 - n % 2][:].rearrange("p (t c) -> p t c", t=NT), ACT.Silu).then_inc(z_kept, 1)
            EA = DT[:, 5, 0:32]
            own.link(nc.scalar.activation(EA, ROWS[:, ROW["a_log"]:ROW["a_log"] + 32], ACT.Exp))
            act.wait_ge(dt_abs, 1)
            nc.scalar.activation(DT[:, 1, :], DT[:, 1, :], ACT.Exp).then_inc(dt_exp, 1)
            act.wait_ge(lam_dot, 1)
            nc.scalar.activation(SM[:, 36:38], SM[:, 36:38], ACT.Exp).then_inc(lam_exp, 1)
            act.wait_ge(cums_neg, 1)
            nc.scalar.activation(EX[:].rearrange("p a t h -> p (a t h)"), PS[6][:, 0:128], ACT.Exp).then_inc(cums_exp, 1)

            u = U_QKV
            for r in range(9):
                if r < 8:
                    g, c = divmod(r, 2)
                    act.wait_ge(ssd_mm, r + 1)
                    if r:
                        act.wait_ge(ssd_y, r)
                    else:
                        act.wait_ge(x_kept, 9)
                    for e in range(HPG):
                        ins = nc.scalar.activation(E[:, e, :], PS[e // 4][:, (e % 4) * P:(e % 4 + 1) * P], ACT.Exp,
                                                   bias=DT[:, 4, c * 32 + g * HPG + e:c * 32 + g * HPG + e + 1])
                    ins.then_inc(ssd_e, 1)
                if r:
                    n = r - 1
                    if n % 2 == 0:
                        act.wait_ge(ssd_st, n + 1)
                        nc.scalar.activation(STATE, PS[6][:], ACT.Copy).then_inc(state_ok, 1)
                    act.wait_ge(y_gated, n + 1)
                    act.wait_ge(ssd_m, min(r + 1, 8)) if r < 8 else None
                    own.inc(nc.scalar.activation(T1, Y, ACT.Square, accum_out=SS[:, 4:5]))
                    rsqrt(RS[:, 4:5], SS[:, 4:5], n + 1, y_rms, 1.0 / GW)
                if r < 8:
                    for _u in range(1 + r % 2):
                        n = u - U_QKV
                        split_hi(u + 3)
                        act.wait_ge(w_used, u + 1)
                        src = PS[5 - n % 2][:].rearrange("p (f t) -> p f t", f=2)
                        if n < 8:
                            dst = QK[:, 2 * (n % 4):2 * (n % 4) + 2, n // 4, :]
                        else:
                            dst = V[:, :, (n - 8) * 256:(n - 7) * 256]
                        nc.scalar.activation(dst, src, ACT.Copy).then_inc(qkv_kept, 1)
                        u += 1

            for h in range(9):
                if h:
                    act.wait_ge(p_turned, h)
                    nc.scalar.activation(PT, PS[6][:, 0:384], ACT.Copy).then_inc(p_kept, 1)
                if h < 8:
                    kt_hi(h, U_SSDW + h - 1)
                    if h:
                        split_hi(U_SSDW + h - 1 + 3)
                    act.wait_ge(s_ready, h + 1)
                    for m in range(2):
                        for i, ks in enumerate((slice(0, P), slice(P, 3 * P))):
                            n = 2 * i + m
                            ins = nc.scalar.activation(SMAP[:, m, ks], SMAP[:, m, ks], ACT.Exp, scale=0.125,
                                                       bias=SM[:, 4 + n:5 + n], accum_out=SM[:, 8 + n:9 + n])
                            if i == 0:
                                own.inc(ins)
                        ins.then_inc(p_exp, 1)
                if h:
                    act.wait_ge(o_kept, h)
                    for i in range(NT):
                        own.wait()
                        own.inc(nc.scalar.activation(SQJ[:, i * P:(i + 1) * P], XN[:, i, (h - 1) * P:h * P], ACT.Square,
                                                     accum_out=SS[:, i * 8 + h - 1:i * 8 + h]))
            split_hi(U_SSDW + 7 + 3)
            rsqrt(RS[:], SS[:], 1, o_rs, 1.0 / P)

            for n in range(8):
                split_hi(U_GATE + n + 3)
                act.wait_ge(g_logit, n + 1)
                s = BUF1[:, :, n * 256:(n + 1) * 256]
                nc.scalar.activation(s, s, ACT.Sigmoid).then_inc(gates_ok, 1)
            products(8, U_DAW, 4, SUBLN)
            split_hi(U_DAW + 3 + 3)
            products(12, U_WOUT, 4)
            split_hi(U_WOUT + 3 + 3)
            post(1, U_WOUT + 3, False)

            norm(2, "ffn2")
            ffn(1, U_FFN2, 0)
            post(2, U_FFN2 + 3 * FF_STEPS - 1, True)

            norm(3, "mix2")
            for n in range(6):
                wide = 256 if n < 5 else PJ - 1280
                split_hi(U_IN2 + n + 3)
                act.wait_ge(w_used, U_IN2 + n + 1)
                nc.scalar.activation(PROJ[:, :, n * 256:n * 256 + wide],
                                     PS[n % 2][:].rearrange("p (t c) -> p t c", t=NT)[:, :, 0:wide],
                                     ACT.Copy).then_inc(proj_kept, 1)
            own.wait()
            act.wait_ge(proj_kept, 6)
            for t in range(NT):
                own.inc(nc.scalar.activation(XN[:, t, 0:Q_RANK], PROJ[:, t, LAT0:LAT0 + Q_RANK], ACT.Square,
                                             scale=Q_RANK ** -0.5, accum_out=SS[:, t:t + 1]))
                own.inc(nc.scalar.activation(XN[:, t, Q_RANK:Q_RANK + KV_RANK],
                                             PROJ[:, t, LAT0 + Q_RANK:KR0], ACT.Square,
                                             scale=KV_RANK ** -0.5, accum_out=SS[:, 2 + t:3 + t]))
            rsqrt(RS[:, 0:4], SS[:, 0:4], 1, lat_rs, 1.0)
            for r in range(3):
                act.wait_ge(swa_turned, r + 1)
                dst = GAIN[:, r * 512:(r + 1) * 512]
                nc.scalar.activation(dst, PS[2 + r][:], ACT.Copy).then_inc(swa_kept, 1)

            def g2(n, u):
                split_hi(u + 3)
                act.wait_ge(w_used, u + 1)
                nc.scalar.activation(BUF2[:, :, n * 256:(n + 1) * 256],
                                     PS[n % 2][:].rearrange("p (t c) -> p t c", t=NT), ACT.Copy).then_inc(g2_kept, 1)
            g2(0, U_GATE2A)
            for j in range(3):
                act.wait_ge(lat_turned, 1 + j // 2)
                ins = nc.scalar.activation(KTH[:, j * TOK:(j + 1) * TOK],
                                           PS[6 + j // 2][:, (j % 2) * TOK:(j % 2 + 1) * TOK], ACT.Copy,
                                           scale=COLS[:, GC["q_lat"] + j:GC["q_lat"] + j + 1])
                if j:
                    ins.then_inc(lat_hi, 1)
            g2(1, U_GATE2A + 1)
            for n in range(2):
                split_hi(U_UQ + n + 3)
                act.wait_ge(w_used, U_UQ + n + 1)
                for t in range(NT):
                    ins = nc.scalar.activation(QM[:, t, 4 * n:4 * n + 4, :].rearrange("p h c -> p (h c)"),
                                               PS[2 + 2 * n + t][:, 0:384], ACT.Copy)
                    ins.then_inc(q_kept, 1)
            act.wait_ge(lat_turned, 3)
            for j in range(2):
                ins = nc.scalar.activation(KTH[:, j * TOK:(j + 1) * TOK], PS[7][:, j * TOK:(j + 1) * TOK], ACT.Copy,
                                           scale=COLS[:, GC["kv_lat"] + j:GC["kv_lat"] + j + 1])
            ins.then_inc(lat_hi, 1)
            split_hi(U_UKV + 3)
            act.wait_ge(w_used, U_UKV + 1)
            for b in range(4):
                nc.scalar.activation(V[:, b // 2, (b % 2) * 512:(b % 2 + 1) * 512], PS[2 + b][:],
                                     ACT.Copy).then_inc(kv_kept, 1)

            for r in range(9):
                if r < 8:
                    act.wait_ge(mla_turned, r + 1)
                    nc.scalar.activation(QK[0:MLA_QK, r, :, :], PS[7][0:MLA_QK, :].rearrange("p (a t) -> p a t", a=2),
                                         ACT.Copy).then_inc(mla_kept, 1)
                if r:
                    for a in range(2):
                        act.wait_ge(p2_turned, 2 * (r - 1) + a + 1)
                        nc.scalar.activation(PT2[a], PS[4 + a][:, 0:384], ACT.Copy).then_inc(p2_kept, 1)
                if r < 8:
                    for a in range(2):
                        act.wait_ge(s2_ready, 2 * r + a + 1)
                        scale = (HD ** -0.5, MLA_QK ** -0.5)[a]
                        for i in range(NT):
                            p = SC[a][:, i * P:i * P + P * (i + 1)]
                            ins = nc.scalar.activation(p, p, ACT.Exp, scale=scale, bias=SM[:, 2 * a + i:2 * a + i + 1],
                                                       accum_out=SM[:, 4 + 2 * a + i:5 + 2 * a + i])
                            if a == 0 or i == 0:
                                own.inc(ins)
                        if a == 0:
                            ins = nc.scalar.activation(SM[:, 8:10], SM[:, 0:2], ACT.Exp,
                                                       bias=ROWS[:, ROW["sinks"] + r:ROW["sinks"] + r + 1])
                        ins.then_inc(p2_exp, 1)
                    if r < 6:
                        g2(2 + r, U_GATE2B + r)
            act.wait_ge(g2_kept, 8)
            for b in range(4):
                s = BUF2[:, b % 2, (b // 2) * D:(b // 2 + 1) * D]
                nc.scalar.activation(s, s, ACT.Sigmoid).then_inc(gates2, 1)
            products(16, U_OSWA, 2)
            split_hi(U_OSWA + 1 + 3)
            products(18, U_OMLA, 2)
            split_hi(U_OMLA + 1 + 3)
            products(20, U_OUT2, 4)
            split_hi(U_OUT2 + 3 + 3)

            norm(4, "ffn3")
            ffn(2, U_FFN3, 1)
            norm(5, None)

        @block.gpsimd
        def _(pool):
            own = Steps(pool, pool_steps)
            pool.wait_ge(loaded, 64)
            pool.wait_ge(a_ok, 1)
            for r in range(8):
                g, c = divmod(r, 2)
                if r:
                    pool.wait_ge(ssd_mm, r)
                a = DT[:, 3, c * 32 + g * HPG:c * 32 + (g + 1) * HPG]
                nc.gpsimd.tensor_copy(AB, a.unsqueeze(2).to_broadcast([P, HPG, P])).then_inc(ab_ok, 1)
                if r:
                    pool.wait_ge(ys_ok, r)
                skip = ROWS[:, ROW["skip"] + g * HPG:ROW["skip"] + (g + 1) * HPG]
                nc.gpsimd.tensor_tensor(Y.rearrange("p (h c) -> p h c", h=HPG),
                                        BUF1[:, c, g * GW:(g + 1) * GW].rearrange("p (h c) -> p h c", h=HPG),
                                        skip.unsqueeze(2).to_broadcast([P, HPG, SSD_P]), ALU.mult).then_inc(skip_ok, 1)
            pool.wait_ge(swa_roped, 1)
            for t in range(NT):
                ins = nc.gpsimd.tensor_copy(
                    KDUP[:, t], PROJ[:, t, 512:640].rearrange("p (j c) -> p j c", j=SWA_KV).unsqueeze(2)
                    .to_broadcast([P, SWA_KV, 2, HD]))
            ins.then_inc(kdup_ok, 1)

        @block.vector
        def _(dve):
            own = Steps(dve, dve_steps)
            tt, ts, stt = nc.vector.tensor_tensor, nc.vector.tensor_scalar, nc.vector.scalar_tensor_tensor

            def split_lo(c, i=0):
                if isinstance(i, int) and c >= U_END:
                    return
                s = slot(c)
                dve.wait_ge(w_hi, c + RING * i + 1)
                tt(WL[:, s, :], RAW[:, s, :], WH[:, s, :].bitcast(F32), ALU.subtract).then_inc(w_lo, 1)

            def norm(n, gain):
                dve.wait_ge(rstd_ok, n + 1)
                own.wait() if own.n else None
                for t in range(NT):
                    ts(XN[:, t, :], H[:, t, :], RS[:, t:t + 1], None, ALU.mult).then_inc(xn_ok, 1)
                if n == 0:
                    for c in range(RING):
                        split_lo(c)
                for r in range(4):
                    dve.wait_ge(xt_hi, 4 * n + r + 1)
                    for k in range(2):
                        j = 2 * r + k
                        ins = stt(XTL[:, j, :], PS[6 + r % 2][:, k * TOK:(k + 1) * TOK],
                                  COLS[:, GC[gain] + j:GC[gain] + j + 1], XTH[:, j, :].bitcast(F32),
                                  ALU.mult, ALU.subtract)
                    ins.then_inc(xt_lo, 1)

            def ffn(f, u0, last):
                n0 = FF_STEPS * f

                def up_part(c, j, i=0):
                    dve.wait_ge(gate_ok, j + n0 + 1)
                    dve.wait_ge(w_used, c + 3 * i + 2)
                    if not isinstance(j, int) or j:
                        dve.wait_ge(hT_lo, j + n0)
                    tt(HS, PS[5][:], SG, ALU.mult).then_inc(h_ready, 1)

                def hidden_lo(j):
                    dve.wait_ge(hT_hi, j + n0 + 1)
                    tt(KTL[:, 0:512], HS, KTH[:, 0:512].bitcast(F32), ALU.subtract).then_inc(hT_lo, 1)
                split_lo(u0 + 3)
                split_lo(u0 + 4)
                own.wait()
                up_part(u0, 0)
                hidden_lo(0)

                def step(c, j, i=0):
                    split_lo(c + 3, i)
                    split_lo(c + 4, i)
                    up_part(c, j, i)
                    split_lo(c + 5, i)
                    hidden_lo(j)
                with dve.Fori(1, FF_STEPS - last) as i:
                    step(u0 - 1, i, i)
                if last:
                    step(u0 + 3 * FF_STEPS - 4, FF_STEPS - 1)
                split_lo(u0 + 3 * FF_STEPS - 1 + 3)

            def post(m, gains):
                dve.wait_ge(y_sq, 4 * (m + 1))
                own.wait() if own.n else None
                s = SS[:, 0:4].rearrange("p (t b) -> p t b", b=2)
                tt(RS[:, 0:NT].unsqueeze(2), s[:, :, 0:1], s[:, :, 1:2], ALU.add).then_inc(y_ss, 1)
                dve.wait_ge(gain_loaded, 16 * gains)
                dve.wait_ge(y_rs, m + 1)
                for b in range(4):
                    cols = slice((b % 2) * 512, (b % 2 + 1) * 512)
                    own.link(stt(TB[:, b, :], PS[b][:], RS[:, b // 2:b // 2 + 1], GAIN[:, cols], ALU.mult, ALU.mult))
                    tt(H[:, b // 2, cols], H[:, b // 2, cols], TB[:, b, :], ALU.add).then_inc(h_done, 1)

            def kt_lo(n, scale=None):
                dve.wait_ge(k_hi, n + 1)
                if scale is None:
                    ins = tt(KTL[:, 0:512], PS[7][:], KTH[:, 0:512].bitcast(F32), ALU.subtract)
                else:
                    ins = stt(KTL[:, 0:512], PS[7][:], scale, KTH[:, 0:512].bitcast(F32), ALU.mult, ALU.subtract)
                ins.then_inc(k_lo, 1)

            def products(n0, u0, n, scale=None):
                for j in range(n):
                    kt_lo(n0 + j, scale)
                    if j:
                        split_lo(u0 + j - 1 + 3)

            dve.wait_ge(loaded, 64)
            own.inc(nc.vector.tensor_copy(ID16[:], IDENT))
            nc.vector.tensor_copy(MASK16[:], tab("causal_t").unsqueeze(1).to_broadcast([P, 4, P])).then_inc(consts16, 1)
            own.link(ts(SUBLN, SUBLN, 1.0 - LAM_INIT, None, ALU.mult))
            norm(0, "ffn1")
            ffn(0, U_FFN1, 0)
            post(0, 1)
            norm(1, "mix")

            for n in range(XBC_TILES // 2):
                split_lo(U_XBC + n + 3)
                dve.wait_ge(conv_1, n + 1)
                for back in (1, 2, 3):
                    for f in range(2):
                        j = GC["conv_w"] + (CONV_K - 1 - back) * XBC_TILES + 2 * n + f
                        dst = CONV[:, f * TOK + back:(f + 1) * TOK]
                        ins = stt(dst, PS[4 + n % 2][:, f * TOK:(f + 1) * TOK - back], COLS[:, j:j + 1], dst,
                                  ALU.mult, ALU.add)
                        if back == 3 and f == 1:
                            ins.then_inc(conv_done, 1)
                        else:
                            own.inc(ins)
                    if back < 3:
                        own.wait()
                if n:
                    m = n - 1
                    x_keep(m) if m < 8 else None
                if n == 0:
                    def x_keep(m):
                        dve.wait_ge(x_turned, m + 1)
                        nc.vector.tensor_copy(
                            BUF1[:, :, m * 256:(m + 1) * 256].rearrange("p t (f c) -> p f t c", f=2),
                            PS[6 + m % 2][:].rearrange("p (f t c) -> p f t c", f=2, t=NT)).then_inc(x_kept, 1)
            split_lo(U_DT + 3)
            dve.wait_ge(x_turned, 9)
            nc.vector.tensor_copy(B0, PS[6][:]).then_inc(x_kept, 1)
            dve.wait_ge(w_used, U_DT + 1)
            bias = ROWS[:, ROW["dt_bias"]:ROW["dt_bias"] + 32].unsqueeze(1).to_broadcast([P, NT, 32])
            tt(DT[:, 0, :].rearrange("p (t h) -> p t h", t=NT),
               PS[4][:].rearrange("p (t c) -> p t c", t=NT)[:, :, 0:32], bias, ALU.add).then_inc(dt_raw, 1)
            dve.wait_ge(dt_raw, 1)
            stt(DT[:, 1, :], DT[:, 0, :], -1.0, DT[:, 0, :], ALU.mult, ALU.min).then_inc(dt_abs, 1)
            own.link(ts(DT[:, 0, :], DT[:, 0, :], 0.0, None, ALU.max))
            lam = ROWS[:, ROW["lam"]:ROW["lam"] + 256].rearrange("p (a b c) -> p a b c", a=2, b=2)
            T1L = T1[:, 0:128].rearrange("p (a c) -> p a c", a=2)
            own.link(tt(T1L, lam[:, :, 0, :], lam[:, :, 1, :], ALU.mult))
            nc.vector.tensor_reduce(SM[:, 36:38], T1L, AX.X, ALU.add).then_inc(lam_dot, 1)
            for n in range(8):
                split_lo(U_Z + n + 3)
            dve.wait_ge(dt_exp, 1)
            e, y, z, q = DT[:, 1, :], DT[:, 2, :], DT[:, 3, :], DT[:, 4, :]
            own.link(ts(y, e, 2.0, None, ALU.add))
            own.link(nc.vector.reciprocal(y, y))
            own.link(tt(y, y, e, ALU.mult))
            own.link(tt(z, y, y, ALU.mult))
            own.link(ts(q, z, 1.0 / 15, None, ALU.mult))
            for d in (13, 11, 9, 7, 5, 3):
                own.link(stt(q, q, 1.0 / d, z, ALU.add, ALU.mult))
            own.link(stt(q, q, 1.0, y, ALU.add, ALU.mult))
            own.link(stt(DT[:, 2, :], q, 2.0, DT[:, 0, :], ALU.mult, ALU.add))
            stt(DT[:, 3, :].rearrange("p (t h) -> p t h", t=NT), DT[:, 2, :].rearrange("p (t h) -> p t h", t=NT), -1.0,
                DT[:, 5, 0:32].unsqueeze(1).to_broadcast([P, NT, 32]), ALU.mult, ALU.mult).then_inc(a_ok, 1)
            dve.wait_ge(lam_exp, 1)
            own.link(tt(SM[:, 38:39], SM[:, 37:38], SM[:, 36:37], ALU.subtract))
            ts(SM[:, 39:40], SM[:, 38:39], -LAM_INIT, None, ALU.add).then_inc(lam_ok, 1)
            dve.wait_ge(lam_ok, 1)
            own.link(ts(ROWS[:, ROW["dt_bias"]:ROW["dt_bias"] + 8], ROWS[:, ROW["sinks"]:ROW["sinks"] + 8], -1.0, None, ALU.mult))
            dve.wait_ge(cums, 1)
            ts(DT[:, 4, :].rearrange("p (t h) -> p t h", t=NT),
               PS[6][:, 0:64].rearrange("p (t h) -> p t h", t=NT), -1.0, None, ALU.mult).then_inc(cums_neg, 1)
            dve.wait_ge(cums_exp, 1)
            dve.wait_ge(gain_loaded, 32)

            def by_head(ap):
                return ap.rearrange("p (h c) -> p h c", h=HPG)

            def heads_bc(ap):
                return ap.unsqueeze(2).to_broadcast([P, HPG, SSD_P])

            u = U_QKV
            for r in range(9):
                if r < 8:
                    g, c = divmod(r, 2)
                    xs = BUF1[:, c, g * GW:(g + 1) * GW]
                    hs = slice(c * 32 + g * HPG, c * 32 + (g + 1) * HPG)
                    if r:
                        dve.wait_ge(ssd_y, r)
                    own.link(tt(by_head(XDT), by_head(xs), heads_bc(DT[:, 2, hs]), ALU.mult))
                    if c == 0:
                        tt(by_head(XDEC), by_head(XDT), heads_bc(EX[:, 1, c, g * HPG:(g + 1) * HPG]),
                           ALU.mult).then_inc(xdec_ok, 1)
                if r:
                    n = r - 1
                    g, c = divmod(n, 2)
                    dve.wait_ge(skip_ok, r)
                    dve.wait_ge(ssd_y, r)
                    own.link(tt(Y, PS[3][:], Y, ALU.add))
                    if c:
                        dve.wait_ge(ssd_st, r)
                        own.link(tt(by_head(T1), by_head(PS[6][:]),
                                    heads_bc(EX[:, 0, c, g * HPG:(g + 1) * HPG]), ALU.mult))
                        own.link(tt(Y, Y, T1, ALU.add))
                    zs = BUF2[:, c, g * GW:(g + 1) * GW]
                    tt(Y, Y, zs, ALU.mult).then_inc(y_gated, 1)
                if r < 8:
                    dve.wait_ge(ssd_e, r + 1)
                    dve.wait_ge(ssd_cb, r + 1)
                    for b in range(2):
                        ins = tt(E[:, 4 * b:4 * b + 4, :], E[:, 4 * b:4 * b + 4, :],
                                 PS[2][:, 0:P].unsqueeze(1).to_broadcast([P, 4, P]), ALU.mult)
                    ins.then_inc(ssd_m, 1)
                if r:
                    dve.wait_ge(y_rms, r)
                    stt(zs, Y, RS[:, 4:5], GAIN[:, g0(n) * GW:(g0(n) + 1) * GW], ALU.mult, ALU.mult).then_inc(ys_ok, 1)
                else:
                    def g0(n):
                        return n // 2
                if r < 8:
                    for _u in range(1 + r % 2):
                        split_lo(u + 3)
                        u += 1

            slopes = [2.0 ** (-8.0 * (h + 1) / DA_HEADS) for h in range(DA_HEADS)]

            def o_keep(h):
                dve.wait_ge(pv, h + 1)
                nc.vector.tensor_copy(XN[:, :, h * P:(h + 1) * P],
                                      PS[6][:, 0:256].rearrange("p (i c) -> p i c", i=NT)).then_inc(o_kept, 1)
            dve.wait_ge(ys_ok, 8)
            for h in range(9):
                if h < 8:
                    kt_lo(h)
                    dve.wait_ge(scores, h + 1)
                    if h:
                        own.wait()
                    f = -8.0 * slopes[h]
                    for m in range(2):
                        own.inc(stt(SMAP[:, m, :], tab("dist"), f, PS[4 + m][:, 0:384], ALU.mult, ALU.add))
                    own.wait()
                    own.inc(nc.vector.tensor_reduce(SM[:, 0:2], SMAP[:, :, 0:P], AX.X, ALU.max))
                    own.link(nc.vector.tensor_reduce(SM[:, 2:4], SMAP[:, :, P:3 * P], AX.X, ALU.max))
                    ts(SM[:, 4:8], SM[:, 0:4], -0.125, None, ALU.mult).then_inc(s_ready, 1)
                    if h:
                        split_lo(U_SSDW + h - 1 + 3)
                if h:
                    o_keep(h - 1)
                if h < 8:
                    dve.wait_ge(p_exp, 2 * (h + 1))
                    own.link(nc.vector.reciprocal(SM[:, 12:16], SM[:, 8:12]))
                    own.link(ts(SM[:, 16:20], SM[:, 12:16], SM[:, 39:40], None, ALU.mult))
                    if h:
                        dve.wait_ge(p_turned, h)
                    own.inc(ts(ATT[:, 0:P], SMAP[:, 0, 0:P], SM[:, 12:13], None, ALU.mult))
                    own.link(ts(ATT[:, P:3 * P], SMAP[:, 0, P:3 * P], SM[:, 14:15], None, ALU.mult))
                    own.inc(stt(ATT[:, 0:P], SMAP[:, 1, 0:P], SM[:, 17:18], ATT[:, 0:P], ALU.mult, ALU.add))
                    stt(ATT[:, P:3 * P], SMAP[:, 1, P:3 * P], SM[:, 19:20], ATT[:, P:3 * P], ALU.mult,
                        ALU.add).then_inc(attn_ok, 1)
                    dve.wait_ge(attn_ok, h + 1)
            split_lo(U_SSDW + 7 + 3)
            dve.wait_ge(o_rs, 1)
            o4 = XN[:].rearrange("p t (h c) -> p (t h) c", c=P)
            tt(o4, o4, RS[:].unsqueeze(2).to_broadcast([P, 16, P]), ALU.mult).then_inc(o_ok, 1)

            dve.wait_ge(gain_loaded, 48)

            def merge(b, gates, first, n, last_sem):
                t, cols = b // 2, slice((b % 2) * 512, (b % 2 + 1) * 512)
                if first:
                    tt(V[:, t, cols], PS[b][:], gates[:, t, cols], ALU.mult).then_inc(last_sem, 1)
                else:
                    own.link(tt(TB[:, b, :], PS[b][:], gates[:, t, D + cols.start:D + cols.stop], ALU.mult))
                    tt(V[:, t, cols], V[:, t, cols], TB[:, b, :], ALU.add).then_inc(last_sem, 1)
            for n in range(8):
                split_lo(U_GATE + n + 3)
                dve.wait_ge(w_used, U_GATE + n + 1)
                cols = slice(n * 256, (n + 1) * 256)
                tt(BUF1[:, :, cols], PS[4 + n % 2][:].rearrange("p (t c) -> p t c", t=NT),
                   GAIN[:, cols].unsqueeze(1).to_broadcast([P, NT, 256]), ALU.add).then_inc(g_logit, 1)
            dve.wait_ge(gates_ok, 8)
            for b in range(4):
                merge(b, BUF1, True, 0, acc_read)
            products(8, U_DAW, 4, SUBLN)
            split_lo(U_DAW + 3 + 3)
            dve.wait_ge(w_used, U_DAW + 4)
            dve.wait_ge(acc_read, 4)
            for b in range(4):
                merge(b, BUF1, False, 0, merged)
            products(12, U_WOUT, 4)
            split_lo(U_WOUT + 3 + 3)
            post(1, 4)
            norm(2, "ffn2")
            ffn(1, U_FFN2, 0)
            post(2, 5)

            norm(3, "mix2")
            for n in range(6):
                split_lo(U_IN2 + n + 3)

            def rope(x, cos, sin, heads, half, signal):
                x1, x2 = x[:, :, :, 0:half], x[:, :, :, half:2 * half]
                cb = cos.rearrange("p (t c) -> p t c", t=NT).unsqueeze(2).to_broadcast([P, NT, heads, half])
                sbc = sin.rearrange("p (t c) -> p t c", t=NT).unsqueeze(2).to_broadcast([P, NT, heads, half])
                n = NT * heads * half
                t = [XN[:].rearrange("p t c -> p (t c)")[:, k * n:(k + 1) * n]
                     .rearrange("p (t h c) -> p t h c", t=NT, h=heads) for k in range(3)]
                own.wait()
                own.inc(tt(t[0], x1, cb, ALU.mult))
                own.inc(tt(t[1], x2, sbc, ALU.mult))
                own.link(tt(t[2], x2, cb, ALU.mult))
                own.link(tt(x2, x1, sbc, ALU.mult))
                own.inc(tt(x1, t[0], t[1], ALU.subtract))
                tt(x2, x2, t[2], ALU.add).then_inc(signal, 1)
            dve.wait_ge(lat_rs, 1)
            for t in range(NT):
                own.inc(ts(PROJ[:, t, LAT0:LAT0 + Q_RANK], PROJ[:, t, LAT0:LAT0 + Q_RANK], RS[:, t:t + 1], None, ALU.mult))
                ts(PROJ[:, t, LAT0 + Q_RANK:KR0], PROJ[:, t, LAT0 + Q_RANK:KR0], RS[:, 2 + t:3 + t], None,
                   ALU.mult).then_inc(lat_ok, 1)
            dve.wait_ge(lat_ok, 2)
            rope(PROJ[:, :, 0:640].rearrange("p t (h c) -> p t h c", c=HD), tab("cos_a"), tab("sin_a"), 10, HD // 2,
                 swa_roped)
            dve.wait_ge(swa_roped, 1)
            split_lo(U_GATE2A + 3)
            for j in range(3):
                dve.wait_ge(lat_hi, 1 + (j == 2))
                if j == 0:
                    dve.wait_ge(lat_hi, 1)
                ins = stt(KTL[:, j * TOK:(j + 1) * TOK], PS[6 + j // 2][:, (j % 2) * TOK:(j % 2 + 1) * TOK],
                          COLS[:, GC["q_lat"] + j:GC["q_lat"] + j + 1], KTH[:, j * TOK:(j + 1) * TOK].bitcast(F32),
                          ALU.mult, ALU.subtract)
            ins.then_inc(lat_lo, 1)
            split_lo(U_GATE2A + 1 + 3)
            for n in range(2):
                split_lo(U_UQ + n + 3)
            dve.wait_ge(lat_hi, 3)
            for j in range(2):
                ins = stt(KTL[:, j * TOK:(j + 1) * TOK], PS[7][:, j * TOK:(j + 1) * TOK],
                          COLS[:, GC["kv_lat"] + j:GC["kv_lat"] + j + 1], KTH[:, j * TOK:(j + 1) * TOK].bitcast(F32),
                          ALU.mult, ALU.subtract)
            ins.then_inc(lat_lo, 1)
            dve.wait_ge(q_kept, 4)
            rope(QM[:, :, :, NOPE:MLA_QK], tab("cos_b"), tab("sin_b"), MLA_HEADS, ROPE // 2, mla_roped)
            dve.wait_ge(mla_roped, 1)
            rope(PROJ[:, :, KR0:PJ].unsqueeze(2), tab("cos_b"), tab("sin_b"), 1, ROPE // 2, mla_roped)
            dve.wait_ge(mla_roped, 2)
            own.inc(nc.vector.tensor_copy(KM[:, :, :, NOPE:MLA_QK],
                                          PROJ[:, :, KR0:PJ].unsqueeze(2).to_broadcast([P, NT, MLA_HEADS, ROPE])))
            split_lo(U_UKV + 3)
            dve.wait_ge(kv_kept, 4)
            nc.vector.tensor_copy(KM[:, :, :, 0:NOPE],
                                  V[:].rearrange("p t (h c) -> p t h c", h=MLA_HEADS)[:, :, :, 0:NOPE]).then_inc(kcat_ok, 1)
            nsinks = ROWS[:, ROW["dt_bias"]:ROW["dt_bias"] + 8]
            for r in range(9):
                if r < 8:
                    for a in range(2):
                        dve.wait_ge(sc2, 2 * r + a + 1)
                        if r and a == 0:
                            dve.wait_ge(o2_kept, r - 1) if r > 1 else None
                        if r:
                            dve.wait_ge(p2_turned, 2 * (r - 1) + a + 1)
                        own.link(tt(SC[a], PS[2 + a][:, 0:384], tab(("swa", "mla")[a]), ALU.add))
                        for i in range(NT):
                            own.inc(nc.vector.tensor_reduce(SM[:, 20 + 2 * a + i:21 + 2 * a + i],
                                                            SC[a][:, i * P:i * P + P * (i + 1)], AX.X, ALU.max))
                        own.wait()
                        if a == 0:
                            if r:
                                dve.wait_ge(p2_exp, 2 * r)
                            ts(SM[:, 0:2], SM[:, 20:22], -HD ** -0.5, nsinks[:, r:r + 1], ALU.mult,
                               ALU.min).then_inc(s2_ready, 1)
                        else:
                            ts(SM[:, 2:4], SM[:, 22:24], -MLA_QK ** -0.5, None, ALU.mult).then_inc(s2_ready, 1)
                if r:
                    dve.wait_ge(pv2, r)
                    dst = XN[:].rearrange("p i (a h c) -> p a i h c", a=2, h=8)[:, :, :, r - 1, :]
                    tt(dst, PS[6][:, 0:256].rearrange("p (a i c) -> p a i c", a=2, i=NT),
                       SM[:, 28 + 0:32].rearrange("p (a i) -> p a i", a=2).unsqueeze(3).to_broadcast([P, 2, NT, 64]),
                       ALU.mult).then_inc(o2_kept, 1)
                    dve.wait_ge(o2_kept, r)
                if r < 8:
                    dve.wait_ge(p2_exp, 2 * (r + 1))
                    own.link(tt(SM[:, 4:6], SM[:, 4:6], SM[:, 8:10], ALU.add))
                    own.link(nc.vector.reciprocal(SM[:, 28:32], SM[:, 4:8]))
                    if r < 6:
                        split_lo(U_GATE2B + r + 3)
            products(16, U_OSWA, 2)
            split_lo(U_OSWA + 1 + 3)
            dve.wait_ge(w_used, U_OSWA + 2)
            dve.wait_ge(gates2, 4)
            for b in range(4):
                merge(b, BUF2, True, 0, acc_read)
            products(18, U_OMLA, 2)
            split_lo(U_OMLA + 1 + 3)
            dve.wait_ge(w_used, U_OMLA + 2)
            dve.wait_ge(acc_read, 8)
            for b in range(4):
                merge(b, BUF2, False, 0, merged)
            products(20, U_OUT2, 4)
            split_lo(U_OUT2 + 3 + 3)

            def add_h(unit):
                dve.wait_ge(w_used, unit + 1)
                for b in range(4):
                    s = H[:, b // 2, (b % 2) * 512:(b % 2 + 1) * 512]
                    tt(s, PS[b][:], s, ALU.add).then_inc(h_done, 1)
            add_h(U_OUT2 + 3)
            norm(4, "ffn3")
            ffn(2, U_FFN3, 1)
            add_h(U_END - 1)
            dve.wait_ge(rstd_ok, 6)
            dve.wait_ge(gain_loaded, 96)
            for t in range(NT):
                stt(XN[:, t, :], H[:, t, :], RS[:, t:t + 1], GAIN[:, 0:D], ALU.mult, ALU.mult).then_inc(out_ok, 1)

        @block.tensor
        def _(pe):
            mm = nc.tensor.matmul

            def norm(n):
                pe.wait_ge(xn_ok, NT * (n + 1))
                for r in range(4):
                    if r >= 2:
                        pe.wait_ge(xt_lo, 4 * n + r - 1)
                    for k in range(2):
                        for t in range(NT):
                            j = 2 * r + k
                            ins = nc.tensor.transpose(PS[6 + r % 2][:, k * TOK + t * P:k * TOK + (t + 1) * P],
                                                      XN[:, t, j * P:(j + 1) * P], IDENT)
                    ins.then_inc(xn_turned, 1)
                pe.wait_ge(xt_lo, 4 * (n + 1))

            def parts(ps, stat_hi, stat_lo, mov_hi, mov_lo, first, last):
                mm(ps, stat_hi, mov_hi, start=first, stop=False)
                mm(ps, stat_hi, mov_lo, start=False, stop=False)
                return mm(ps, stat_lo, mov_hi, start=False, stop=last)

            def channels(c, bank, i=0):
                s = slot(c)
                pe.wait_ge(w_lo, c + RING * i + 1)
                for f in range(2):
                    for k in range(KD):
                        ws = slice(k * 256 + f * P, k * 256 + (f + 1) * P)
                        ins = parts(PS[bank][:, f * TOK:(f + 1) * TOK], WH[:, s, ws], WL[:, s, ws],
                                    XTH[:, k, :], XTL[:, k, :], k == 0, k == KD - 1)
                ins.then_inc(w_used, 1)

            def tokens(c, bank, wide=256):
                s = slot(c)
                pe.wait_ge(w_lo, c + 1)
                for t in range(NT):
                    for k in range(KD):
                        ws = slice(k * wide, (k + 1) * wide)
                        xs = slice(t * P, (t + 1) * P)
                        ins = parts(PS[bank][:, t * 256:t * 256 + wide], XTH[:, k, xs], XTL[:, k, xs],
                                    WH[:, s, ws], WL[:, s, ws], k == 0, k == KD - 1)
                ins.then_inc(w_used, 1)

            def rows(c, first, last, i=0, banks=0, nk=2):
                s = slot(c)
                pe.wait_ge(w_lo, c + RING * i + 1)
                for k in range(nk):
                    for t in range(NT):
                        a = slice(k * TOK + t * P, k * TOK + (t + 1) * P)
                        for h in range(2):
                            ws = slice(k * D + h * 512, k * D + (h + 1) * 512)
                            ins = parts(PS[banks + 2 * t + h][:], KTH[:, a], KTL[:, a], WH[:, s, ws], WL[:, s, ws],
                                        first and k == 0, last and k == 1)
                ins.then_inc(w_used, 1)

            def ffn(f, u0):
                n0 = FF_STEPS * f
                channels(u0, 4)
                channels(u0 + 1, 5)

                def step(c, j, i=0, first=False):
                    pe.wait_ge(gate_ok, j + n0)
                    channels(c, 4, i)
                    pe.wait_ge(h_ready, j + n0)
                    channels(c + 1, 5, i)
                    pe.wait_ge(hT_lo, j + n0)
                    rows(c + 2, first, False, i)
                step(u0 + 2, 1, 0, True)
                with pe.Fori(2, FF_STEPS) as i:
                    step(u0 - 1, i, i)
                pe.wait_ge(hT_lo, n0 + FF_STEPS)
                rows(u0 + 3 * FF_STEPS - 1, False, True)

            def turn_rows(n, src, k0):
                if n:
                    pe.wait_ge(k_lo, n)
                for k in range(2):
                    for t in range(NT):
                        ins = nc.tensor.transpose(PS[7][:, k * TOK + t * P:k * TOK + (t + 1) * P],
                                                  src[:, t, (k0 + k) * P:(k0 + k + 1) * P], IDENT)
                ins.then_inc(k_turned, 1)

            def products(n0, u0, n, src, k0=0):
                for j in range(n):
                    turn_rows(n0 + j, src, k0 + 2 * j)
                    pe.wait_ge(k_lo, n0 + j + 1)
                    rows(u0 + j, j == 0, j == n - 1)

            pe.wait_ge(loaded, 64)
            norm(0)
            ffn(0, U_FFN1)
            norm(1)

            def turn_x(n):
                pe.wait_ge(conv_silu, n + 1)
                if n >= 2:
                    pe.wait_ge(x_kept, n - 1)
                for f in range(2):
                    for t in range(NT):
                        ins = nc.tensor.transpose(PS[6 + n % 2][:, f * TOK + t * P:f * TOK + (t + 1) * P],
                                                  XSIL[:, f * TOK + t * P:f * TOK + (t + 1) * P], IDENT)
                ins.then_inc(x_turned, 1)
            for n in range(XBC_TILES // 2):
                if n >= 2:
                    pe.wait_ge(conv_done, n - 1)
                channels(U_XBC + n, 4 + n % 2)
                if 1 <= n <= 8:
                    turn_x(n - 1)
            pe.wait_ge(conv_done, 11)
            tokens(U_DT, 4, SSD_HEADS)
            pe.wait_ge(conv_silu, 10)
            pe.wait_ge(x_kept, 7)
            for g in range(SSD_GROUPS):
                ins = nc.tensor.transpose(PS[6][:, g * P:(g + 1) * P], BT[:, g, 0:P], IDENT)
            ins.then_inc(x_turned, 1)
            for n in range(8):
                if n == 0:
                    pe.wait_ge(conv_done, 12)
                elif n == 1:
                    pe.wait_ge(dt_raw, 1)
                else:
                    pe.wait_ge(z_kept, n - 1)
                tokens(U_Z + n, 5 - n % 2)
            pe.wait_ge(a_ok, 1)
            pe.wait_ge(x_kept, 9)
            for k, tri in enumerate((UPTO, AFTER)):
                for c in range(NT):
                    ins = mm(PS[6][:, k * 64 + c * 32:k * 64 + (c + 1) * 32], tri, DT[:, 3, c * 32:(c + 1) * 32],
                             start=True, stop=True)
            ins.then_inc(cums, 1)
            pe.wait_ge(consts16, 1)
            pe.wait_ge(conv_silu, 12)
            u = U_QKV
            for r in range(9):
                if r < 8:
                    g, c = divmod(r, 2)
                    if r:
                        pe.wait_ge(ssd_e, r)
                        pe.wait_ge(ssd_m, r)
                    mm(PS[2][:, 0:P], BT[:, g, c * P:(c + 1) * P], CT[:, g, c * P:(c + 1) * P], start=True,
                       stop=True).then_inc(ssd_cb, 1)
                    pe.wait_ge(ab_ok, r + 1)
                    for b in range(2):
                        mm(PS[b][:], ID16[:], MASK16[:].rearrange("p h l -> p (h l)"), start=True, stop=False)
                        for e in range(4):
                            ins = mm(PS[b][:, e * P:(e + 1) * P], AB[:, 4 * b + e, :], UPTO, start=False, stop=e == 3)
                    ins.then_inc(ssd_mm, 1)
                if r:
                    n = r - 1
                    g, c = divmod(n, 2)
                    if n:
                        pe.wait_ge(y_gated, n)
                    pe.wait_ge(cums_exp, 1)
                    pe.wait_ge(cums_neg, 1)
                    if c == 0:
                        pe.wait_ge(xdec_ok, n // 2 + 1)
                        mm(PS[6][:], B0[:, g * P:(g + 1) * P], XDEC, start=True, stop=True).then_inc(ssd_st, 1)
                    else:
                        pe.wait_ge(state_ok, n // 2 + 1)
                        mm(PS[6][:], CT[:, g, P:TOK], STATE, start=True, stop=True).then_inc(ssd_st, 1)
                    pe.wait_ge(ssd_m, r)
                    for e in range(HPG):
                        ins = mm(PS[3][:, e * SSD_P:(e + 1) * SSD_P], E[:, e, :], XDT[:, e * SSD_P:(e + 1) * SSD_P],
                                 start=True, stop=True)
                    ins.then_inc(ssd_y, 1)
                if r < 8:
                    for _u in range(1 + r % 2):
                        n = u - U_QKV
                        pe.wait_ge(z_kept, 7 + n) if n < 2 else pe.wait_ge(qkv_kept, n - 1)
                        (channels if n < 8 else tokens)(u, 5 - n % 2)
                        u += 1
            pe.wait_ge(ys_ok, 8)
            pe.wait_ge(qkv_kept, 12)
            for h in range(9):
                if h:
                    pe.wait_ge(attn_ok, h)
                    if h >= 2:
                        pe.wait_ge(o_kept, h - 1)
                    for b in range(3):
                        ins = nc.tensor.transpose(PS[6][:, b * P:(b + 1) * P], ATT[:, b * P:(b + 1) * P], IDENT)
                    ins.then_inc(p_turned, 1)
                if h < 8:
                    turn_rows(h, BUF2, 2 * h)
                    if h:
                        pe.wait_ge(s_ready, h)
                    for m in range(2):
                        ms = slice(m * 64, (m + 1) * 64)
                        mm(PS[4 + m][:, 0:P], QK[ms, h, 0, 0:P], QK[ms, h, 1, 0:P], start=True, stop=True)
                        ins = mm(PS[4 + m][:, P:3 * P], QK[ms, h, 0, P:TOK], QK[ms, h, 1, :], start=True, stop=True)
                    ins.then_inc(scores, 1)
                if h:
                    pe.wait_ge(p_kept, h)
                    vs = slice((h - 1) * P, h * P)
                    mm(PS[6][:, 0:P], PT[:, 0:P], V[:, 0, vs], start=True, stop=True)
                    mm(PS[6][:, P:2 * P], PT[:, P:2 * P], V[:, 0, vs], start=True, stop=False)
                    mm(PS[6][:, P:2 * P], PT[:, 2 * P:3 * P], V[:, 1, vs], start=False, stop=True).then_inc(pv, 1)
                if h < 8:
                    pe.wait_ge(k_lo, h + 1)
                    rows(U_SSDW + h, h == 0, h == 7)
            for n in range(8):
                pe.wait_ge(s_ready, 8) if n < 2 else pe.wait_ge(g_logit, n - 1)
                tokens(U_GATE + n, 4 + n % 2)
            pe.wait_ge(o_ok, 1)
            pe.wait_ge(acc_read, 4)
            products(8, U_DAW, 4, XN)
            pe.wait_ge(merged, 4)
            products(12, U_WOUT, 4, V)
            norm(2)
            ffn(1, U_FFN2)
            norm(3)

            for n in range(6):
                if n < 2:
                    pe.wait_ge(h_done, 12)
                else:
                    pe.wait_ge(proj_kept, n - 1)
                tokens(U_IN2 + n, n % 2, 256 if n < 5 else PJ - 1280)
            pe.wait_ge(proj_kept, 5)
            tokens(U_GATE2A, 0)

            def turn_latent(bank, c0, tiles):
                for k in range(tiles):
                    for t in range(NT):
                        ins = nc.tensor.transpose(PS[bank][:, k * TOK + t * P:k * TOK + (t + 1) * P],
                                                  PROJ[:, t, c0 + k * P:c0 + (k + 1) * P], IDENT)
                ins.then_inc(lat_turned, 1)
            pe.wait_ge(lat_ok, 2)
            turn_latent(6, LAT0, 2)
            turn_latent(7, LAT0 + 2 * P, 1)
            pe.wait_ge(swa_roped, 1)
            for r in range(2):
                for k in range(2):
                    for t in range(NT):
                        ins = nc.tensor.transpose(PS[2 + r][:, k * TOK + t * P:k * TOK + (t + 1) * P],
                                                  PROJ[:, t, (2 * r + k) * P:(2 * r + k + 1) * P], IDENT)
                ins.then_inc(swa_turned, 1)
            pe.wait_ge(kdup_ok, 1)
            for k in range(SWA_KV):
                for t in range(NT):
                    ins = nc.tensor.transpose(PS[4][:, k * TOK + t * P:k * TOK + (t + 1) * P],
                                              KDUP[:, t, k, :, :].rearrange("p u c -> p (u c)"), IDENT)
            ins.then_inc(swa_turned, 1)
            pe.wait_ge(proj_kept, 6)
            tokens(U_GATE2A + 1, 1)
            pe.wait_ge(lat_lo, 1)
            pe.wait_ge(swa_kept, 3)
            for n in range(2):
                c = U_UQ + n
                pe.wait_ge(w_lo, c + 1)
                for t in range(NT):
                    for k in range(3):
                        a = slice(k * TOK + t * P, k * TOK + (t + 1) * P)
                        ws = slice(k * 384, (k + 1) * 384)
                        ins = parts(PS[2 + 2 * n + t][:, 0:384], KTH[:, a], KTL[:, a], WH[:, slot(c), ws],
                                    WL[:, slot(c), ws], k == 0, k == 2)
                ins.then_inc(w_used, 1)
            turn_latent(7, LAT0 + Q_RANK, 2)
            pe.wait_ge(lat_lo, 2)
            pe.wait_ge(q_kept, 4)
            rows(U_UKV, True, True, banks=2)
            pe.wait_ge(kcat_ok, 1)
            pe.wait_ge(kv_kept, 4)
            for r in range(9):
                if r < 8:
                    if r:
                        pe.wait_ge(mla_kept, r)
                    for a, src in enumerate((QM, KM)):
                        for t in range(NT):
                            ins = nc.tensor.transpose(PS[7][0:MLA_QK, a * TOK + t * P:a * TOK + (t + 1) * P],
                                                      src[:, t, r, :], IDENT)
                    ins.then_inc(mla_turned, 1)
                if r:
                    pe.wait_ge(p2_exp, 2 * r)
                    if r >= 2:
                        pe.wait_ge(p2_kept, 2 * (r - 1))
                    for a in range(2):
                        for b in range(3):
                            ins = nc.tensor.transpose(PS[4 + a][:, b * P:(b + 1) * P], SC[a][:, b * P:(b + 1) * P],
                                                      IDENT)
                        ins.then_inc(p2_turned, 1)

                def score(a, qt, kt, r):
                    if r:
                        pe.wait_ge(s2_ready, 2 * (r - 1) + a + 1)
                    mm(PS[2 + a][:, 0:P], qt[:, 0:P], kt[:, 0:P], start=True, stop=True)
                    mm(PS[2 + a][:, P:3 * P], qt[:, P:TOK], kt[:, :], start=True, stop=True).then_inc(sc2, 1)
                if r < 8:
                    ms = slice((r % 2) * 64, (r % 2 + 1) * 64)
                    score(0, SQT[ms, r // 2, :], SKT[ms, r // 4, :], r)
                if r:
                    h = r - 1
                    if r >= 2:
                        pe.wait_ge(o2_kept, r - 1)
                    for a in range(2):
                        pe.wait_ge(p2_kept, 2 * h + a + 1)
                        if a == 0:
                            v = PROJ[:, :, 640 + (h // 4) * HD:640 + (h // 4 + 1) * HD]
                        else:
                            v = V[:, :, h * P + NOPE:(h + 1) * P]
                        mm(PS[6][:, a * P:a * P + 64], PT2[a][:, 0:P], v[:, 0, :], start=True, stop=True)
                        mm(PS[6][:, a * P + 64:(a + 1) * P], PT2[a][:, P:2 * P], v[:, 0, :], start=True, stop=False)
                        ins = mm(PS[6][:, a * P + 64:(a + 1) * P], PT2[a][:, 2 * P:3 * P], v[:, 1, :], start=False,
                                 stop=True)
                    ins.then_inc(pv2, 1)
                if r < 8:
                    pe.wait_ge(mla_kept, r + 1)
                    score(1, QK[0:MLA_QK, r, 0, :], QK[0:MLA_QK, r, 1, :], r)
                    if r < 6:
                        pe.wait_ge(g2_kept, r + 1)
                        tokens(U_GATE2B + r, r % 2)
            pe.wait_ge(g2_kept, 8)
            pe.wait_ge(o2_kept, 8)
            products(16, U_OSWA, 2, XN)
            pe.wait_ge(acc_read, 8)
            products(18, U_OMLA, 2, XN, 4)
            pe.wait_ge(merged, 8)
            products(20, U_OUT2, 4, V)
            norm(4)
            ffn(2, U_FFN3)


_SQUEEZED = ["ffn1_w_gate", "ffn1_w_up", "ffn1_w_down", "ffn1_post_g", "w_in", "gate_b", "ssd_norm_g", "ssd_w_branch",
             "da_w_branch", "w_out", "mix_post_g", "ffn2_w_gate", "ffn2_w_up", "ffn2_w_down", "ffn2_post_g",
             "w_in_2", "w_uq_2", "w_ukv_2", "w_o_swa_2", "w_o_mla_2", "w_out_2", "w_gate_2", "w_up_2", "w_down_2"]


def kernel(**inputs):
    import concourse.bacc as bacc
    from concourse.bass_utils import run_bass_kernel_spmd

    v = {k: np.asarray(a) for k, a in inputs.items()}

    def tiles(a):
        return a.reshape(-1, P).T
    cols = [tiles(v[k][0]) for k in ("ffn1_pre_g", "mix_pre_g", "ffn2_pre_g", "mix_norm_g_2", "ffn_norm_g_2",
                                     "q_norm_g_2", "kv_norm_g_2", "da_subln_g", "ssd_conv_b")]
    cols += [tiles(v["ssd_conv_w"][0][k]) for k in range(CONV_K)]
    rows = [v[k][0] for k in ("ssd_dt_bias", "ssd_A_log", "ssd_D", "da_lambda_q1", "da_lambda_k1", "da_lambda_q2",
                              "da_lambda_k2", "swa_sinks_2")]
    host = {"x": v["x"], "cols": np.concatenate(cols, 1), "rows": np.concatenate(rows), "tables": TABLES,
            "final_norm_g_2": v["final_norm_g_2"]}
    host.update({k: v[k][0] for k in _SQUEEZED})
    nc = bacc.Bacc("TRN2", target_bir_lowering=False, num_devices=1)
    arrays, aps = {}, {}
    for name, a in host.items():
        a = np.ascontiguousarray(a)
        arrays[f"in_{name}"] = a
        aps[name] = nc.dram_tensor(f"in_{name}", a.shape, mybir.dt.from_np(a.dtype), kind="ExternalInput").ap()
    out = nc.dram_tensor("out_x", (1, TOK, D), F32, kind="ExternalOutput").ap()
    program(nc, aps, out)
    r = run_bass_kernel_spmd(nc, [arrays], core_ids=[0])
    return r.results[0]["out_x"]
```

```python
import math
from contextlib import ExitStack

import numpy as np
import concourse.bass as bass
from concourse import mybir

ALU = mybir.AluOpType
ACT = mybir.ActivationFunctionType
AX = mybir.AxisListType
F32 = mybir.dt.float32
F32R = mybir.dt.float32r
BF16 = mybir.dt.bfloat16

P = 128
D = 1024
KD = D // P
NT = 2
TOK = NT * P
D_FF = 2816
FF_STEPS = D_FF // 256
EPS = 1e-6
HIDE = -1e30
SSD_INNER, SSD_GROUPS, SSD_HEADS, SSD_P, SSD_N = 2048, 4, 32, 64, 128
HPG = SSD_HEADS // SSD_GROUPS
GW = HPG * SSD_P
CONV_K = 4
XBC_TILES = (SSD_INNER + 2 * SSD_GROUPS * SSD_N) // P
DA_HEADS = 8
LAM_INIT = 0.8 - 0.6 * math.exp(0.0)
SWA_HEADS, SWA_KV, HD = 8, 2, 64
MLA_HEADS, NOPE, ROPE, MLA_V = 8, 64, 32, 64
MLA_QK = NOPE + ROPE
Q_RANK, KV_RANK = 384, 256

RING = 3
UNIT = 2048
U_FFN1 = 0
U_XZ = U_FFN1 + 3 * FF_STEPS
XZ = [("z", 0), ("z", 1), ("dt", 0)] + [v for n in range(6) for v in (("x", 2 * n), ("x", 2 * n + 1), ("z", n + 2))]
U_QKV = U_XZ + len(XZ)
U_SSDW = U_QKV + 12
U_GATE = U_SSDW + 8
U_DAW = U_GATE + 8
U_WOUT = U_DAW + 4
U_FFN2 = U_WOUT + 4
U_IN2 = U_FFN2 + 3 * FF_STEPS
U_GATE2A = U_IN2 + 6
U_UQ = U_GATE2A + 2
U_UKV = U_UQ + 2
U_GATE2B = U_UKV + 1
U_OSWA = U_GATE2B + 6
U_OMLA = U_OSWA + 2
U_OUT2 = U_OMLA + 2
U_FFN3 = U_OUT2 + 4
U_END = U_FFN3 + 3 * FF_STEPS

C_XBC = SSD_INNER
C_DT = C_XBC + XBC_TILES * P
C_Q = C_DT + SSD_HEADS
C_GATE = C_Q + 3 * D
LAT0 = SWA_HEADS * HD + 2 * SWA_KV * HD
KR0 = LAT0 + Q_RANK + KV_RANK
PJ = KR0 + ROPE

GC = {}
_n = 0
for _name, _tiles in (("q_lat", 3), ("kv_lat", 2), ("subln", 1), ("conv_b", XBC_TILES), ("conv_w", CONV_K * XBC_TILES)):
    GC[_name] = _n
    _n += _tiles
N_COLS = _n
ROW = dict(dt_bias=0, a_log=32, skip=64, sinks=96)
N_ROWS = ROW["sinks"] + SWA_HEADS


def tables():
    r, c = np.arange(P)[:, None], np.arange(P)[None, :]
    hide = lambda keep: np.where(keep, 0.0, HIDE)
    causal = hide(r >= c)
    near = np.where(r >= c, r - c, -HIDE)
    cols = dict(
        ident=np.eye(P), upto=r <= c, after=r > c,
        swa=np.concatenate([causal, hide(c > r), causal], 1),
        mla=np.concatenate([causal, np.zeros((P, P)), causal], 1),
        dist=np.concatenate([near, P + r - c, near], 1),
        causal_t=hide(r <= c),
    )
    for name, dim in (("a", HD), ("b", ROPE)):
        inv = np.float32(10000.0) ** (-np.arange(0, dim, 2, dtype=np.float32) / np.float32(dim))
        ang = (np.arange(TOK, dtype=np.float32)[:, None] * inv[None, :].astype(np.float32)).astype(np.float32)
        for f, fn in (("cos", np.cos), ("sin", np.sin)):
            t = fn(ang.astype(np.float64)).astype(np.float32)
            cols[f"{f}_{name}"] = t.reshape(NT, P, dim // 2).transpose(1, 0, 2).reshape(P, -1)
    at, n = {}, 0
    for k, v in cols.items():
        at[k] = (n, n + v.shape[1])
        n += v.shape[1]
    return np.concatenate([np.asarray(v, np.float32) for v in cols.values()], 1), at, n


TABLES, T_AT, N_TABLES = tables()


class Steps:

    def __init__(self, eng, sem):
        self.eng, self.sem, self.n = eng, sem, 0

    def inc(self, ins):
        self.n += 1
        ins.then_inc(self.sem, 1)
        return self.n

    def wait(self):
        self.eng.wait_ge(self.sem, self.n)

    def link(self, ins):
        self.inc(ins)
        self.wait()


def program(nc, w, out):
    with ExitStack() as ctx:
        def sb(name, shape, dt=F32):
            return ctx.enter_context(nc.sbuf_tensor(name, shape, dt))

        def sem(name):
            return ctx.enter_context(nc.semaphore(name))

        RAW = sb("RAW", [P, RING, UNIT])
        WH = sb("WH", [P, RING, UNIT], F32R)
        WL = sb("WL", [P, RING, UNIT], F32R)
        H = sb("H", [P, NT, D])
        XN = sb("XN", [P, NT, D])
        XTH = sb("XTH", [P, KD, TOK], F32R)
        XTL = sb("XTL", [P, KD, TOK], F32R)
        KTH = sb("KTH", [P, 1024], F32R)
        KTL = sb("KTL", [P, 1024], F32R)
        BUF1 = sb("BUF1", [P, NT, 2048])
        BUF2 = sb("BUF2", [P, NT, 2048])
        QK = sb("QK", [P, 8, 2, TOK])
        V = sb("V", [P, NT, D])
        GAIN = sb("GAIN", [P, 2048])
        SCR = sb("SCR", [P, 5120])
        COLS = sb("COLS", [P, N_COLS])
        ROWS = sb("ROWS", [P, N_ROWS])
        TAB = sb("TAB", [P, N_TABLES])
        ID16 = sb("ID16", [P, P], BF16)
        MASK16 = sb("MASK16", [P, 4, P], BF16)
        SS = sb("SS", [P, 16])
        RS = sb("RS", [P, 16])
        DT = sb("DT", [P, 6, 64])
        EX = sb("EX", [P, 2, NT, SSD_HEADS])
        SM = sb("SM", [P, 40])
        PS = [ctx.enter_context(nc.psum_tensor(f"PS{i}", [P, 512], F32)) for i in range(8)]

        def tab(name):
            return TAB[:, T_AT[name][0]:T_AT[name][1]]

        SUBLN = COLS[:, GC["subln"]:GC["subln"] + 1]
        IDENT, UPTO, AFTER = tab("ident"), tab("upto"), tab("after")
        BT = XN[:, 0, :].rearrange("p (g t) -> p g t", g=SSD_GROUPS)
        CT = XN[:, 1, :].rearrange("p (g t) -> p g t", g=SSD_GROUPS)
        CONV = SCR[:, 0:512]
        XSIL = SCR[:, 512:1024]
        E = SCR[:, 0:1024].rearrange("p (h l) -> p h l", h=HPG)
        AB = SCR[:, 1024:2048].rearrange("p (h l) -> p h l", h=HPG)
        XDT, XDEC, STATE, Y, T1, B0 = (SCR[:, 2048 + 512 * n:2560 + 512 * n] for n in range(6))
        SG = SCR[:, 0:512]
        HS = SCR[:, 512:1024]
        TB = SCR[:, 1024:3072].rearrange("p (b c) -> p b c", b=4)
        SMAP = SCR[:, 0:768].rearrange("p (m k) -> p m k", m=2)
        ATT = SCR[:, 768:1152]
        PT = SCR[:, 1152:1536]
        SQJ = SCR[:, 1536:1792]
        PROJ = BUF1[:].rearrange("p t c -> p (t c)")[:, 0:NT * PJ].rearrange("p (t c) -> p t c", t=NT)
        QM = SCR[:, 0:1536].rearrange("p (t h c) -> p t h c", t=NT, h=MLA_HEADS)
        KM = SCR[:, 1536:3072].rearrange("p (t h c) -> p t h c", t=NT, h=MLA_HEADS)
        SC = [SCR[:, 3072:3456], SCR[:, 3456:3840]]
        PT2 = [SCR[:, 3840:4224], SCR[:, 4224:4608]]
        KDUP = SCR[:, 4608:5120].rearrange("p (t j u c) -> p t j u c", t=NT, j=SWA_KV, u=2)
        GPRE = SCR[:, 4096:5120]
        REST = BUF1[:].rearrange("p t c -> p (t c)")[:, NT * PJ:4096]
        BC = XN[:].rearrange("p t c -> p (t c)")
        SQT = GAIN[:, 0:1024].rearrange("p (j t) -> p j t", j=4)
        SKT = GAIN[:, 1024:1536].rearrange("p (j t) -> p j t", j=2)

        raw = [sem(f"weights_loaded{i}") for i in range(RING)]
        w_hi, w_lo, w_used = sem("weights_hi"), sem("weights_lo"), sem("weights_used")
        x_loaded = [sem(f"x_loaded{t}") for t in range(NT)]
        loaded, tab_loaded, stored = sem("loaded"), sem("tables_loaded"), sem("stored")
        lam_loaded = sem("lam_loaded")
        gain_loaded, gpre_loaded, acc_half, y_gained = map(
            sem, ("gain_loaded", "pre_gain_loaded", "acc_half", "y_gained"))
        act_steps, dve_steps, pool_steps = sem("act_steps"), sem("dve_steps"), sem("pool_steps")
        rstd_ok, xn_ok, xn_turned, xt_hi, xt_lo = map(sem, ("rstd_ok", "xn_ok", "xn_turned", "xt_hi", "xt_lo"))
        gate_ok, h_ready, hT_hi, hT_lo = map(sem, ("gate_ok", "hidden_ready", "hidden_hi", "hidden_lo"))
        y_sq, y_ss, y_rs, h_done = map(sem, ("y_squares", "y_sums", "y_rstd", "h_done"))
        out_ok = sem("out_ok")
        conv_1, conv_done, conv_silu, x_turned, x_kept = map(
            sem, ("conv_first_tap", "conv_done", "conv_silu", "x_turned", "x_kept"))
        consts16, dt_raw, z_kept, qkv_kept = map(sem, ("consts16", "dt_raw", "z_kept", "qkv_kept"))
        dt_abs, dt_exp, a_ok, cums, cums_exp, cums_neg = map(
            sem, ("dt_abs", "dt_exp", "a_ok", "cums", "cums_exp", "cums_neg"))
        ab_ok, ssd_mm, ssd_cb, ssd_e, ssd_m, xdec_ok, ssd_y, ssd_st = map(
            sem, ("a_spread", "ssd_sums", "ssd_cb", "ssd_decay", "ssd_mix", "ssd_xdec", "ssd_y", "ssd_state"))
        state_ok, skip_ok, y_read, y_gated, y_rms, ys_ok = map(
            sem, ("state_ok", "skip_ok", "y_read", "y_gated", "y_rms", "ys_ok"))
        k_turned, k_hi, k_lo = map(sem, ("k_turned", "k_hi", "k_lo"))
        lam_dot, lam_exp, lam_ok = map(sem, ("lam_dot", "lam_exp", "lam_ok"))
        scores, s_ready, p_exp, attn_ok, p_turned, p_kept, pv, o_kept, o_sq, o_rs, o_ok = map(
            sem, ("scores", "scores_masked", "probs", "attn_ok", "probs_turned", "probs_kept", "pv", "o_kept",
                  "o_squares", "o_rstd", "o_ok"))
        g_logit, gates_ok, merged, acc_read = map(sem, ("gate_logits", "gates_ok", "merged", "acc_read"))
        proj_kept, lat_rs, lat_ok, lat_turned, lat_hi, lat_lo, q_kept, kv_kept = map(
            sem, ("proj_kept", "lat_rstd", "lat_ok", "lat_turned", "lat_hi", "lat_lo", "q_kept", "kv_kept"))
        swa_roped, kdup_ok, swa_turned, swa_kept, mla_roped, kcat_ok, g2_kept, mla_turned, mla_kept = map(
            sem, ("swa_roped", "kdup_ok", "swa_turned", "swa_kept", "mla_roped", "kcat_ok", "gate2_kept",
                  "mla_turned", "mla_kept"))
        sc2, s2_ready, p2_exp, p2_turned, p2_kept, pv2, o2_kept, gates2 = map(
            sem, ("scores2", "scores2_masked", "probs2", "probs2_turned", "probs2_kept", "pv2", "o2_kept", "gates2"))

        post_no = {0: 0, 1: 1, 2: 2}

        def half_of(n):
            return slice((n % 2) * 512, (n % 2 + 1) * 512)

        def slot(c):
            return c % RING

        block = ctx.enter_context(nc.Block())

        @block.sync
        def _(sp):
            def load(c, src, wide, i=0):
                s = slot(c)
                rows = src.shape[0] // P
                if c >= RING or not isinstance(i, int):
                    sp.wait_ge(w_lo, c + RING * i - RING + 1)
                sp.dma_start(RAW[:, s, 0:rows * wide].rearrange("p (k c) -> p k c", c=wide),
                             src.rearrange("(k p) c -> p k c", p=P)).then_inc(raw[s], 16)

            def ffn_loads(u0, gate, up, down):
                def g(c, j, i=0):
                    load(c, gate[:, bass.ds(j * 256, 256)], 256, i)

                def u(c, j, i=0):
                    load(c, up[:, bass.ds(j * 256, 256)], 256, i)

                def d(c, j, i=0):
                    load(c, down[bass.ds(j * 256, 256), :], D, i)
                g(u0, 0)
                u(u0 + 1, 0)
                if u0 == U_FFN1:
                    sp.dma_start(COLS[:], w["cols"]).then_inc(loaded, 16)
                    sp.dma_start(ROWS[:], w["rows"].partition_broadcast(P)).then_inc(loaded, 16)
                with sp.Fori(1, FF_STEPS) as i:
                    g(u0 - 1, i, i)
                    u(u0, i, i)
                    d(u0 + 1, i - 1, i)
                d(u0 + 3 * FF_STEPS - 1, FF_STEPS - 1)

            def cols_units(u0, src, c0, n, wide=256):
                for j in range(n):
                    load(u0 + j, src[:, c0 + wide * j:c0 + wide * (j + 1)], wide)

            def rows_units(u0, src, n):
                for j in range(n):
                    load(u0 + j, src[256 * j:256 * (j + 1), :], D)

            x_in, x_out = (a.rearrange("o (t p) d -> p (o t) d", p=P) for a in (w["x"], out))
            sp.dma_start(H[:, 0, :], x_in[:, 0, :]).then_inc(x_loaded[0], 16)
            sp.dma_start(H[:, 1, :], x_in[:, 1, :]).then_inc(x_loaded[1], 16)
            sp.dma_start(TAB[:], w["tables"]).then_inc(tab_loaded, 16)
            ffn_loads(U_FFN1, w["ffn1_w_gate"], w["ffn1_w_up"], w["ffn1_w_down"])
            for m, (kind, n) in enumerate(XZ):
                c0 = {"z": 256 * n, "dt": C_DT, "x": C_XBC + 256 * n}[kind]
                wide = SSD_HEADS if kind == "dt" else 256
                load(U_XZ + m, w["w_in"][:, c0:c0 + wide], wide)
            cols_units(U_QKV, w["w_in"], C_Q, 12)
            rows_units(U_SSDW, w["ssd_w_branch"], 8)
            cols_units(U_GATE, w["w_in"], C_GATE, 8)
            rows_units(U_DAW, w["da_w_branch"], 4)
            rows_units(U_WOUT, w["w_out"], 4)
            ffn_loads(U_FFN2, w["ffn2_w_gate"], w["ffn2_w_up"], w["ffn2_w_down"])
            cols_units(U_IN2, w["w_in_2"], 0, 5)
            load(U_IN2 + 5, w["w_in_2"][:, 1280:PJ], PJ - 1280)
            cols_units(U_GATE2A, w["w_in_2"], PJ, 2)
            cols_units(U_UQ, w["w_uq_2"], 0, 2, 384)
            load(U_UKV, w["w_ukv_2"], D)
            cols_units(U_GATE2B, w["w_in_2"], PJ + 512, 6)
            rows_units(U_OSWA, w["w_o_swa_2"], 2)
            rows_units(U_OMLA, w["w_o_mla_2"], 2)
            rows_units(U_OUT2, w["w_out_2"], 4)
            ffn_loads(U_FFN3, w["w_gate_2"], w["w_up_2"], w["w_down_2"])
            for t in range(NT):
                sp.wait_ge(out_ok, t + 1)
                sp.dma_start(x_out[:, t, :], XN[:, t, :]).then_inc(stored, 16)
            sp.wait_ge(stored, 16 * NT)

        @block.scalar
        def _(act):
            own = Steps(act, act_steps)

            def split_hi(c, i=0):
                if isinstance(i, int) and c >= U_END:
                    return
                s = slot(c)
                act.wait_ge(raw[s], 16 * (c // RING + i + 1))
                if c >= RING or not isinstance(i, int):
                    act.wait_ge(w_used, c + RING * i - RING + 1)
                nc.scalar.activation(WH[:, s, :], RAW[:, s, :], ACT.Copy).then_inc(w_hi, 1)

            def rsqrt(dst, src, n, signal, eps_scale=1.0 / D):
                own.wait()
                own.link(nc.scalar.activation(dst, src, ACT.Ln, scale=eps_scale, bias=EPS))
                nc.scalar.activation(dst, dst, ACT.Exp, scale=-0.5).then_inc(signal, 1)
                act.wait_ge(signal, n)

            def ln_exp():
                nc.scalar.preload_act_table_set("natural_log_exp_and_others")

            def h_rstd(n, t):
                if n:
                    act.wait_ge(h_done, NT * (n - 1) + t + 1)
                else:
                    act.wait_ge(x_loaded[t], 16)
                own.wait() if own.n else None
                own.link(nc.scalar.activation(XN[:, t, :], H[:, t, :], ACT.Square, accum_out=SS[:, t:t + 1]))
                own.link(nc.scalar.activation(RS[:, t:t + 1], SS[:, t:t + 1], ACT.Ln, scale=1.0 / D, bias=EPS))
                nc.scalar.activation(RS[:, t:t + 1], RS[:, t:t + 1], ACT.Exp, scale=-0.5).then_inc(rstd_ok, 1)

            def xn_hi(n, t):
                for q in range(2):
                    act.wait_ge(xn_turned, 4 * n + 2 * t + q + 1)
                    nc.scalar.activation(XTH[:, 4 * q:4 * q + 4, t * P:(t + 1) * P],
                                         PS[6 + q][:].rearrange("p (k c) -> p k c", k=4), ACT.Copy).then_inc(xt_hi, 1)

            def ffn(f, u0, last):
                n0 = FF_STEPS * f

                def g_part(c, j, i=0):
                    split_hi(c + 3, i)
                    act.wait_ge(w_used, c + 3 * i + 1)
                    if not isinstance(j, int) or j:
                        act.wait_ge(h_ready, j + n0)
                    nc.scalar.activation(SG, PS[4][:], ACT.Silu).then_inc(gate_ok, 1)

                def hidden_hi(j):
                    act.wait_ge(h_ready, j + n0 + 1)
                    nc.scalar.activation(KTH[:, 0:512], HS, ACT.Copy).then_inc(hT_hi, 1)
                g_part(u0, 0)
                split_hi(u0 + 4)
                hidden_hi(0)

                def step(c, j, i=0):
                    g_part(c, j, i)
                    split_hi(c + 4, i)
                    split_hi(c + 5, i)
                    act.wait_ge(w_used, c + 3 * i + 3)
                    hidden_hi(j)
                end = FF_STEPS - last
                with act.Fori(1, end) as i:
                    step(u0 - 1, i, i)
                if last:
                    step(u0 + 3 * FF_STEPS - 4, FF_STEPS - 1)

            def y_squares(m, unit, t):
                act.wait_ge(acc_half, m + 1) if t == 0 else act.wait_ge(w_used, unit + 1)
                for b in (2 * t, 2 * t + 1):
                    if b % 2:
                        act.wait_ge(y_gained, 4 * post_no[m] + b)
                    own.wait()
                    nc.scalar.activation(XN[:, t, (b % 2) * 512:(b % 2 + 1) * 512], PS[b][:], ACT.Square,
                                         accum_out=SS[:, 8 + b:9 + b]).then_inc(y_sq, 1)

            def y_rstd(m, t, half):
                act.wait_ge(y_ss, NT * post_no[m] + t + 1)
                own.link(nc.scalar.activation(RS[:, 8 + t:9 + t], RS[:, 8 + t:9 + t], ACT.Ln, scale=1.0 / D, bias=EPS))
                nc.scalar.activation(RS[:, 8 + t:9 + t], RS[:, 8 + t:9 + t], ACT.Exp, scale=-0.5,
                                     bias=math.log(0.5) if half else 0.0).then_inc(y_rs, 1)

            def boundary(m, unit, half, next_table=None):
                ln_exp()
                if m in post_no:
                    y_squares(m, unit, 0)
                    y_rstd(m, 0, half)
                    y_squares(m, unit, 1)
                    h_rstd(m + 1, 0)
                    y_rstd(m, 1, half)
                else:
                    h_rstd(m + 1, 0)
                if m == 4:
                    h_rstd(m + 1, 1)
                    return
                xn_hi(m + 1, 0)
                h_rstd(m + 1, 1)
                if next_table:
                    nc.scalar.preload_act_table(next_table)
                xn_hi(m + 1, 1)
                split_hi(unit + 3)

            def kt_hi(n, prev_unit, scale=1.0):
                act.wait_ge(k_turned, n + 1)
                act.wait_ge(w_used, prev_unit)
                nc.scalar.activation(KTH[:, half_of(n)], PS[7][:], ACT.Copy, scale=scale).then_inc(k_hi, 1)

            def products(n0, u0, n, scale=1.0):
                for j in range(n):
                    kt_hi(n0 + j, u0 + j - 1, scale)
                    if j:
                        split_hi(u0 + j - 1 + 3)

            ln_exp()
            for t in range(NT):
                h_rstd(0, t)
            nc.scalar.preload_act_table(ACT.Silu)
            split_hi(0)
            xn_hi(0, 0)
            split_hi(1)
            xn_hi(0, 1)
            split_hi(2)
            ffn(0, U_FFN1, 0)
            boundary(0, U_FFN1 + 3 * FF_STEPS - 1, True)

            def z_silu(n):
                nc.scalar.activation(BUF2[:, :, n * 256:(n + 1) * 256],
                                     PS[n % 2][:].rearrange("p (t c) -> p t c", t=NT), ACT.Silu).then_inc(z_kept, 1)

            for m, (kind, n) in enumerate(XZ):
                c = U_XZ + m
                if kind == "x":
                    act.wait_ge(w_used, c + 1)
                    if n:
                        act.wait_ge(conv_silu, n)
                    for f in range(2):
                        j = 2 * n + f
                        tap = GC["conv_w"] + 3 * XBC_TILES + j
                        ins = nc.scalar.activation(CONV[:, f * TOK:(f + 1) * TOK],
                                                   PS[4 + n % 2][:, f * TOK:(f + 1) * TOK], ACT.Identity,
                                                   scale=COLS[:, tap:tap + 1],
                                                   bias=COLS[:, GC["conv_b"] + j:GC["conv_b"] + j + 1])
                    ins.then_inc(conv_1, 1)
                    split_hi(c + 3)
                    act.wait_ge(conv_done, n + 1)
                    if n < 8:
                        if n:
                            act.wait_ge(x_turned, n)
                        nc.scalar.activation(XSIL, CONV, ACT.Silu).then_inc(conv_silu, 1)
                    else:
                        nc.scalar.activation(BC[:, (n - 8) * 512:(n - 7) * 512], CONV, ACT.Silu).then_inc(conv_silu, 1)
                elif kind == "z":
                    split_hi(c + 3)
                    if n >= 2:
                        act.wait_ge(w_used, c + 1)
                        z_silu(n)
                else:
                    split_hi(c + 3)
                    own.inc(nc.scalar.activation(DT[:, 5, 0:32], ROWS[:, ROW["a_log"]:ROW["a_log"] + 32], ACT.Exp))
                    act.wait_ge(dt_abs, 1)
                    own.wait()
                    nc.scalar.activation(DT[:, 1, :], DT[:, 1, :], ACT.Exp).then_inc(dt_exp, 1)
                    act.wait_ge(lam_dot, 1)
                    nc.scalar.activation(SM[:, 36:38], SM[:, 36:38], ACT.Exp).then_inc(lam_exp, 1)
                    nc.scalar.preload_act_table(ACT.Silu)
                    z_silu(0)
                    z_silu(1)
            ln_exp()
            act.wait_ge(cums_neg, 1)
            nc.scalar.activation(EX[:].rearrange("p a t h -> p (a t h)"), PS[3][:, 0:128], ACT.Exp).then_inc(cums_exp, 1)

            u = U_QKV
            for r in range(9):
                if r < 8:
                    g, c = divmod(r, 2)
                    act.wait_ge(ssd_mm, r + 1)
                    if r:
                        act.wait_ge(ssd_y, r)
                    else:
                        act.wait_ge(x_kept, 9)
                    for e in range(HPG):
                        ins = nc.scalar.activation(E[:, e, :], PS[e // 4][:, (e % 4) * P:(e % 4 + 1) * P], ACT.Exp,
                                                   bias=DT[:, 4, c * 32 + g * HPG + e:c * 32 + g * HPG + e + 1])
                    ins.then_inc(ssd_e, 1)
                if r:
                    n = r - 1
                    if n % 2 == 0:
                        act.wait_ge(ssd_st, n + 1)
                        nc.scalar.activation(STATE, PS[6][:], ACT.Copy).then_inc(state_ok, 1)
                    act.wait_ge(y_gated, n + 1)
                    act.wait_ge(ssd_m, min(r + 1, 8)) if r < 8 else None
                    own.inc(nc.scalar.activation(T1, Y, ACT.Square, accum_out=SS[:, 4:5]))
                    rsqrt(RS[:, 4:5], SS[:, 4:5], n + 1, y_rms, 1.0 / GW)
                if r < 8:
                    for _u in range(1 + r % 2):
                        n = u - U_QKV
                        split_hi(u + 3)
                        act.wait_ge(w_used, u + 1)
                        src = PS[5 - n % 2][:].rearrange("p (f t) -> p f t", f=2)
                        if n < 8:
                            dst = QK[:, 2 * (n % 4):2 * (n % 4) + 2, n // 4, :]
                        else:
                            dst = V[:, :, (n - 8) * 256:(n - 7) * 256]
                        nc.scalar.activation(dst, src, ACT.Copy).then_inc(qkv_kept, 1)
                        u += 1

            for h in range(9):
                if h:
                    act.wait_ge(p_turned, h)
                    nc.scalar.activation(PT, PS[6][:, 0:384], ACT.Copy).then_inc(p_kept, 1)
                if h < 8:
                    kt_hi(h, U_SSDW + h - 1)
                    if h:
                        split_hi(U_SSDW + h - 1 + 3)
                    act.wait_ge(s_ready, h + 1)
                    for m in range(2):
                        for i, ks in enumerate((slice(0, P), slice(P, 3 * P))):
                            n = 2 * i + m
                            ins = nc.scalar.activation(SMAP[:, m, ks], SMAP[:, m, ks], ACT.Exp, scale=0.125,
                                                       bias=SM[:, 4 + n:5 + n], accum_out=SM[:, 8 + n:9 + n])
                            if i == 0:
                                own.inc(ins)
                        ins.then_inc(p_exp, 1)
                if h:
                    act.wait_ge(o_kept, h)
                    for i in range(NT):
                        own.wait()
                        own.inc(nc.scalar.activation(SQJ[:, i * P:(i + 1) * P], XN[:, i, (h - 1) * P:h * P], ACT.Square,
                                                     accum_out=SS[:, i * 8 + h - 1:i * 8 + h]))
            split_hi(U_SSDW + 7 + 3)
            rsqrt(RS[:], SS[:], 1, o_rs, 1.0 / P)

            nc.scalar.preload_act_table(ACT.Sigmoid)
            for n in range(8):
                split_hi(U_GATE + n + 3)
                act.wait_ge(g_logit, n + 1)
                s = BUF1[:, :, n * 256:(n + 1) * 256]
                nc.scalar.activation(s, s, ACT.Sigmoid).then_inc(gates_ok, 1)
            products(8, U_DAW, 4, SUBLN)
            split_hi(U_DAW + 3 + 3)
            products(12, U_WOUT, 4)
            boundary(1, U_WOUT + 3, False, ACT.Silu)
            ffn(1, U_FFN2, 0)
            boundary(2, U_FFN2 + 3 * FF_STEPS - 1, True)

            for n in range(6):
                wide = 256 if n < 5 else PJ - 1280
                split_hi(U_IN2 + n + 3)
                act.wait_ge(w_used, U_IN2 + n + 1)
                nc.scalar.activation(PROJ[:, :, n * 256:n * 256 + wide],
                                     PS[(4, 5, 0, 1)[n % 4]][:].rearrange("p (t c) -> p t c", t=NT)[:, :, 0:wide],
                                     ACT.Copy).then_inc(proj_kept, 1)
            own.wait()
            act.wait_ge(proj_kept, 6)
            for t in range(NT):
                own.inc(nc.scalar.activation(XN[:, t, 0:Q_RANK], PROJ[:, t, LAT0:LAT0 + Q_RANK], ACT.Square,
                                             scale=Q_RANK ** -0.5, accum_out=SS[:, t:t + 1]))
                own.inc(nc.scalar.activation(XN[:, t, Q_RANK:Q_RANK + KV_RANK],
                                             PROJ[:, t, LAT0 + Q_RANK:KR0], ACT.Square,
                                             scale=KV_RANK ** -0.5, accum_out=SS[:, 2 + t:3 + t]))
            rsqrt(RS[:, 0:4], SS[:, 0:4], 1, lat_rs, 1.0)
            for r in range(3):
                act.wait_ge(swa_turned, r + 1)
                dst = GAIN[:, r * 512:(r + 1) * 512]
                nc.scalar.activation(dst, PS[2 + r][:], ACT.Copy).then_inc(swa_kept, 1)

            def g2(n, u):
                split_hi(u + 3)
                act.wait_ge(w_used, u + 1)
                nc.scalar.activation(BUF2[:, :, n * 256:(n + 1) * 256],
                                     PS[n % 2][:].rearrange("p (t c) -> p t c", t=NT), ACT.Copy).then_inc(g2_kept, 1)
            g2(0, U_GATE2A)
            for j in range(3):
                act.wait_ge(lat_turned, 1 + j // 2)
                ins = nc.scalar.activation(KTH[:, j * TOK:(j + 1) * TOK],
                                           PS[6 + j // 2][:, (j % 2) * TOK:(j % 2 + 1) * TOK], ACT.Copy,
                                           scale=COLS[:, GC["q_lat"] + j:GC["q_lat"] + j + 1])
                if j:
                    ins.then_inc(lat_hi, 1)
            g2(1, U_GATE2A + 1)
            for n in range(2):
                split_hi(U_UQ + n + 3)
                act.wait_ge(w_used, U_UQ + n + 1)
                for t in range(NT):
                    ins = nc.scalar.activation(QM[:, t, 4 * n:4 * n + 4, :].rearrange("p h c -> p (h c)"),
                                               PS[2 + 2 * n + t][:, 0:384], ACT.Copy)
                    ins.then_inc(q_kept, 1)
            act.wait_ge(lat_turned, 3)
            for j in range(2):
                ins = nc.scalar.activation(KTH[:, j * TOK:(j + 1) * TOK], PS[7][:, j * TOK:(j + 1) * TOK], ACT.Copy,
                                           scale=COLS[:, GC["kv_lat"] + j:GC["kv_lat"] + j + 1])
            ins.then_inc(lat_hi, 1)
            split_hi(U_UKV + 3)
            act.wait_ge(w_used, U_UKV + 1)
            for b in range(4):
                nc.scalar.activation(V[:, b // 2, (b % 2) * 512:(b % 2 + 1) * 512], PS[2 + b][:],
                                     ACT.Copy).then_inc(kv_kept, 1)

            for r in range(9):
                if r < 8:
                    act.wait_ge(mla_turned, r + 1)
                    nc.scalar.activation(QK[0:MLA_QK, r, :, :], PS[7][0:MLA_QK, :].rearrange("p (a t) -> p a t", a=2),
                                         ACT.Copy).then_inc(mla_kept, 1)
                if r:
                    for a in range(2):
                        act.wait_ge(p2_turned, 2 * (r - 1) + a + 1)
                        nc.scalar.activation(PT2[a], PS[4 + a][:, 0:384], ACT.Copy).then_inc(p2_kept, 1)
                if r < 8:
                    for a in range(2):
                        act.wait_ge(s2_ready, 2 * r + a + 1)
                        scale = (HD ** -0.5, MLA_QK ** -0.5)[a]
                        for i in range(NT):
                            p = SC[a][:, i * P:i * P + P * (i + 1)]
                            ins = nc.scalar.activation(p, p, ACT.Exp, scale=scale, bias=SM[:, 2 * a + i:2 * a + i + 1],
                                                       accum_out=SM[:, 4 + 2 * a + i:5 + 2 * a + i])
                            if a == 0 or i == 0:
                                own.inc(ins)
                        if a == 0:
                            ins = nc.scalar.activation(SM[:, 8:10], SM[:, 0:2], ACT.Exp,
                                                       bias=ROWS[:, ROW["sinks"] + r:ROW["sinks"] + r + 1])
                        ins.then_inc(p2_exp, 1)
                    if r < 6:
                        g2(2 + r, U_GATE2B + r)
            nc.scalar.preload_act_table(ACT.Sigmoid)
            act.wait_ge(g2_kept, 8)
            for b in range(4):
                s = BUF2[:, b % 2, (b // 2) * D:(b // 2 + 1) * D]
                nc.scalar.activation(s, s, ACT.Sigmoid).then_inc(gates2, 1)
            products(16, U_OSWA, 2)
            split_hi(U_OSWA + 1 + 3)
            products(18, U_OMLA, 2)
            split_hi(U_OMLA + 1 + 3)
            products(20, U_OUT2, 4)
            boundary(3, U_OUT2 + 3, False, ACT.Silu)
            ffn(2, U_FFN3, 1)
            boundary(4, U_END - 1, False)

        @block.gpsimd
        def _(pool):

            def gain(name, n=1):
                pool.dma_start(GAIN[:, 0:n * D], w[name].partition_broadcast(P)).then_inc(gain_loaded, 16)

            def pre_gain(name):
                pool.dma_start(GPRE, w[name].partition_broadcast(P)).then_inc(gpre_loaded, 16)

            pre_gain("ffn1_pre_g")
            gain("ffn1_post_g")
            pool.wait_ge(xn_ok, NT)
            pre_gain("mix_pre_g")
            pool.wait_ge(h_done, NT)
            gain("ssd_norm_g", 2)
            pool.dma_start(XDT[:, 0:256], w["lam"].partition_broadcast(P)).then_inc(lam_loaded, 16)
            pool.wait_ge(loaded, 32)
            pool.wait_ge(a_ok, 1)

            def spread_a(r):
                g, c = divmod(r, 2)
                if r:
                    pool.wait_ge(ssd_mm, r)
                a = DT[:, 3, c * 32 + g * HPG:c * 32 + (g + 1) * HPG]
                nc.gpsimd.tensor_copy(AB, a.unsqueeze(2).to_broadcast([P, HPG, P])).then_inc(ab_ok, 1)

            for r in range(8):
                g, c = divmod(r, 2)
                if r == 0:
                    spread_a(0)
                if r < 7:
                    spread_a(r + 1)
                if r:
                    pool.wait_ge(ys_ok, r)
                skip = ROWS[:, ROW["skip"] + g * HPG:ROW["skip"] + (g + 1) * HPG]
                nc.gpsimd.tensor_tensor(Y.rearrange("p (h c) -> p h c", h=HPG),
                                        BUF1[:, c, g * GW:(g + 1) * GW].rearrange("p (h c) -> p h c", h=HPG),
                                        skip.unsqueeze(2).to_broadcast([P, HPG, SSD_P]), ALU.mult).then_inc(skip_ok, 1)
            pool.wait_ge(ys_ok, 8)
            gain("gate_b", 2)
            pre_gain("ffn2_pre_g")
            pool.wait_ge(g_logit, 8)
            gain("mix_post_g")
            pool.wait_ge(h_done, 2 * NT)
            gain("ffn2_post_g")
            pool.wait_ge(xn_ok, 3 * NT)
            pre_gain("mix_norm_g_2")
            pool.wait_ge(swa_roped, 1)
            for t in range(NT):
                ins = nc.gpsimd.tensor_copy(
                    KDUP[:, t], PROJ[:, t, 512:640].rearrange("p (j c) -> p j c", j=SWA_KV).unsqueeze(2)
                    .to_broadcast([P, SWA_KV, 2, HD]))
            ins.then_inc(kdup_ok, 1)
            pool.wait_ge(sc2, 2 * SWA_HEADS)
            gain("final_norm_g_2")
            pool.wait_ge(pv2, SWA_HEADS)
            pre_gain("ffn_norm_g_2")

        @block.vector
        def _(dve):
            own = Steps(dve, dve_steps)
            tt, ts, stt = nc.vector.tensor_tensor, nc.vector.tensor_scalar, nc.vector.scalar_tensor_tensor

            def split_lo(c, i=0):
                if isinstance(i, int) and c >= U_END:
                    return
                s = slot(c)
                dve.wait_ge(w_hi, c + RING * i + 1)
                tt(WL[:, s, :], RAW[:, s, :], WH[:, s, :].bitcast(F32), ALU.subtract).then_inc(w_lo, 1)

            def xn(n, t):
                dve.wait_ge(rstd_ok, NT * n + t + 1)
                dve.wait_ge(gpre_loaded, 16 * (n + 1))
                stt(XN[:, t, :], H[:, t, :], RS[:, t:t + 1], GPRE, ALU.mult, ALU.mult).then_inc(xn_ok, 1)

            def xn_lo(n, t):
                for q in range(2):
                    dve.wait_ge(xt_hi, 4 * n + 2 * t + q + 1)
                    a = (slice(None), slice(4 * q, 4 * q + 4), slice(t * P, (t + 1) * P))
                    tt(XTL[a], PS[6 + q][:].rearrange("p (k c) -> p k c", k=4), XTH[a].bitcast(F32),
                       ALU.subtract).then_inc(xt_lo, 1)

            def ffn(f, u0, last):
                n0 = FF_STEPS * f

                def up_part(c, j, i=0):
                    dve.wait_ge(gate_ok, j + n0 + 1)
                    dve.wait_ge(w_used, c + 3 * i + 2)
                    if not isinstance(j, int) or j:
                        dve.wait_ge(hT_lo, j + n0)
                    tt(HS, PS[5][:], SG, ALU.mult).then_inc(h_ready, 1)

                def hidden_lo(j):
                    dve.wait_ge(hT_hi, j + n0 + 1)
                    tt(KTL[:, 0:512], HS, KTH[:, 0:512].bitcast(F32), ALU.subtract).then_inc(hT_lo, 1)
                split_lo(u0 + 3)
                split_lo(u0 + 4)
                up_part(u0, 0)
                hidden_lo(0)

                def step(c, j, i=0):
                    split_lo(c + 3, i)
                    split_lo(c + 4, i)
                    up_part(c, j, i)
                    split_lo(c + 5, i)
                    hidden_lo(j)
                with dve.Fori(1, FF_STEPS - last) as i:
                    step(u0 - 1, i, i)
                if last:
                    step(u0 + 3 * FF_STEPS - 4, FF_STEPS - 1)

            def y_gain(m, unit, t):
                dve.wait_ge(acc_half, m + 1) if t == 0 else dve.wait_ge(w_used, unit + 1)
                for b in (2 * t + 1, 2 * t):
                    if b % 2 == 0:
                        dve.wait_ge(y_sq, 4 * post_no[m] + b + 1)
                    tt(TB[:, b, :], PS[b][:], GAIN[:, (b % 2) * 512:(b % 2 + 1) * 512], ALU.mult).then_inc(y_gained, 1)

            def y_sum(m, t):
                dve.wait_ge(y_sq, 4 * post_no[m] + 2 * t + 2)
                tt(RS[:, 8 + t:9 + t], SS[:, 8 + 2 * t:9 + 2 * t], SS[:, 9 + 2 * t:10 + 2 * t],
                   ALU.add).then_inc(y_ss, 1)

            def residual(m, t):
                dve.wait_ge(y_rs, NT * post_no[m] + t + 1)
                dve.wait_ge(y_gained, 4 * post_no[m] + 2 * t + 2)
                stt(H[:, t, :], TB[:, 2 * t:2 * t + 2, :].rearrange("p b c -> p (b c)"), RS[:, 8 + t:9 + t], H[:, t, :],
                    ALU.mult, ALU.add).then_inc(h_done, 1)

            def add_h(m, unit, t):
                dve.wait_ge(acc_half, m + 1) if t == 0 else dve.wait_ge(w_used, unit + 1)
                for h in range(2):
                    s = H[:, t, h * 512:(h + 1) * 512]
                    ins = tt(s, PS[2 * t + h][:], s, ALU.add)
                    ins.then_inc(h_done, 1) if h else own.inc(ins)
                own.wait()

            def boundary(m, unit, gains=0):
                own.wait()
                if m in post_no:
                    dve.wait_ge(gain_loaded, 16 * gains)
                    y_gain(m, unit, 0)
                    y_sum(m, 0)
                    residual(m, 0)
                    y_gain(m, unit, 1)
                    y_sum(m, 1)
                    xn(m + 1, 0)
                    residual(m, 1)
                else:
                    add_h(m, unit, 0)
                    if m < 4:
                        xn(m + 1, 0)
                    add_h(m, unit, 1)
                if m == 4:
                    return
                xn_lo(m + 1, 0)
                xn(m + 1, 1)
                xn_lo(m + 1, 1)
                split_lo(unit + 3)

            def kt_lo(n, scale=None):
                dve.wait_ge(k_hi, n + 1)
                if scale is None:
                    ins = tt(KTL[:, half_of(n)], PS[7][:], KTH[:, half_of(n)].bitcast(F32), ALU.subtract)
                else:
                    ins = stt(KTL[:, half_of(n)], PS[7][:], scale, KTH[:, half_of(n)].bitcast(F32), ALU.mult, ALU.subtract)
                ins.then_inc(k_lo, 1)

            def products(n0, u0, n, scale=None):
                for j in range(n):
                    kt_lo(n0 + j, scale)
                    if j:
                        split_lo(u0 + j - 1 + 3)

            xn(0, 0)
            xn(0, 1)
            split_lo(0)
            xn_lo(0, 0)
            split_lo(1)
            xn_lo(0, 1)
            split_lo(2)
            dve.wait_ge(loaded, 32)
            dve.wait_ge(tab_loaded, 16)
            own.inc(nc.vector.tensor_copy(ID16[:], IDENT))
            nc.vector.tensor_copy(MASK16[:], tab("causal_t").unsqueeze(1).to_broadcast([P, 4, P])).then_inc(consts16, 1)
            own.link(ts(SUBLN, SUBLN, 1.0 - LAM_INIT, None, ALU.mult))
            ffn(0, U_FFN1, 0)
            boundary(0, U_FFN1 + 3 * FF_STEPS - 1, 1)

            def x_keep(m):
                dve.wait_ge(x_turned, m + 1)
                nc.vector.tensor_copy(
                    BUF1[:, :, m * 256:(m + 1) * 256].rearrange("p t (f c) -> p f t c", f=2),
                    PS[6 + m % 2][:].rearrange("p (f t c) -> p f t c", f=2, t=NT)).then_inc(x_kept, 1)

            def step_sizes(c):
                dve.wait_ge(w_used, U_XZ + 3)
                bias = ROWS[:, ROW["dt_bias"]:ROW["dt_bias"] + 32].unsqueeze(1).to_broadcast([P, NT, 32])
                tt(DT[:, 0, :].rearrange("p (t h) -> p t h", t=NT),
                   PS[5][:].rearrange("p (t c) -> p t c", t=NT)[:, :, 0:32], bias, ALU.add).then_inc(dt_raw, 1)
                dve.wait_ge(dt_raw, 1)
                stt(DT[:, 1, :], DT[:, 0, :], -1.0, DT[:, 0, :], ALU.mult, ALU.min).then_inc(dt_abs, 1)
                own.link(ts(DT[:, 0, :], DT[:, 0, :], 0.0, None, ALU.max))
                dve.wait_ge(lam_loaded, 16)
                lam = XDT[:, 0:256].rearrange("p (a b c) -> p a b c", a=2, b=2)
                T1L = T1[:, 0:128].rearrange("p (a c) -> p a c", a=2)
                own.link(tt(T1L, lam[:, :, 0, :], lam[:, :, 1, :], ALU.mult))
                nc.vector.tensor_reduce(SM[:, 36:38], T1L, AX.X, ALU.add).then_inc(lam_dot, 1)
                split_lo(c + 3)
                dve.wait_ge(dt_exp, 1)
                e, y, z, q = DT[:, 1, :], DT[:, 2, :], DT[:, 3, :], DT[:, 4, :]
                own.link(ts(y, e, 2.0, None, ALU.add))
                own.link(nc.vector.reciprocal(y, y))
                own.link(tt(y, y, e, ALU.mult))
                own.link(tt(z, y, y, ALU.mult))
                own.link(ts(q, z, 1.0 / 15, None, ALU.mult))
                for d in (13, 11, 9, 7, 5, 3):
                    own.link(stt(q, q, 1.0 / d, z, ALU.add, ALU.mult))
                own.link(stt(q, q, 1.0, y, ALU.add, ALU.mult))
                own.link(stt(DT[:, 2, :], q, 2.0, DT[:, 0, :], ALU.mult, ALU.add))
                stt(DT[:, 3, :].rearrange("p (t h) -> p t h", t=NT), DT[:, 2, :].rearrange("p (t h) -> p t h", t=NT), -1.0,
                    DT[:, 5, 0:32].unsqueeze(1).to_broadcast([P, NT, 32]), ALU.mult, ALU.mult).then_inc(a_ok, 1)
                dve.wait_ge(lam_exp, 1)
                own.link(tt(SM[:, 38:39], SM[:, 37:38], SM[:, 36:37], ALU.subtract))
                ts(SM[:, 39:40], SM[:, 38:39], -LAM_INIT, None, ALU.add).then_inc(lam_ok, 1)
                dve.wait_ge(lam_ok, 1)
                own.link(ts(ROWS[:, ROW["dt_bias"]:ROW["dt_bias"] + 8], ROWS[:, ROW["sinks"]:ROW["sinks"] + 8], -1.0, None, ALU.mult))

            for m, (kind, n) in enumerate(XZ):
                c = U_XZ + m
                if kind == "dt":
                    step_sizes(c)
                    continue
                if kind == "x":
                    dve.wait_ge(conv_1, n + 1)
                    for back in (1, 2, 3):
                        for f in range(2):
                            j = GC["conv_w"] + (CONV_K - 1 - back) * XBC_TILES + 2 * n + f
                            dst = CONV[:, f * TOK + back:(f + 1) * TOK]
                            ins = stt(dst, PS[4 + n % 2][:, f * TOK:(f + 1) * TOK - back], COLS[:, j:j + 1], dst,
                                      ALU.mult, ALU.add)
                            if back == 3 and f == 1:
                                ins.then_inc(conv_done, 1)
                            else:
                                own.inc(ins)
                        if back < 3:
                            own.wait()
                    if 1 <= n <= 8:
                        x_keep(n - 1)
                split_lo(c + 3)
            dve.wait_ge(x_turned, 9)
            nc.vector.tensor_copy(B0, PS[6][:]).then_inc(x_kept, 1)
            dve.wait_ge(cums, 1)
            ts(DT[:, 4, :].rearrange("p (t h) -> p t h", t=NT),
               PS[3][:, 0:64].rearrange("p (t h) -> p t h", t=NT), -1.0, None, ALU.mult).then_inc(cums_neg, 1)
            dve.wait_ge(cums_exp, 1)
            dve.wait_ge(gain_loaded, 32)

            def by_head(ap):
                return ap.rearrange("p (h c) -> p h c", h=HPG)

            def heads_bc(ap):
                return ap.unsqueeze(2).to_broadcast([P, HPG, SSD_P])

            u = U_QKV
            for r in range(9):
                if r < 8:
                    g, c = divmod(r, 2)
                    xs = BUF1[:, c, g * GW:(g + 1) * GW]
                    hs = slice(c * 32 + g * HPG, c * 32 + (g + 1) * HPG)
                    if r:
                        dve.wait_ge(ssd_y, r)
                    own.link(tt(by_head(XDT), by_head(xs), heads_bc(DT[:, 2, hs]), ALU.mult))
                    if c == 0:
                        tt(by_head(XDEC), by_head(XDT), heads_bc(EX[:, 1, c, g * HPG:(g + 1) * HPG]),
                           ALU.mult).then_inc(xdec_ok, 1)
                if r:
                    n = r - 1
                    g, c = divmod(n, 2)
                    dve.wait_ge(skip_ok, r)
                    dve.wait_ge(ssd_y, r)
                    own.link(tt(Y, PS[3][:], Y, ALU.add))
                    if c:
                        dve.wait_ge(ssd_st, r)
                        own.link(tt(by_head(T1), by_head(PS[6][:]),
                                    heads_bc(EX[:, 0, c, g * HPG:(g + 1) * HPG]), ALU.mult))
                        own.link(tt(Y, Y, T1, ALU.add))
                    zs = BUF2[:, c, g * GW:(g + 1) * GW]
                    tt(Y, Y, zs, ALU.mult).then_inc(y_gated, 1)
                if r < 8:
                    dve.wait_ge(ssd_e, r + 1)
                    dve.wait_ge(ssd_cb, r + 1)
                    for b in range(2):
                        ins = tt(E[:, 4 * b:4 * b + 4, :], E[:, 4 * b:4 * b + 4, :],
                                 PS[2][:, 0:P].unsqueeze(1).to_broadcast([P, 4, P]), ALU.mult)
                    ins.then_inc(ssd_m, 1)
                if r:
                    dve.wait_ge(y_rms, r)
                    stt(zs, Y, RS[:, 4:5], GAIN[:, g0(n) * GW:(g0(n) + 1) * GW], ALU.mult, ALU.mult).then_inc(ys_ok, 1)
                else:
                    def g0(n):
                        return n // 2
                if r < 8:
                    for _u in range(1 + r % 2):
                        split_lo(u + 3)
                        u += 1

            slopes = [2.0 ** (-8.0 * (h + 1) / DA_HEADS) for h in range(DA_HEADS)]

            def o_keep(h):
                dve.wait_ge(pv, h + 1)
                nc.vector.tensor_copy(XN[:, :, h * P:(h + 1) * P],
                                      PS[6][:, 0:256].rearrange("p (i c) -> p i c", i=NT)).then_inc(o_kept, 1)
            dve.wait_ge(ys_ok, 8)
            for h in range(9):
                if h < 8:
                    kt_lo(h)
                    dve.wait_ge(scores, h + 1)
                    if h:
                        own.wait()
                    f = -8.0 * slopes[h]
                    for m in range(2):
                        own.inc(stt(SMAP[:, m, :], tab("dist"), f, PS[4 + m][:, 0:384], ALU.mult, ALU.add))
                    own.wait()
                    own.inc(nc.vector.tensor_reduce(SM[:, 0:2], SMAP[:, :, 0:P], AX.X, ALU.max))
                    own.link(nc.vector.tensor_reduce(SM[:, 2:4], SMAP[:, :, P:3 * P], AX.X, ALU.max))
                    ts(SM[:, 4:8], SM[:, 0:4], -0.125, None, ALU.mult).then_inc(s_ready, 1)
                    if h:
                        split_lo(U_SSDW + h - 1 + 3)
                if h:
                    o_keep(h - 1)
                if h < 8:
                    dve.wait_ge(p_exp, 2 * (h + 1))
                    own.link(nc.vector.reciprocal(SM[:, 12:16], SM[:, 8:12]))
                    own.link(ts(SM[:, 16:20], SM[:, 12:16], SM[:, 39:40], None, ALU.mult))
                    if h:
                        dve.wait_ge(p_turned, h)
                    own.inc(ts(ATT[:, 0:P], SMAP[:, 0, 0:P], SM[:, 12:13], None, ALU.mult))
                    own.link(ts(ATT[:, P:3 * P], SMAP[:, 0, P:3 * P], SM[:, 14:15], None, ALU.mult))
                    own.inc(stt(ATT[:, 0:P], SMAP[:, 1, 0:P], SM[:, 17:18], ATT[:, 0:P], ALU.mult, ALU.add))
                    stt(ATT[:, P:3 * P], SMAP[:, 1, P:3 * P], SM[:, 19:20], ATT[:, P:3 * P], ALU.mult,
                        ALU.add).then_inc(attn_ok, 1)
                    dve.wait_ge(attn_ok, h + 1)
            split_lo(U_SSDW + 7 + 3)
            dve.wait_ge(o_rs, 1)
            o4 = XN[:].rearrange("p t (h c) -> p (t h) c", c=P)
            tt(o4, o4, RS[:].unsqueeze(2).to_broadcast([P, 16, P]), ALU.mult).then_inc(o_ok, 1)

            dve.wait_ge(gain_loaded, 48)

            def first_merge(gates, b, signal):
                t, cols = b // 2, slice((b % 2) * 512, (b % 2 + 1) * 512)
                tt(V[:, t, cols], PS[b][:], gates[:, t, cols], ALU.mult).then_inc(signal, 1)

            def second_merge(m, gates, unit):
                def product(b):
                    t, cols = b // 2, slice((b % 2) * 512, (b % 2 + 1) * 512)
                    own.inc(tt(TB[:, b, :], PS[b][:], gates[:, t, D + cols.start:D + cols.stop], ALU.mult))

                def add(b):
                    t, cols = b // 2, slice((b % 2) * 512, (b % 2 + 1) * 512)
                    tt(V[:, t, cols], V[:, t, cols], TB[:, b, :], ALU.add).then_inc(merged, 1)
                dve.wait_ge(w_used, unit + 1)
                product(0)
                product(2)
                own.wait()
                add(0)
                add(2)
                product(1)
                product(3)
                own.wait()
                add(1)
                add(3)
            for n in range(8):
                split_lo(U_GATE + n + 3)
                dve.wait_ge(w_used, U_GATE + n + 1)
                cols = slice(n * 256, (n + 1) * 256)
                tt(BUF1[:, :, cols], PS[4 + n % 2][:].rearrange("p (t c) -> p t c", t=NT),
                   GAIN[:, cols].unsqueeze(1).to_broadcast([P, NT, 256]), ALU.add).then_inc(g_logit, 1)
                if n == 5:
                    dve.wait_ge(gates_ok, 4)
                    for b in range(4):
                        first_merge(BUF1, b, acc_read)
            products(8, U_DAW, 4, SUBLN)
            split_lo(U_DAW + 3 + 3)
            dve.wait_ge(acc_read, 4)
            dve.wait_ge(gates_ok, 8)
            second_merge(0, BUF1, U_DAW + 3)
            products(12, U_WOUT, 4)
            boundary(1, U_WOUT + 3, 4)
            ffn(1, U_FFN2, 0)
            boundary(2, U_FFN2 + 3 * FF_STEPS - 1, 5)

            for n in range(6):
                split_lo(U_IN2 + n + 3)

            def rope(x, cos, sin, heads, half, signal):
                x1, x2 = x[:, :, :, 0:half], x[:, :, :, half:2 * half]
                cb = cos.rearrange("p (t c) -> p t c", t=NT).unsqueeze(2).to_broadcast([P, NT, heads, half])
                sbc = sin.rearrange("p (t c) -> p t c", t=NT).unsqueeze(2).to_broadcast([P, NT, heads, half])
                n = NT * heads * half
                t = [XN[:].rearrange("p t c -> p (t c)")[:, k * n:(k + 1) * n]
                     .rearrange("p (t h c) -> p t h c", t=NT, h=heads) for k in range(3)]
                own.wait()
                own.inc(tt(t[0], x1, cb, ALU.mult))
                own.inc(tt(t[1], x2, sbc, ALU.mult))
                own.link(tt(t[2], x2, cb, ALU.mult))
                own.link(tt(x2, x1, sbc, ALU.mult))
                own.inc(tt(x1, t[0], t[1], ALU.subtract))
                tt(x2, x2, t[2], ALU.add).then_inc(signal, 1)
            dve.wait_ge(lat_rs, 1)
            for t in range(NT):
                own.inc(ts(PROJ[:, t, LAT0:LAT0 + Q_RANK], PROJ[:, t, LAT0:LAT0 + Q_RANK], RS[:, t:t + 1], None, ALU.mult))
                ts(PROJ[:, t, LAT0 + Q_RANK:KR0], PROJ[:, t, LAT0 + Q_RANK:KR0], RS[:, 2 + t:3 + t], None,
                   ALU.mult).then_inc(lat_ok, 1)
            dve.wait_ge(lat_ok, 2)
            rope(PROJ[:, :, 0:640].rearrange("p t (h c) -> p t h c", c=HD), tab("cos_a"), tab("sin_a"), 10, HD // 2,
                 swa_roped)
            dve.wait_ge(swa_roped, 1)
            split_lo(U_GATE2A + 3)
            for j in range(3):
                dve.wait_ge(lat_hi, 1 + (j == 2))
                if j == 0:
                    dve.wait_ge(lat_hi, 1)
                ins = stt(KTL[:, j * TOK:(j + 1) * TOK], PS[6 + j // 2][:, (j % 2) * TOK:(j % 2 + 1) * TOK],
                          COLS[:, GC["q_lat"] + j:GC["q_lat"] + j + 1], KTH[:, j * TOK:(j + 1) * TOK].bitcast(F32),
                          ALU.mult, ALU.subtract)
            ins.then_inc(lat_lo, 1)
            split_lo(U_GATE2A + 1 + 3)
            for n in range(2):
                split_lo(U_UQ + n + 3)
            dve.wait_ge(lat_hi, 3)
            for j in range(2):
                ins = stt(KTL[:, j * TOK:(j + 1) * TOK], PS[7][:, j * TOK:(j + 1) * TOK],
                          COLS[:, GC["kv_lat"] + j:GC["kv_lat"] + j + 1], KTH[:, j * TOK:(j + 1) * TOK].bitcast(F32),
                          ALU.mult, ALU.subtract)
            ins.then_inc(lat_lo, 1)
            dve.wait_ge(q_kept, 4)
            rope(QM[:, :, :, NOPE:MLA_QK], tab("cos_b"), tab("sin_b"), MLA_HEADS, ROPE // 2, mla_roped)
            dve.wait_ge(mla_roped, 1)
            rope(PROJ[:, :, KR0:PJ].unsqueeze(2), tab("cos_b"), tab("sin_b"), 1, ROPE // 2, mla_roped)
            dve.wait_ge(mla_roped, 2)
            own.inc(nc.vector.tensor_copy(KM[:, :, :, NOPE:MLA_QK],
                                          PROJ[:, :, KR0:PJ].unsqueeze(2).to_broadcast([P, NT, MLA_HEADS, ROPE])))
            split_lo(U_UKV + 3)
            dve.wait_ge(kv_kept, 4)
            nc.vector.tensor_copy(KM[:, :, :, 0:NOPE],
                                  V[:].rearrange("p t (h c) -> p t h c", h=MLA_HEADS)[:, :, :, 0:NOPE]).then_inc(kcat_ok, 1)
            nsinks = ROWS[:, ROW["dt_bias"]:ROW["dt_bias"] + 8]
            for r in range(9):
                if r < 8:
                    for a in range(2):
                        dve.wait_ge(sc2, 2 * r + a + 1)
                        if r and a == 0:
                            dve.wait_ge(o2_kept, r - 1) if r > 1 else None
                        if r:
                            dve.wait_ge(p2_turned, 2 * (r - 1) + a + 1)
                        own.link(tt(SC[a], PS[2 + a][:, 0:384], tab(("swa", "mla")[a]), ALU.add))
                        for i in range(NT):
                            own.inc(nc.vector.tensor_reduce(SM[:, 20 + 2 * a + i:21 + 2 * a + i],
                                                            SC[a][:, i * P:i * P + P * (i + 1)], AX.X, ALU.max))
                        own.wait()
                        if a == 0:
                            if r:
                                dve.wait_ge(p2_exp, 2 * r)
                            ts(SM[:, 0:2], SM[:, 20:22], -HD ** -0.5, nsinks[:, r:r + 1], ALU.mult,
                               ALU.min).then_inc(s2_ready, 1)
                        else:
                            ts(SM[:, 2:4], SM[:, 22:24], -MLA_QK ** -0.5, None, ALU.mult).then_inc(s2_ready, 1)
                if r:
                    dve.wait_ge(pv2, r)
                    dst = XN[:].rearrange("p i (a h c) -> p a i h c", a=2, h=8)[:, :, :, r - 1, :]
                    tt(dst, PS[6][:, 0:256].rearrange("p (a i c) -> p a i c", a=2, i=NT),
                       SM[:, 28 + 0:32].rearrange("p (a i) -> p a i", a=2).unsqueeze(3).to_broadcast([P, 2, NT, 64]),
                       ALU.mult).then_inc(o2_kept, 1)
                    dve.wait_ge(o2_kept, r)
                if r < 8:
                    dve.wait_ge(p2_exp, 2 * (r + 1))
                    own.link(tt(SM[:, 4:6], SM[:, 4:6], SM[:, 8:10], ALU.add))
                    own.link(nc.vector.reciprocal(SM[:, 28:32], SM[:, 4:8]))
                    if r < 6:
                        split_lo(U_GATE2B + r + 3)
            products(16, U_OSWA, 2)
            split_lo(U_OSWA + 1 + 3)
            dve.wait_ge(w_used, U_OSWA + 2)
            dve.wait_ge(gates2, 4)
            for b in range(4):
                first_merge(BUF2, b, acc_read)
            products(18, U_OMLA, 2)
            split_lo(U_OMLA + 1 + 3)
            dve.wait_ge(acc_read, 8)
            second_merge(1, BUF2, U_OMLA + 1)
            products(20, U_OUT2, 4)
            boundary(3, U_OUT2 + 3)
            ffn(2, U_FFN3, 1)
            boundary(4, U_END - 1)
            dve.wait_ge(gain_loaded, 96)
            for t in range(NT):
                dve.wait_ge(rstd_ok, NT * 5 + t + 1)
                stt(XN[:, t, :], H[:, t, :], RS[:, t:t + 1], GAIN[:, 0:D], ALU.mult, ALU.mult).then_inc(out_ok, 1)

        @block.tensor
        def _(pe):
            mm = nc.tensor.matmul

            def norm(n, c=0, bank=0):
                for t in range(NT):
                    pe.wait_ge(xn_ok, NT * n + t + 1)
                    for q in range(2):
                        if t:
                            pe.wait_ge(xt_lo, 4 * n + q + 1)
                        for k in range(4):
                            j = 4 * q + k
                            ins = nc.tensor.transpose(PS[6 + q][:, k * P:(k + 1) * P], XN[:, t, j * P:(j + 1) * P],
                                                      IDENT)
                        ins.then_inc(xn_turned, 1)
                    if c:
                        pe.wait_ge(xt_lo, 4 * n + 2 * t + 2)
                        for v in range(2):
                            tokens(c + v, bank + v, only=t)
                pe.wait_ge(xt_lo, 4 * n + 4)

            def parts(ps, stat_hi, stat_lo, mov_hi, mov_lo, first, last):
                mm(ps, stat_hi, mov_hi, start=first, stop=False)
                mm(ps, stat_hi, mov_lo, start=False, stop=False)
                return mm(ps, stat_lo, mov_hi, start=False, stop=last)

            def channels(c, bank, i=0):
                s = slot(c)
                pe.wait_ge(w_lo, c + RING * i + 1)
                for f in range(2):
                    for k in range(KD):
                        ws = slice(k * 256 + f * P, k * 256 + (f + 1) * P)
                        ins = parts(PS[bank][:, f * TOK:(f + 1) * TOK], WH[:, s, ws], WL[:, s, ws],
                                    XTH[:, k, :], XTL[:, k, :], k == 0, k == KD - 1)
                ins.then_inc(w_used, 1)

            def tokens(c, bank, wide=256, only=None):
                s = slot(c)
                pe.wait_ge(w_lo, c + 1)
                for t in range(NT) if only is None else (only,):
                    for k in range(KD):
                        ws = slice(k * wide, (k + 1) * wide)
                        xs = slice(t * P, (t + 1) * P)
                        ins = parts(PS[bank][:, t * 256:t * 256 + wide], XTH[:, k, xs], XTL[:, k, xs],
                                    WH[:, s, ws], WL[:, s, ws], k == 0, k == KD - 1)
                if only != 0:
                    ins.then_inc(w_used, 1)

            def rows(c, first, last, i=0, banks=0, half=0, by_tile=False):
                s = slot(c)
                pe.wait_ge(w_lo, c + RING * i + 1)
                order = [(k, t) for k in range(2) for t in range(NT)]
                if by_tile:
                    order.sort(key=lambda kt: kt[1])
                for k, t in order:
                    a = slice(half * 512 + k * TOK + t * P, half * 512 + k * TOK + (t + 1) * P)
                    for h in range(2):
                        ws = slice(k * D + h * 512, k * D + (h + 1) * 512)
                        ins = parts(PS[banks + 2 * t + h][:], KTH[:, a], KTL[:, a], WH[:, s, ws], WL[:, s, ws],
                                    first and k == 0, last and k == 1)
                    if by_tile and (k, t) == (1, 0):
                        ins.then_inc(acc_half, 1)
                ins.then_inc(w_used, 1)

            def ffn(f, u0):
                n0 = FF_STEPS * f
                channels(u0, 4)
                channels(u0 + 1, 5)

                def step(c, j, i=0, first=False):
                    pe.wait_ge(gate_ok, j + n0)
                    channels(c, 4, i)
                    pe.wait_ge(h_ready, j + n0)
                    channels(c + 1, 5, i)
                    pe.wait_ge(hT_lo, j + n0)
                    rows(c + 2, first, False, i)
                step(u0 + 2, 1, 0, True)
                with pe.Fori(2, FF_STEPS) as i:
                    step(u0 - 1, i, i)
                pe.wait_ge(hT_lo, n0 + FF_STEPS)
                rows(u0 + 3 * FF_STEPS - 1, False, True, by_tile=True)

            def turn_rows(n, src, k0):
                if n:
                    pe.wait_ge(k_lo, n)
                for k in range(2):
                    for t in range(NT):
                        ins = nc.tensor.transpose(PS[7][:, k * TOK + t * P:k * TOK + (t + 1) * P],
                                                  src[:, t, (k0 + k) * P:(k0 + k + 1) * P], IDENT)
                ins.then_inc(k_turned, 1)

            def products(n0, u0, n, src, k0=0, ready=None, by_tile=False):
                def turn(j):
                    if ready:
                        ready(j)
                    turn_rows(n0 + j, src, k0 + 2 * j)
                turn(0)
                for j in range(n):
                    if j + 1 < n:
                        turn(j + 1)
                    pe.wait_ge(k_lo, n0 + j + 1)
                    rows(u0 + j, j == 0, j == n - 1, half=(n0 + j) % 2, by_tile=by_tile and j == n - 1)

            pe.wait_ge(tab_loaded, 16)
            norm(0)
            ffn(0, U_FFN1)
            norm(1, U_XZ)

            def turn_x(n):
                pe.wait_ge(conv_silu, n + 1)
                if n >= 2:
                    pe.wait_ge(x_kept, n - 1)
                for f in range(2):
                    for t in range(NT):
                        ins = nc.tensor.transpose(PS[6 + n % 2][:, f * TOK + t * P:f * TOK + (t + 1) * P],
                                                  XSIL[:, f * TOK + t * P:f * TOK + (t + 1) * P], IDENT)
                ins.then_inc(x_turned, 1)
            for m, (kind, n) in enumerate(XZ):
                c = U_XZ + m
                if kind == "x":
                    if n >= 2:
                        pe.wait_ge(conv_done, n - 1)
                    elif n == 1:
                        pe.wait_ge(dt_raw, 1)
                    channels(c, 4 + n % 2)
                    if 1 <= n <= 8:
                        turn_x(n - 1)
                elif kind == "dt":
                    tokens(c, 5, SSD_HEADS)
                elif n >= 2:
                    pe.wait_ge(z_kept, n - 1)
                    tokens(c, n % 2)
                if (kind, n) == ("z", 3):
                    pe.wait_ge(a_ok, 1)
                    for k, tri in enumerate((UPTO, AFTER)):
                        for v in range(NT):
                            ins = mm(PS[3][:, k * 64 + v * 32:k * 64 + (v + 1) * 32], tri, DT[:, 3, v * 32:(v + 1) * 32],
                                     start=True, stop=True)
                    ins.then_inc(cums, 1)
                if (kind, n) == ("x", 11):
                    pe.wait_ge(conv_silu, 10)
                    pe.wait_ge(x_kept, 7)
                    for g in range(SSD_GROUPS):
                        ins = nc.tensor.transpose(PS[6][:, g * P:(g + 1) * P], BT[:, g, 0:P], IDENT)
                    ins.then_inc(x_turned, 1)
            pe.wait_ge(consts16, 1)
            pe.wait_ge(conv_silu, 12)
            pe.wait_ge(z_kept, 8)
            u = U_QKV
            for r in range(9):
                if r < 8:
                    g, c = divmod(r, 2)
                    if r:
                        pe.wait_ge(ssd_e, r)
                        pe.wait_ge(ssd_m, r)
                    mm(PS[2][:, 0:P], BT[:, g, c * P:(c + 1) * P], CT[:, g, c * P:(c + 1) * P], start=True,
                       stop=True).then_inc(ssd_cb, 1)
                    pe.wait_ge(ab_ok, r + 1)
                    for b in range(2):
                        mm(PS[b][:], ID16[:], MASK16[:].rearrange("p h l -> p (h l)"), start=True, stop=False)
                        for e in range(4):
                            ins = mm(PS[b][:, e * P:(e + 1) * P], AB[:, 4 * b + e, :], UPTO, start=False, stop=e == 3)
                    ins.then_inc(ssd_mm, 1)
                if r:
                    n = r - 1
                    g, c = divmod(n, 2)
                    if n:
                        pe.wait_ge(y_gated, n)
                    pe.wait_ge(cums_exp, 1)
                    pe.wait_ge(cums_neg, 1)
                    if c == 0:
                        pe.wait_ge(xdec_ok, n // 2 + 1)
                        mm(PS[6][:], B0[:, g * P:(g + 1) * P], XDEC, start=True, stop=True).then_inc(ssd_st, 1)
                    else:
                        pe.wait_ge(state_ok, n // 2 + 1)
                        mm(PS[6][:], CT[:, g, P:TOK], STATE, start=True, stop=True).then_inc(ssd_st, 1)
                    pe.wait_ge(ssd_m, r)
                    for e in range(HPG):
                        ins = mm(PS[3][:, e * SSD_P:(e + 1) * SSD_P], E[:, e, :], XDT[:, e * SSD_P:(e + 1) * SSD_P],
                                 start=True, stop=True)
                    ins.then_inc(ssd_y, 1)
                if r < 8:
                    for _u in range(1 + r % 2):
                        n = u - U_QKV
                        pe.wait_ge(conv_done, 12 - n) if n < 2 else pe.wait_ge(qkv_kept, n - 1)
                        (channels if n < 8 else tokens)(u, 5 - n % 2)
                        u += 1
            pe.wait_ge(ys_ok, 8)
            pe.wait_ge(qkv_kept, 12)
            for h in range(9):
                if h:
                    pe.wait_ge(attn_ok, h)
                    if h >= 2:
                        pe.wait_ge(o_kept, h - 1)
                    for b in range(3):
                        ins = nc.tensor.transpose(PS[6][:, b * P:(b + 1) * P], ATT[:, b * P:(b + 1) * P], IDENT)
                    ins.then_inc(p_turned, 1)
                if h < 8:
                    if h == 0:
                        turn_rows(0, BUF2, 0)
                    if h:
                        pe.wait_ge(s_ready, h)
                    for m in range(2):
                        ms = slice(m * 64, (m + 1) * 64)
                        mm(PS[4 + m][:, 0:P], QK[ms, h, 0, 0:P], QK[ms, h, 1, 0:P], start=True, stop=True)
                        ins = mm(PS[4 + m][:, P:3 * P], QK[ms, h, 0, P:TOK], QK[ms, h, 1, :], start=True, stop=True)
                    ins.then_inc(scores, 1)
                if h:
                    pe.wait_ge(p_kept, h)
                    vs = slice((h - 1) * P, h * P)
                    mm(PS[6][:, 0:P], PT[:, 0:P], V[:, 0, vs], start=True, stop=True)
                    mm(PS[6][:, P:2 * P], PT[:, P:2 * P], V[:, 0, vs], start=True, stop=False)
                    mm(PS[6][:, P:2 * P], PT[:, 2 * P:3 * P], V[:, 1, vs], start=False, stop=True).then_inc(pv, 1)
                if h < 8:
                    if h < 7:
                        turn_rows(h + 1, BUF2, 2 * (h + 1))
                    pe.wait_ge(k_lo, h + 1)
                    rows(U_SSDW + h, h == 0, h == 7, half=h % 2)
            for n in range(8):
                pe.wait_ge(s_ready, 8) if n < 2 else pe.wait_ge(g_logit, n - 1)
                tokens(U_GATE + n, 4 + n % 2)
            pe.wait_ge(o_ok, 1)
            pe.wait_ge(acc_read, 4)
            products(8, U_DAW, 4, XN)
            products(12, U_WOUT, 4, V, ready=lambda j: pe.wait_ge(merged, 2 + 2 * (j // 2)), by_tile=True)
            norm(2)
            ffn(1, U_FFN2)
            norm(3, U_IN2, 4)

            for n in range(2, 6):
                if n >= 4:
                    pe.wait_ge(proj_kept, n - 3)
                tokens(U_IN2 + n, (4, 5, 0, 1)[n % 4], 256 if n < 5 else PJ - 1280)
            pe.wait_ge(proj_kept, 5)
            tokens(U_GATE2A, 0)

            def turn_latent(bank, c0, tiles):
                for k in range(tiles):
                    for t in range(NT):
                        ins = nc.tensor.transpose(PS[bank][:, k * TOK + t * P:k * TOK + (t + 1) * P],
                                                  PROJ[:, t, c0 + k * P:c0 + (k + 1) * P], IDENT)
                ins.then_inc(lat_turned, 1)
            pe.wait_ge(lat_ok, 2)
            turn_latent(6, LAT0, 2)
            turn_latent(7, LAT0 + 2 * P, 1)
            pe.wait_ge(swa_roped, 1)
            for r in range(2):
                for k in range(2):
                    for t in range(NT):
                        ins = nc.tensor.transpose(PS[2 + r][:, k * TOK + t * P:k * TOK + (t + 1) * P],
                                                  PROJ[:, t, (2 * r + k) * P:(2 * r + k + 1) * P], IDENT)
                ins.then_inc(swa_turned, 1)
            pe.wait_ge(kdup_ok, 1)
            for k in range(SWA_KV):
                for t in range(NT):
                    ins = nc.tensor.transpose(PS[4][:, k * TOK + t * P:k * TOK + (t + 1) * P],
                                              KDUP[:, t, k, :, :].rearrange("p u c -> p (u c)"), IDENT)
            ins.then_inc(swa_turned, 1)
            pe.wait_ge(proj_kept, 6)
            tokens(U_GATE2A + 1, 1)
            pe.wait_ge(lat_lo, 1)
            pe.wait_ge(swa_kept, 3)
            for n in range(2):
                c = U_UQ + n
                pe.wait_ge(w_lo, c + 1)
                for t in range(NT):
                    for k in range(3):
                        a = slice(k * TOK + t * P, k * TOK + (t + 1) * P)
                        ws = slice(k * 384, (k + 1) * 384)
                        ins = parts(PS[2 + 2 * n + t][:, 0:384], KTH[:, a], KTL[:, a], WH[:, slot(c), ws],
                                    WL[:, slot(c), ws], k == 0, k == 2)
                ins.then_inc(w_used, 1)
            turn_latent(7, LAT0 + Q_RANK, 2)
            pe.wait_ge(lat_lo, 2)
            pe.wait_ge(q_kept, 4)
            rows(U_UKV, True, True, banks=2)
            pe.wait_ge(kcat_ok, 1)
            pe.wait_ge(kv_kept, 4)
            for r in range(9):
                if r < 8:
                    if r:
                        pe.wait_ge(mla_kept, r)
                    for a, src in enumerate((QM, KM)):
                        for t in range(NT):
                            ins = nc.tensor.transpose(PS[7][0:MLA_QK, a * TOK + t * P:a * TOK + (t + 1) * P],
                                                      src[:, t, r, :], IDENT)
                    ins.then_inc(mla_turned, 1)
                if r:
                    pe.wait_ge(p2_exp, 2 * r)
                    if r >= 2:
                        pe.wait_ge(p2_kept, 2 * (r - 1))
                    for a in range(2):
                        for b in range(3):
                            ins = nc.tensor.transpose(PS[4 + a][:, b * P:(b + 1) * P], SC[a][:, b * P:(b + 1) * P],
                                                      IDENT)
                        ins.then_inc(p2_turned, 1)

                def score(a, qt, kt, r):
                    if r:
                        pe.wait_ge(s2_ready, 2 * (r - 1) + a + 1)
                    mm(PS[2 + a][:, 0:P], qt[:, 0:P], kt[:, 0:P], start=True, stop=True)
                    mm(PS[2 + a][:, P:3 * P], qt[:, P:TOK], kt[:, :], start=True, stop=True).then_inc(sc2, 1)
                if r < 8:
                    ms = slice((r % 2) * 64, (r % 2 + 1) * 64)
                    score(0, SQT[ms, r // 2, :], SKT[ms, r // 4, :], r)
                if r:
                    h = r - 1
                    if r >= 2:
                        pe.wait_ge(o2_kept, r - 1)
                    for a in range(2):
                        pe.wait_ge(p2_kept, 2 * h + a + 1)
                        if a == 0:
                            v = PROJ[:, :, 640 + (h // 4) * HD:640 + (h // 4 + 1) * HD]
                        else:
                            v = V[:, :, h * P + NOPE:(h + 1) * P]
                        mm(PS[6][:, a * P:a * P + 64], PT2[a][:, 0:P], v[:, 0, :], start=True, stop=True)
                        mm(PS[6][:, a * P + 64:(a + 1) * P], PT2[a][:, P:2 * P], v[:, 0, :], start=True, stop=False)
                        ins = mm(PS[6][:, a * P + 64:(a + 1) * P], PT2[a][:, 2 * P:3 * P], v[:, 1, :], start=False,
                                 stop=True)
                    ins.then_inc(pv2, 1)
                if r < 8:
                    pe.wait_ge(mla_kept, r + 1)
                    score(1, QK[0:MLA_QK, r, 0, :], QK[0:MLA_QK, r, 1, :], r)
                    if r < 6:
                        pe.wait_ge(g2_kept, r + 1)
                        tokens(U_GATE2B + r, r % 2)
            pe.wait_ge(g2_kept, 8)
            pe.wait_ge(o2_kept, 8)
            products(16, U_OSWA, 2, XN)
            pe.wait_ge(acc_read, 8)
            products(18, U_OMLA, 2, XN, 4)
            products(20, U_OUT2, 4, V, ready=lambda j: pe.wait_ge(merged, 6 + 2 * (j // 2)), by_tile=True)
            norm(4)
            ffn(2, U_FFN3)


_SQUEEZED = ["ffn1_pre_g", "mix_pre_g", "ffn2_pre_g", "mix_norm_g_2", "ffn_norm_g_2",
             "ffn1_w_gate", "ffn1_w_up", "ffn1_w_down", "ffn1_post_g", "w_in", "gate_b", "ssd_norm_g", "ssd_w_branch",
             "da_w_branch", "w_out", "mix_post_g", "ffn2_w_gate", "ffn2_w_up", "ffn2_w_down", "ffn2_post_g",
             "w_in_2", "w_uq_2", "w_ukv_2", "w_o_swa_2", "w_o_mla_2", "w_out_2", "w_gate_2", "w_up_2", "w_down_2"]


def kernel(**inputs):
    import concourse.bacc as bacc
    from concourse.bass_utils import run_bass_kernel_spmd

    v = {k: np.asarray(a) for k, a in inputs.items()}

    def tiles(a):
        return a.reshape(-1, P).T
    cols = [tiles(v[k][0]) for k in ("q_norm_g_2", "kv_norm_g_2", "da_subln_g", "ssd_conv_b")]
    cols += [tiles(v["ssd_conv_w"][0][k]) for k in range(CONV_K)]
    rows = [v[k][0] for k in ("ssd_dt_bias", "ssd_A_log", "ssd_D", "swa_sinks_2")]
    lam = [v[f"da_lambda_{k}"][0] for k in ("q1", "k1", "q2", "k2")]
    host = {"x": v["x"], "cols": np.concatenate(cols, 1), "rows": np.concatenate(rows), "lam": np.concatenate(lam),
            "tables": TABLES,
            "final_norm_g_2": v["final_norm_g_2"]}
    host.update({k: v[k][0] for k in _SQUEEZED})
    nc = bacc.Bacc("TRN2", target_bir_lowering=False, num_devices=1)
    arrays, aps = {}, {}
    for name, a in host.items():
        a = np.ascontiguousarray(a)
        arrays[f"in_{name}"] = a
        aps[name] = nc.dram_tensor(f"in_{name}", a.shape, mybir.dt.from_np(a.dtype), kind="ExternalInput").ap()
    out = nc.dram_tensor("out_x", (1, TOK, D), F32, kind="ExternalOutput").ap()
    program(nc, aps, out)
    r = run_bass_kernel_spmd(nc, [arrays], core_ids=[0])
    return r.results[0]["out_x"]
```

```python
import math
from contextlib import ExitStack

import numpy as np
import concourse.bass as bass
from concourse import mybir

ALU = mybir.AluOpType
ACT = mybir.ActivationFunctionType
AX = mybir.AxisListType
F32 = mybir.dt.float32
F32R = mybir.dt.float32r
BF16 = mybir.dt.bfloat16

P = 128
D = 1024
KD = D // P
NT = 2
TOK = NT * P
D_FF = 2816
FF_STEPS = D_FF // 256
EPS = 1e-6
HIDE = -1e30
SSD_INNER, SSD_GROUPS, SSD_HEADS, SSD_P, SSD_N = 2048, 4, 32, 64, 128
HPG = SSD_HEADS // SSD_GROUPS
GW = HPG * SSD_P
CONV_K = 4
XBC_TILES = (SSD_INNER + 2 * SSD_GROUPS * SSD_N) // P
DA_HEADS = 8
LAM_INIT = 0.8 - 0.6 * math.exp(0.0)
SWA_HEADS, SWA_KV, HD = 8, 2, 64
MLA_HEADS, NOPE, ROPE, MLA_V = 8, 64, 32, 64
MLA_QK = NOPE + ROPE
Q_RANK, KV_RANK = 384, 256

RING = 3
UNIT = 2048
U_FFN1 = 0
U_XZ = U_FFN1 + 3 * FF_STEPS
XZ = [("z", 0), ("z", 1), ("dt", 0)] + [v for n in range(6) for v in (("x", 2 * n), ("x", 2 * n + 1), ("z", n + 2))]
U_QKV = U_XZ + len(XZ)
U_GATE0 = U_QKV + 12
U_SSDW = U_GATE0 + 1
U_GATE = U_SSDW + 8
U_DAW = U_GATE + 7
U_WOUT = U_DAW + 4
U_FFN2 = U_WOUT + 4
U_IN2 = U_FFN2 + 3 * FF_STEPS
IN2 = (3, 4, 5, 0, 1, 2)
U_GATE2A = U_IN2 + 6
U_UQ = U_GATE2A + 1
U_GATE2B = U_UQ + 2
U_UKV = U_GATE2B + 1
U_GATE2C = U_UKV + 1
U_OSWA = U_GATE2C + 6
U_OMLA = U_OSWA + 2
U_OUT2 = U_OMLA + 2
U_FFN3 = U_OUT2 + 4
U_END = U_FFN3 + 3 * FF_STEPS

C_XBC = SSD_INNER
C_DT = C_XBC + XBC_TILES * P
C_Q = C_DT + SSD_HEADS
C_GATE = C_Q + 3 * D
LAT0 = SWA_HEADS * HD + 2 * SWA_KV * HD
KR0 = LAT0 + Q_RANK + KV_RANK
PJ = KR0 + ROPE

GC = {}
_n = 0
for _name, _tiles in (("q_lat", 3), ("kv_lat", 2), ("subln", 1), ("conv_b", XBC_TILES), ("conv_w", CONV_K * XBC_TILES)):
    GC[_name] = _n
    _n += _tiles
N_COLS = _n
ROW = dict(dt_bias=0, a_log=32, skip=64, sinks=96)
N_ROWS = ROW["sinks"] + SWA_HEADS


def tables():
    r, c = np.arange(P)[:, None], np.arange(P)[None, :]
    hide = lambda keep: np.where(keep, 0.0, HIDE)
    causal = hide(r >= c)
    near = np.where(r >= c, r - c, -HIDE)
    cols = dict(
        ident=np.eye(P), upto=r <= c, after=r > c,
        swa=np.concatenate([causal, hide(c > r), causal], 1),
        mla=np.concatenate([causal, np.zeros((P, P)), causal], 1),
        dist=np.concatenate([near, P + r - c, near], 1),
        causal_t=hide(r <= c),
    )
    for name, dim in (("a", HD), ("b", ROPE)):
        inv = np.float32(10000.0) ** (-np.arange(0, dim, 2, dtype=np.float32) / np.float32(dim))
        ang = (np.arange(TOK, dtype=np.float32)[:, None] * inv[None, :].astype(np.float32)).astype(np.float32)
        for f, fn in (("cos", np.cos), ("sin", np.sin)):
            t = fn(ang.astype(np.float64)).astype(np.float32)
            cols[f"{f}_{name}"] = t.reshape(NT, P, dim // 2).transpose(1, 0, 2).reshape(P, -1)
    at, n = {}, 0
    for k, v in cols.items():
        at[k] = (n, n + v.shape[1])
        n += v.shape[1]
    return np.concatenate([np.asarray(v, np.float32) for v in cols.values()], 1), at, n


TABLES, T_AT, N_TABLES = tables()


class Steps:

    def __init__(self, eng, sem):
        self.eng, self.sem, self.n = eng, sem, 0

    def inc(self, ins):
        self.n += 1
        ins.then_inc(self.sem, 1)
        return self.n

    def wait(self):
        self.eng.wait_ge(self.sem, self.n)

    def link(self, ins):
        self.inc(ins)
        self.wait()


def program(nc, w, out):
    with ExitStack() as ctx:
        def sb(name, shape, dt=F32):
            return ctx.enter_context(nc.sbuf_tensor(name, shape, dt))

        def sem(name):
            return ctx.enter_context(nc.semaphore(name))

        RAW = sb("RAW", [P, RING, UNIT])
        WH = sb("WH", [P, RING, UNIT], F32R)
        WL = sb("WL", [P, RING, UNIT], F32R)
        H = sb("H", [P, NT, D])
        XN = sb("XN", [P, NT, D])
        XTH = sb("XTH", [P, KD, TOK], F32R)
        XTL = sb("XTL", [P, KD, TOK], F32R)
        KTH = sb("KTH", [P, 1024], F32R)
        KTL = sb("KTL", [P, 1024], F32R)
        BUF1 = sb("BUF1", [P, NT, 2048])
        BUF2 = sb("BUF2", [P, NT, 2048])
        QK = sb("QK", [P, 8, 2, TOK])
        V = sb("V", [P, NT, D])
        GAIN = sb("GAIN", [P, 2048])
        SCR = sb("SCR", [P, 5120])
        COLS = sb("COLS", [P, N_COLS])
        ROWS = sb("ROWS", [P, N_ROWS])
        TAB = sb("TAB", [P, N_TABLES])
        ID16 = sb("ID16", [P, P], BF16)
        MASK16 = sb("MASK16", [P, 4, P], BF16)
        SS = sb("SS", [P, 16])
        RS = sb("RS", [P, 16])
        DT = sb("DT", [P, 6, 64])
        EX = sb("EX", [P, 2, NT, SSD_HEADS])
        SM = sb("SM", [P, 40])
        PS = [ctx.enter_context(nc.psum_tensor(f"PS{i}", [P, 512], F32)) for i in range(8)]

        def tab(name):
            return TAB[:, T_AT[name][0]:T_AT[name][1]]

        SUBLN = COLS[:, GC["subln"]:GC["subln"] + 1]
        IDENT, UPTO, AFTER = tab("ident"), tab("upto"), tab("after")
        BT = XN[:, 0, :].rearrange("p (g t) -> p g t", g=SSD_GROUPS)
        CT = XN[:, 1, :].rearrange("p (g t) -> p g t", g=SSD_GROUPS)
        CONV = SCR[:, 0:512]
        XSIL = SCR[:, 512:1024]
        E = SCR[:, 0:1024].rearrange("p (h l) -> p h l", h=HPG)
        AB = SCR[:, 1024:2048].rearrange("p (h l) -> p h l", h=HPG)
        XDT, XDEC, STATE, Y, T1, B0 = (SCR[:, 2048 + 512 * n:2560 + 512 * n] for n in range(6))
        SG = SCR[:, 0:512]
        HS = SCR[:, 512:1024]
        TB = SCR[:, 1024:3072].rearrange("p (b c) -> p b c", b=4)
        SMAP = SCR[:, 0:768].rearrange("p (m k) -> p m k", m=2)
        ATT = SCR[:, 768:1152]
        PT = SCR[:, 1152:1536]
        SQJ = SCR[:, 1536:1792]
        PROJ = BUF1[:].rearrange("p t c -> p (t c)")[:, 0:NT * PJ].rearrange("p (t c) -> p t c", t=NT)
        QM = SCR[:, 0:1536].rearrange("p (t h c) -> p t h c", t=NT, h=MLA_HEADS)
        KM = SCR[:, 1536:3072].rearrange("p (t h c) -> p t h c", t=NT, h=MLA_HEADS)
        SC = [SCR[:, 3072:3456], SCR[:, 3456:3840]]
        PT2 = [SCR[:, 3840:4224], SCR[:, 4224:4608]]
        KDUP = SCR[:, 4608:5120].rearrange("p (t j u c) -> p t j u c", t=NT, j=SWA_KV, u=2)
        GPRE = SCR[:, 4096:5120]
        BC = XN[:].rearrange("p t c -> p (t c)")
        SQT = GAIN[:, 0:1024].rearrange("p (j t) -> p j t", j=4)
        SKT = GAIN[:, 1024:1536].rearrange("p (j t) -> p j t", j=2)

        raw = [sem(f"weights_loaded{i}") for i in range(RING)]
        w_hi, w_lo, w_used = sem("weights_hi"), sem("weights_lo"), sem("weights_used")
        x_loaded = [sem(f"x_loaded{t}") for t in range(NT)]
        loaded, tab_loaded, stored = sem("loaded"), sem("tables_loaded"), sem("stored")
        lam_loaded = sem("lam_loaded")
        gain_loaded, gpre_loaded, acc_half, y_gained = map(
            sem, ("gain_loaded", "pre_gain_loaded", "acc_half", "y_gained"))
        act_steps, dve_steps, pool_steps = sem("act_steps"), sem("dve_steps"), sem("pool_steps")
        rstd_ok, xn_ok, xn_turned, xt_hi, xt_lo = map(sem, ("rstd_ok", "xn_ok", "xn_turned", "xt_hi", "xt_lo"))
        ident_loaded = sem("ident_loaded")
        swa_half = sem("swa_branch_half")
        gate0_kept = sem("gate0_kept")
        branch_half = sem("branch_half")
        h0_turned = sem("first_hidden_turned")
        gate_ok, h_ready, hT_hi, hT_lo = map(sem, ("gate_ok", "hidden_ready", "hidden_hi", "hidden_lo"))
        y_sq, y_ss, y_rs, h_done = map(sem, ("y_squares", "y_sums", "y_rstd", "h_done"))
        out_ok = sem("out_ok")
        conv_1, conv_done, conv_silu, x_turned, x_kept = map(
            sem, ("conv_first_tap", "conv_done", "conv_silu", "x_turned", "x_kept"))
        consts16, dt_raw, z_kept, qkv_kept = map(sem, ("consts16", "dt_raw", "z_kept", "qkv_kept"))
        dt_abs, dt_exp, a_ok, cums, cums_exp, cums_neg = map(
            sem, ("dt_abs", "dt_exp", "a_ok", "cums", "cums_exp", "cums_neg"))
        ab_ok, ssd_mm, ssd_cb, ssd_e, ssd_m, xdec_ok, ssd_y, ssd_st = map(
            sem, ("a_spread", "ssd_sums", "ssd_cb", "ssd_decay", "ssd_mix", "ssd_xdec", "ssd_y", "ssd_state"))
        state_ok, skip_ok, y_read, y_gated, y_rms, ys_ok = map(
            sem, ("state_ok", "skip_ok", "y_read", "y_gated", "y_rms", "ys_ok"))
        k_turned, k_hi, k_lo = map(sem, ("k_turned", "k_hi", "k_lo"))
        lam_dot, lam_exp, lam_ok = map(sem, ("lam_dot", "lam_exp", "lam_ok"))
        scores, s_ready, p_exp, attn_ok, p_turned, p_kept, pv, o_kept, o_sq, o_rs, o_ok = map(
            sem, ("scores", "scores_masked", "probs", "attn_ok", "probs_turned", "probs_kept", "pv", "o_kept",
                  "o_squares", "o_rstd", "o_ok"))
        g_logit, gates_ok, merged, acc_read = map(sem, ("gate_logits", "gates_ok", "merged", "acc_read"))
        proj_kept, lat_rs, lat_ok, lat_turned, lat_hi, lat_lo, q_kept, kv_kept = map(
            sem, ("proj_kept", "lat_rstd", "lat_ok", "lat_turned", "lat_hi", "lat_lo", "q_kept", "kv_kept"))
        swa_roped, kdup_ok, swa_turned, swa_kept, mla_roped, kcat_ok, g2_kept, mla_turned, mla_kept = map(
            sem, ("swa_roped", "kdup_ok", "swa_turned", "swa_kept", "mla_roped", "kcat_ok", "gate2_kept",
                  "mla_turned", "mla_kept"))
        sc2, s2_ready, p2_exp, p2_turned, p2_kept, pv2, o2_kept, gates2 = map(
            sem, ("scores2", "scores2_masked", "probs2", "probs2_turned", "probs2_kept", "pv2", "o2_kept", "gates2"))

        post_no = {0: 0, 1: 1, 2: 2}

        def half_of(n):
            return slice((n % 2) * 512, (n % 2 + 1) * 512)

        def beside(r):
            return 2 if r in (2, 4) else 1

        def g2_unit(n):
            return (U_GATE2A, U_GATE2B)[n] if n < 2 else U_GATE2C + n - 2

        def gate_unit(n):
            return U_GATE + n - 1 if n else U_GATE0

        def slot(c):
            return c % RING

        block = ctx.enter_context(nc.Block())

        @block.sync
        def _(sp):
            def load(c, src, wide, i=0):
                s = slot(c)
                rows = src.shape[0] // P
                if c >= RING or not isinstance(i, int):
                    sp.wait_ge(w_lo, c + RING * i - RING + 1)
                sp.dma_start(RAW[:, s, 0:rows * wide].rearrange("p (k c) -> p k c", c=wide),
                             src.rearrange("(k p) c -> p k c", p=P)).then_inc(raw[s], 16)

            def ffn_loads(u0, gate, up, down):
                def g(c, j, i=0):
                    load(c, gate[:, bass.ds(j * 256, 256)], 256, i)

                def u(c, j, i=0):
                    load(c, up[:, bass.ds(j * 256, 256)], 256, i)

                def d(c, j, i=0):
                    load(c, down[bass.ds(j * 256, 256), :], D, i)
                g(u0, 0)
                if u0 == U_FFN1:
                    sp.dma_start(H[:, 1, :], x_in[:, 1, :]).then_inc(x_loaded[1], 16)
                u(u0 + 1, 0)
                if u0 == U_FFN1:
                    sp.dma_start(TAB[:, P:], w["tables"][:, P:]).then_inc(tab_loaded, 16)
                    sp.dma_start(COLS[:], w["cols"]).then_inc(loaded, 16)
                    sp.dma_start(ROWS[:], w["rows"].partition_broadcast(P)).then_inc(loaded, 16)
                with sp.Fori(1, FF_STEPS) as i:
                    g(u0 - 1, i, i)
                    u(u0, i, i)
                    d(u0 + 1, i - 1, i)
                d(u0 + 3 * FF_STEPS - 1, FF_STEPS - 1)

            def cols_units(u0, src, c0, n, wide=256):
                for j in range(n):
                    load(u0 + j, src[:, c0 + wide * j:c0 + wide * (j + 1)], wide)

            def rows_units(u0, src, n):
                for j in range(n):
                    load(u0 + j, src[256 * j:256 * (j + 1), :], D)

            x_in, x_out = (a.rearrange("o (t p) d -> p (o t) d", p=P) for a in (w["x"], out))
            sp.dma_start(H[:, 0, :], x_in[:, 0, :]).then_inc(x_loaded[0], 16)
            sp.dma_start(IDENT, w["tables"][:, 0:P]).then_inc(ident_loaded, 16)
            ffn_loads(U_FFN1, w["ffn1_w_gate"], w["ffn1_w_up"], w["ffn1_w_down"])
            for m, (kind, n) in enumerate(XZ):
                c0 = {"z": 256 * n, "dt": C_DT, "x": C_XBC + 256 * n}[kind]
                wide = SSD_HEADS if kind == "dt" else 256
                load(U_XZ + m, w["w_in"][:, c0:c0 + wide], wide)
            cols_units(U_QKV, w["w_in"], C_Q, 12)
            cols_units(U_GATE0, w["w_in"], C_GATE, 1)
            rows_units(U_SSDW, w["ssd_w_branch"], 8)
            cols_units(U_GATE, w["w_in"], C_GATE + 256, 7)
            rows_units(U_DAW, w["da_w_branch"], 4)
            rows_units(U_WOUT, w["w_out"], 4)
            ffn_loads(U_FFN2, w["ffn2_w_gate"], w["ffn2_w_up"], w["ffn2_w_down"])
            for q, n in enumerate(IN2):
                wide = min(256, PJ - 256 * n)
                load(U_IN2 + q, w["w_in_2"][:, 256 * n:256 * n + wide], wide)
            cols_units(U_GATE2A, w["w_in_2"], PJ, 1)
            cols_units(U_UQ, w["w_uq_2"], 0, 2, 384)
            cols_units(U_GATE2B, w["w_in_2"], PJ + 256, 1)
            load(U_UKV, w["w_ukv_2"], D)
            cols_units(U_GATE2C, w["w_in_2"], PJ + 512, 6)
            rows_units(U_OSWA, w["w_o_swa_2"], 2)
            rows_units(U_OMLA, w["w_o_mla_2"], 2)
            rows_units(U_OUT2, w["w_out_2"], 4)
            ffn_loads(U_FFN3, w["w_gate_2"], w["w_up_2"], w["w_down_2"])
            for t in range(NT):
                sp.wait_ge(out_ok, t + 1)
                sp.dma_start(x_out[:, t, :], XN[:, t, :]).then_inc(stored, 16)
            sp.wait_ge(stored, 16 * NT)

        @block.scalar
        def _(act):
            own = Steps(act, act_steps)

            def split_hi(c, i=0):
                if isinstance(i, int) and c >= U_END:
                    return
                s = slot(c)
                act.wait_ge(raw[s], 16 * (c // RING + i + 1))
                if c >= RING or not isinstance(i, int):
                    act.wait_ge(w_used, c + RING * i - RING + 1)
                nc.scalar.activation(WH[:, s, :], RAW[:, s, :], ACT.Copy).then_inc(w_hi, 1)

            def rsqrt(dst, src, n, signal, eps_scale=1.0 / D):
                own.wait()
                own.link(nc.scalar.activation(dst, src, ACT.Ln, scale=eps_scale, bias=EPS))
                nc.scalar.activation(dst, dst, ACT.Exp, scale=-0.5).then_inc(signal, 1)
                act.wait_ge(signal, n)

            def ln_exp():
                nc.scalar.preload_act_table_set("natural_log_exp_and_others")

            def h_rstd(n, t):
                if n:
                    act.wait_ge(h_done, NT * (n - 1) + t + 1)
                else:
                    act.wait_ge(x_loaded[t], 16)
                own.wait() if own.n else None
                own.link(nc.scalar.activation(XN[:, t, :], H[:, t, :], ACT.Square, accum_out=SS[:, t:t + 1]))
                own.link(nc.scalar.activation(RS[:, t:t + 1], SS[:, t:t + 1], ACT.Ln, scale=1.0 / D, bias=EPS))
                nc.scalar.activation(RS[:, t:t + 1], RS[:, t:t + 1], ACT.Exp, scale=-0.5).then_inc(rstd_ok, 1)

            def xn_hi(n, t):
                for q in range(2):
                    act.wait_ge(xn_turned, 4 * n + 2 * t + q + 1)
                    nc.scalar.activation(XTH[:, 4 * q:4 * q + 4, t * P:(t + 1) * P],
                                         PS[6 + q][:].rearrange("p (k c) -> p k c", k=4), ACT.Copy).then_inc(xt_hi, 1)

            def ffn(f, u0):
                n0 = FF_STEPS * f

                def g_part(c, j, i=0):
                    split_hi(c + 3, i)
                    act.wait_ge(w_used, c + 3 * i + 1)
                    if not isinstance(j, int) or j:
                        act.wait_ge(h_ready, j + n0)
                    nc.scalar.activation(SG, PS[4][:], ACT.Silu).then_inc(gate_ok, 1)

                def hidden_hi(j, src=HS, half=0):
                    nc.scalar.activation(KTH[:, half_of(half)], src, ACT.Copy).then_inc(hT_hi, 1)
                g_part(u0, 0)
                split_hi(u0 + 4)
                act.wait_ge(h0_turned, f + 1)
                hidden_hi(0, PS[7][:])

                def step(c, j, i=0):
                    g_part(c, j, i)
                    split_hi(c + 4, i)
                    split_hi(c + 5, i)
                    act.wait_ge(w_used, c + 3 * i + 3)
                    act.wait_ge(h_ready, j + n0 + 1)
                    hidden_hi(j)
                with act.Fori(1, FF_STEPS - 1) as i:
                    step(u0 - 1, i, i)
                c, j = u0 + 3 * FF_STEPS - 4, FF_STEPS - 1
                g_part(c, j)
                split_hi(c + 4)
                act.wait_ge(h_ready, j + n0 + 1)
                hidden_hi(j, HS, 1)
                split_hi(c + 5)

            def y_square(m, unit, b):
                act.wait_ge(acc_half, m + 1) if b < 2 else act.wait_ge(w_used, unit + 1)
                if b % 2:
                    act.wait_ge(y_gained, 4 * post_no[m] + b)
                own.wait()
                nc.scalar.activation(XN[:, b // 2, (b % 2) * 512:(b % 2 + 1) * 512], PS[b][:], ACT.Square,
                                     accum_out=SS[:, 8 + b:9 + b]).then_inc(y_sq, 1)

            def y_rstd(m, t, half):
                act.wait_ge(y_ss, NT * post_no[m] + t + 1)
                own.link(nc.scalar.activation(RS[:, 8 + t:9 + t], RS[:, 8 + t:9 + t], ACT.Ln, scale=1.0 / D, bias=EPS))
                nc.scalar.activation(RS[:, 8 + t:9 + t], RS[:, 8 + t:9 + t], ACT.Exp, scale=-0.5,
                                     bias=math.log(0.5) if half else 0.0).then_inc(y_rs, 1)

            def boundary(m, unit, half, next_table=None):
                if m in (0, 2, 4):
                    ln_exp()
                if m in post_no:
                    y_square(m, unit, 0)
                    y_square(m, unit, 1)
                    y_rstd(m, 0, half)
                    y_square(m, unit, 2)
                    h_rstd(m + 1, 0)
                    y_square(m, unit, 3)
                    y_rstd(m, 1, half)
                else:
                    h_rstd(m + 1, 0)
                if m == 4:
                    h_rstd(m + 1, 1)
                    return
                xn_hi(m + 1, 0)
                h_rstd(m + 1, 1)
                if next_table:
                    nc.scalar.preload_act_table(next_table)
                xn_hi(m + 1, 1)
                split_hi(unit + 3)

            def kt_hi(n, prev_unit, scale=1.0):
                act.wait_ge(k_turned, n + 1)
                act.wait_ge(w_used, prev_unit)
                nc.scalar.activation(KTH[:, half_of(n)], PS[7][:], ACT.Copy, scale=scale).then_inc(k_hi, 1)

            def products(n0, u0, n, scale=1.0, turned=False):
                for j in range(n):
                    if j or not turned:
                        kt_hi(n0 + j, u0 + j - 1, scale)
                    if n0 + j in (12, 20):
                        ln_exp()
                    if j:
                        split_hi(u0 + j - 1 + 3)

            ln_exp()
            h_rstd(0, 0)
            xn_hi(0, 0)
            split_hi(0)
            h_rstd(0, 1)
            split_hi(1)
            nc.scalar.preload_act_table(ACT.Silu)
            xn_hi(0, 1)
            split_hi(2)
            ffn(0, U_FFN1)
            boundary(0, U_FFN1 + 3 * FF_STEPS - 1, True)

            def z_silu(n):
                nc.scalar.activation(BUF2[:, :, n * 256:(n + 1) * 256],
                                     PS[n % 2][:].rearrange("p (t c) -> p t c", t=NT), ACT.Silu).then_inc(z_kept, 1)

            for m, (kind, n) in enumerate(XZ):
                c = U_XZ + m
                if kind == "x":
                    act.wait_ge(w_used, c + 1)
                    if n:
                        act.wait_ge(conv_silu, n)
                    for f in range(2):
                        j = 2 * n + f
                        tap = GC["conv_w"] + 3 * XBC_TILES + j
                        ins = nc.scalar.activation(CONV[:, f * TOK:(f + 1) * TOK],
                                                   PS[4 + n % 2][:, f * TOK:(f + 1) * TOK], ACT.Identity,
                                                   scale=COLS[:, tap:tap + 1],
                                                   bias=COLS[:, GC["conv_b"] + j:GC["conv_b"] + j + 1])
                    ins.then_inc(conv_1, 1)
                    split_hi(c + 3)
                    act.wait_ge(conv_done, n + 1)
                    if n < 8:
                        if n:
                            act.wait_ge(x_turned, n)
                        nc.scalar.activation(XSIL, CONV, ACT.Silu).then_inc(conv_silu, 1)
                    else:
                        nc.scalar.activation(BC[:, (n - 8) * 512:(n - 7) * 512], CONV, ACT.Silu).then_inc(conv_silu, 1)
                elif kind == "z":
                    split_hi(c + 3)
                    if n >= 2:
                        act.wait_ge(w_used, c + 1)
                        z_silu(n)
                else:
                    split_hi(c + 3)
                    own.inc(nc.scalar.activation(DT[:, 5, 0:32], ROWS[:, ROW["a_log"]:ROW["a_log"] + 32], ACT.Exp))
                    act.wait_ge(dt_abs, 1)
                    own.wait()
                    nc.scalar.activation(DT[:, 1, :], DT[:, 1, :], ACT.Exp).then_inc(dt_exp, 1)
                    act.wait_ge(lam_dot, 1)
                    nc.scalar.activation(SM[:, 36:38], SM[:, 36:38], ACT.Exp).then_inc(lam_exp, 1)
                    nc.scalar.preload_act_table(ACT.Silu)
                    z_silu(0)
                    z_silu(1)
            ln_exp()
            act.wait_ge(cums_neg, 1)
            nc.scalar.activation(EX[:].rearrange("p a t h -> p (a t h)"), PS[3][:, 0:128], ACT.Exp).then_inc(cums_exp, 1)

            def qkv(u):
                n = u - U_QKV
                split_hi(u + 3)
                act.wait_ge(w_used, u + 1)
                src = PS[5 - n % 2][:].rearrange("p (f t) -> p f t", f=2)
                if n < 8:
                    dst = QK[:, 2 * (n % 4):2 * (n % 4) + 2, n // 4, :]
                else:
                    dst = V[:, :, (n - 8) * 256:(n - 7) * 256]
                nc.scalar.activation(dst, src, ACT.Copy).then_inc(qkv_kept, 1)

            qkv(U_QKV)
            u = U_QKV + 1
            for r in range(9):
                if r < 8:
                    g, c = divmod(r, 2)
                    act.wait_ge(ssd_mm, r + 1)
                    if r:
                        act.wait_ge(ssd_y, r)
                    else:
                        act.wait_ge(x_kept, 9)
                    for e in range(HPG):
                        ins = nc.scalar.activation(E[:, e, :], PS[e // 4][:, (e % 4) * P:(e % 4 + 1) * P], ACT.Exp,
                                                   bias=DT[:, 4, c * 32 + g * HPG + e:c * 32 + g * HPG + e + 1])
                    ins.then_inc(ssd_e, 1)
                if r:
                    n = r - 1
                    if n % 2 == 0:
                        act.wait_ge(ssd_st, n + 1)
                        nc.scalar.activation(STATE, PS[6][:], ACT.Copy).then_inc(state_ok, 1)
                    act.wait_ge(y_gated, n + 1)
                    act.wait_ge(ssd_m, min(r + 1, 8)) if r < 8 else None
                    own.inc(nc.scalar.activation(T1, Y, ACT.Square, accum_out=SS[:, 4:5]))
                    rsqrt(RS[:, 4:5], SS[:, 4:5], n + 1, y_rms, 1.0 / GW)
                for _u in range(beside(r)):
                    qkv(u)
                    u += 1
            act.wait_ge(w_used, U_GATE0 + 1)
            nc.scalar.activation(BUF1[:, :, 0:256], PS[2][:].rearrange("p (t c) -> p t c", t=NT),
                                 ACT.Copy).then_inc(gate0_kept, 1)

            for h in range(9):
                if h:
                    act.wait_ge(p_turned, h)
                    nc.scalar.activation(PT, PS[6][:, 0:384], ACT.Copy).then_inc(p_kept, 1)
                if h < 8:
                    kt_hi(h, U_SSDW + h - 1)
                    split_hi(U_SSDW + h - 1 + 3)
                    act.wait_ge(s_ready, h + 1)
                    for m in range(2):
                        for i, ks in enumerate((slice(0, P), slice(P, 3 * P))):
                            n = 2 * i + m
                            ins = nc.scalar.activation(SMAP[:, m, ks], SMAP[:, m, ks], ACT.Exp, scale=0.125,
                                                       bias=SM[:, 4 + n:5 + n], accum_out=SM[:, 8 + n:9 + n])
                            if i == 0:
                                own.inc(ins)
                        ins.then_inc(p_exp, 1)
                if h:
                    act.wait_ge(o_kept, h)
                    for i in range(NT):
                        own.wait()
                        own.inc(nc.scalar.activation(SQJ[:, i * P:(i + 1) * P], XN[:, i, (h - 1) * P:h * P], ACT.Square,
                                                     accum_out=SS[:, i * 8 + h - 1:i * 8 + h]))
            split_hi(U_SSDW + 7 + 3)
            rsqrt(RS[:], SS[:], 1, o_rs, 1.0 / P)

            nc.scalar.preload_act_table(ACT.Sigmoid)
            for n in range(8):
                if n == 7:
                    kt_hi(8, U_DAW - 1, SUBLN)
                if n:
                    split_hi(gate_unit(n) + 3)
                act.wait_ge(g_logit, n + 1)
                s = BUF1[:, :, n * 256:(n + 1) * 256]
                nc.scalar.activation(s, s, ACT.Sigmoid).then_inc(gates_ok, 1)
            products(8, U_DAW, 4, SUBLN, True)
            split_hi(U_DAW + 3 + 3)
            products(12, U_WOUT, 4)
            boundary(1, U_WOUT + 3, False, ACT.Silu)
            ffn(1, U_FFN2)
            boundary(2, U_FFN2 + 3 * FF_STEPS - 1, True)

            for q, n in enumerate(IN2):
                wide = min(256, PJ - 256 * n)
                split_hi(U_IN2 + q + 3)
                act.wait_ge(w_used, U_IN2 + q + 1)
                nc.scalar.activation(PROJ[:, :, n * 256:n * 256 + wide],
                                     PS[(4, 5, 0, 1)[q % 4]][:].rearrange("p (t c) -> p t c", t=NT)[:, :, 0:wide],
                                     ACT.Copy).then_inc(proj_kept, 1)
                if q == 2:
                    own.wait()
                    act.wait_ge(proj_kept, 3)
                    for t in range(NT):
                        own.inc(nc.scalar.activation(XN[:, t, 0:Q_RANK], PROJ[:, t, LAT0:LAT0 + Q_RANK], ACT.Square,
                                                     scale=Q_RANK ** -0.5, accum_out=SS[:, t:t + 1]))
                        own.inc(nc.scalar.activation(XN[:, t, Q_RANK:Q_RANK + KV_RANK],
                                                     PROJ[:, t, LAT0 + Q_RANK:KR0], ACT.Square,
                                                     scale=KV_RANK ** -0.5, accum_out=SS[:, 2 + t:3 + t]))
                    rsqrt(RS[:, 0:4], SS[:, 0:4], 1, lat_rs, 1.0)

            def g2(n):
                split_hi(g2_unit(n) + 3)
                act.wait_ge(w_used, g2_unit(n) + 1)
                nc.scalar.activation(BUF2[:, :, n * 256:(n + 1) * 256],
                                     PS[n % 2][:].rearrange("p (t c) -> p t c", t=NT), ACT.Copy).then_inc(g2_kept, 1)
            for j in range(3):
                act.wait_ge(lat_turned, 1 + j // 2)
                ins = nc.scalar.activation(KTH[:, j * TOK:(j + 1) * TOK],
                                           PS[6 + j // 2][:, (j % 2) * TOK:(j % 2 + 1) * TOK], ACT.Copy,
                                           scale=COLS[:, GC["q_lat"] + j:GC["q_lat"] + j + 1])
                if j:
                    ins.then_inc(lat_hi, 1)
            g2(0)

            def swa_keep(r):
                act.wait_ge(swa_turned, r + 1)
                dst = GAIN[:, r * 512:(r + 1) * 512]
                nc.scalar.activation(dst, PS[(6, 0, 6)[r]][:], ACT.Copy).then_inc(swa_kept, 1)
            for n in range(2):
                split_hi(U_UQ + n + 3)
                act.wait_ge(w_used, U_UQ + n + 1)
                for t in range(NT):
                    ins = nc.scalar.activation(QM[:, t, 4 * n:4 * n + 4, :].rearrange("p h c -> p (h c)"),
                                               PS[4 - 2 * n + t][:, 0:384], ACT.Copy)
                    ins.then_inc(q_kept, 1)
            act.wait_ge(lat_turned, 3)
            for j in range(2):
                ins = nc.scalar.activation(KTH[:, j * TOK:(j + 1) * TOK], PS[7][:, j * TOK:(j + 1) * TOK], ACT.Copy,
                                           scale=COLS[:, GC["kv_lat"] + j:GC["kv_lat"] + j + 1])
            ins.then_inc(lat_hi, 1)
            swa_keep(0)
            g2(1)
            swa_keep(1)
            swa_keep(2)
            split_hi(U_UKV + 3)
            act.wait_ge(w_used, U_UKV + 1)
            for b in range(4):
                nc.scalar.activation(V[:, b // 2, (b % 2) * 512:(b % 2 + 1) * 512], PS[2 + b][:],
                                     ACT.Copy).then_inc(kv_kept, 1)

            for r in range(9):
                if r == 8:
                    kt_hi(16, U_OSWA - 1)
                if r < 8:
                    act.wait_ge(mla_turned, r + 1)
                    nc.scalar.activation(QK[0:MLA_QK, r, :, :], PS[7][0:MLA_QK, :].rearrange("p (a t) -> p a t", a=2),
                                         ACT.Copy).then_inc(mla_kept, 1)
                if r:
                    for a in range(2):
                        act.wait_ge(p2_turned, 2 * (r - 1) + a + 1)
                        nc.scalar.activation(PT2[a], PS[4 + a][:, 0:384], ACT.Copy).then_inc(p2_kept, 1)
                if r < 6:
                    g2(2 + r)
                if r < 8:
                    for a in range(2):
                        act.wait_ge(s2_ready, 2 * r + a + 1)
                        scale = (HD ** -0.5, MLA_QK ** -0.5)[a]
                        for i in range(NT):
                            p = SC[a][:, i * P:i * P + P * (i + 1)]
                            ins = nc.scalar.activation(p, p, ACT.Exp, scale=scale, bias=SM[:, 2 * a + i:2 * a + i + 1],
                                                       accum_out=SM[:, 4 + 2 * a + i:5 + 2 * a + i])
                            if a == 0 or i == 0:
                                own.inc(ins)
                        if a == 0:
                            ins = nc.scalar.activation(SM[:, 8:10], SM[:, 0:2], ACT.Exp,
                                                       bias=ROWS[:, ROW["sinks"] + r:ROW["sinks"] + r + 1])
                        ins.then_inc(p2_exp, 1)

            def sigmoids(half):
                for t in range(NT):
                    s = BUF2[:, t, half * D:(half + 1) * D]
                    nc.scalar.activation(s, s, ACT.Sigmoid).then_inc(gates2, 1)
            kt_hi(17, U_OSWA)
            nc.scalar.preload_act_table(ACT.Sigmoid)
            act.wait_ge(g2_kept, 8)
            sigmoids(0)
            split_hi(U_OSWA + 3)
            kt_hi(18, U_OSWA + 1)
            sigmoids(1)
            split_hi(U_OSWA + 1 + 3)
            kt_hi(19, U_OMLA)
            split_hi(U_OMLA + 3)
            split_hi(U_OMLA + 1 + 3)
            products(20, U_OUT2, 4)
            boundary(3, U_OUT2 + 3, False, ACT.Silu)
            ffn(2, U_FFN3)
            boundary(4, U_END - 1, False)

        @block.gpsimd
        def _(pool):

            def gain(name, n=1):
                pool.dma_start(GAIN[:, 0:n * D], w[name].partition_broadcast(P)).then_inc(gain_loaded, 16)

            def pre_gain(name):
                pool.dma_start(GPRE, w[name].partition_broadcast(P)).then_inc(gpre_loaded, 16)

            pre_gain("ffn1_pre_g")
            def split_lo(c):
                s = slot(c)
                pool.wait_ge(w_hi, c + 1)
                pool.wait_ge(w_lo, c)
                nc.gpsimd.tensor_tensor(WL[:, s, :], RAW[:, s, :], WH[:, s, :].bitcast(F32),
                                        ALU.subtract).then_inc(w_lo, 1)

            gain("ffn1_post_g")
            pool.wait_ge(xn_ok, 4)
            pre_gain("mix_pre_g")
            split_lo(U_XZ + 1)
            pool.wait_ge(h_done, NT)
            gain("ssd_norm_g", 2)
            pool.dma_start(XDT[:, 0:256], w["lam"].partition_broadcast(P)).then_inc(lam_loaded, 16)
            pool.wait_ge(loaded, 32)
            pool.wait_ge(a_ok, 1)

            def spread_a(r):
                g, c = divmod(r, 2)
                if r:
                    pool.wait_ge(ssd_mm, r)
                a = DT[:, 3, c * 32 + g * HPG:c * 32 + (g + 1) * HPG]
                nc.gpsimd.tensor_copy(AB, a.unsqueeze(2).to_broadcast([P, HPG, P])).then_inc(ab_ok, 1)

            for r in range(8):
                g, c = divmod(r, 2)
                if r == 0:
                    spread_a(0)
                if r < 7:
                    spread_a(r + 1)
                if r:
                    pool.wait_ge(ys_ok, r)
                skip = ROWS[:, ROW["skip"] + g * HPG:ROW["skip"] + (g + 1) * HPG]
                nc.gpsimd.tensor_tensor(Y.rearrange("p (h c) -> p h c", h=HPG),
                                        BUF1[:, c, g * GW:(g + 1) * GW].rearrange("p (h c) -> p h c", h=HPG),
                                        skip.unsqueeze(2).to_broadcast([P, HPG, SSD_P]), ALU.mult).then_inc(skip_ok, 1)
            pool.wait_ge(ys_ok, 8)
            gain("gate_b", 2)
            pre_gain("ffn2_pre_g")
            pool.wait_ge(g_logit, 8)
            gain("mix_post_g")
            split_lo(U_FFN2 + 1)
            pool.wait_ge(h_done, 2 * NT)
            gain("ffn2_post_g")
            pool.wait_ge(xn_ok, 12)
            pre_gain("mix_norm_g_2")
            split_lo(U_IN2 + 1)
            pool.wait_ge(swa_roped, 1)
            for t in range(NT):
                ins = nc.gpsimd.tensor_copy(
                    KDUP[:, t], PROJ[:, t, 512:640].rearrange("p (j c) -> p j c", j=SWA_KV).unsqueeze(2)
                    .to_broadcast([P, SWA_KV, 2, HD]))
            ins.then_inc(kdup_ok, 1)
            pool.wait_ge(sc2, 2 * SWA_HEADS)
            gain("final_norm_g_2")
            pool.wait_ge(pv2, SWA_HEADS)
            pre_gain("ffn_norm_g_2")
            split_lo(U_FFN3 + 1)

        @block.vector
        def _(dve):
            own = Steps(dve, dve_steps)
            tt, ts, stt = nc.vector.tensor_tensor, nc.vector.tensor_scalar, nc.vector.scalar_tensor_tensor

            def split_lo(c, i=0):
                if isinstance(i, int) and c >= U_END:
                    return
                s = slot(c)
                dve.wait_ge(w_hi, c + RING * i + 1)
                tt(WL[:, s, :], RAW[:, s, :], WH[:, s, :].bitcast(F32), ALU.subtract).then_inc(w_lo, 1)

            def xn(n, t):
                dve.wait_ge(rstd_ok, NT * n + t + 1)
                dve.wait_ge(gpre_loaded, 16 * (n + 1))
                for q in range(2):
                    a = slice(q * 512, (q + 1) * 512)
                    stt(XN[:, t, a], H[:, t, a], RS[:, t:t + 1], GPRE[:, a], ALU.mult, ALU.mult).then_inc(xn_ok, 1)

            def xn_lo(n, t):
                for q in range(2):
                    dve.wait_ge(xt_hi, 4 * n + 2 * t + q + 1)
                    a = (slice(None), slice(4 * q, 4 * q + 4), slice(t * P, (t + 1) * P))
                    tt(XTL[a], PS[6 + q][:].rearrange("p (k c) -> p k c", k=4), XTH[a].bitcast(F32),
                       ALU.subtract).then_inc(xt_lo, 1)

            def ffn(f, u0):
                n0 = FF_STEPS * f

                def up_part(c, j, i=0):
                    dve.wait_ge(gate_ok, j + n0 + 1)
                    dve.wait_ge(w_used, c + 3 * i + 2)
                    if not isinstance(j, int) or j:
                        dve.wait_ge(hT_lo, j + n0)
                    tt(HS, PS[5][:], SG, ALU.mult).then_inc(h_ready, 1)

                def hidden_lo(j, src=HS, half=0):
                    dve.wait_ge(hT_hi, j + n0 + 1)
                    tt(KTL[:, half_of(half)], src, KTH[:, half_of(half)].bitcast(F32), ALU.subtract).then_inc(hT_lo, 1)
                split_lo(u0 + 3)
                up_part(u0, 0)
                split_lo(u0 + 4)
                hidden_lo(0, PS[7][:])

                def step(c, j, i=0):
                    split_lo(c + 3, i)
                    split_lo(c + 4, i)
                    up_part(c, j, i)
                    split_lo(c + 5, i)
                    hidden_lo(j)
                with dve.Fori(1, FF_STEPS - 1) as i:
                    step(u0 - 1, i, i)
                c, j = u0 + 3 * FF_STEPS - 4, FF_STEPS - 1
                split_lo(c + 3)
                up_part(c, j)
                hidden_lo(j, HS, 1)
                split_lo(c + 4)

            def y_gain(m, unit, t):
                dve.wait_ge(acc_half, m + 1) if t == 0 else dve.wait_ge(w_used, unit + 1)
                for b in (2 * t + 1, 2 * t):
                    if b % 2 == 0:
                        dve.wait_ge(y_sq, 4 * post_no[m] + b + 1)
                    tt(TB[:, b, :], PS[b][:], GAIN[:, (b % 2) * 512:(b % 2 + 1) * 512], ALU.mult).then_inc(y_gained, 1)

            def y_sum(m, t):
                dve.wait_ge(y_sq, 4 * post_no[m] + 2 * t + 2)
                tt(RS[:, 8 + t:9 + t], SS[:, 8 + 2 * t:9 + 2 * t], SS[:, 9 + 2 * t:10 + 2 * t],
                   ALU.add).then_inc(y_ss, 1)

            def residual(m, t):
                dve.wait_ge(y_rs, NT * post_no[m] + t + 1)
                dve.wait_ge(y_gained, 4 * post_no[m] + 2 * t + 2)
                stt(H[:, t, :], TB[:, 2 * t:2 * t + 2, :].rearrange("p b c -> p (b c)"), RS[:, 8 + t:9 + t], H[:, t, :],
                    ALU.mult, ALU.add).then_inc(h_done, 1)

            def add_h(m, unit, t):
                dve.wait_ge(acc_half, m + 1) if t == 0 else dve.wait_ge(w_used, unit + 1)
                for h in range(2):
                    s = H[:, t, h * 512:(h + 1) * 512]
                    ins = tt(s, PS[2 * t + h][:], s, ALU.add)
                    ins.then_inc(h_done, 1) if h else own.inc(ins)
                own.wait()

            def boundary(m, unit, gains=0):
                own.wait()
                if m in post_no:
                    dve.wait_ge(gain_loaded, 16 * gains)
                    y_gain(m, unit, 0)
                    y_sum(m, 0)
                    residual(m, 0)
                    y_gain(m, unit, 1)
                    xn(m + 1, 0)
                    y_sum(m, 1)
                    residual(m, 1)
                else:
                    add_h(m, unit, 0)
                    if m < 4:
                        xn(m + 1, 0)
                    add_h(m, unit, 1)
                if m == 4:
                    return
                xn_lo(m + 1, 0)
                xn(m + 1, 1)
                xn_lo(m + 1, 1)
                dve.wait_ge(w_lo, unit + 3)
                split_lo(unit + 3)

            def kt_lo(n, scale=None):
                dve.wait_ge(k_hi, n + 1)
                if scale is None:
                    ins = tt(KTL[:, half_of(n)], PS[7][:], KTH[:, half_of(n)].bitcast(F32), ALU.subtract)
                else:
                    ins = stt(KTL[:, half_of(n)], PS[7][:], scale, KTH[:, half_of(n)].bitcast(F32), ALU.mult, ALU.subtract)
                ins.then_inc(k_lo, 1)

            def products(n0, u0, n, scale=None, turned=False):
                for j in range(n):
                    if j or not turned:
                        kt_lo(n0 + j, scale)
                    if n0 == 8:
                        if 0 < j < n - 1:
                            split_lo(u0 + j - 1 + 3)
                    elif j < 3:
                        split_lo(u0 + j - 2 + 3)
                    else:
                        split_lo(u0 + 1 + 3)

            xn(0, 0)
            xn_lo(0, 0)
            split_lo(0)
            xn(0, 1)
            split_lo(1)
            xn_lo(0, 1)
            split_lo(2)
            dve.wait_ge(loaded, 32)
            dve.wait_ge(ident_loaded, 16)
            dve.wait_ge(tab_loaded, 16)
            own.inc(nc.vector.tensor_copy(ID16[:], IDENT))
            nc.vector.tensor_copy(MASK16[:], tab("causal_t").unsqueeze(1).to_broadcast([P, 4, P])).then_inc(consts16, 1)
            own.link(ts(SUBLN, SUBLN, 1.0 - LAM_INIT, None, ALU.mult))
            ffn(0, U_FFN1)
            boundary(0, U_FFN1 + 3 * FF_STEPS - 1, 1)

            def x_keep(m):
                dve.wait_ge(x_turned, m + 1)
                nc.vector.tensor_copy(
                    BUF1[:, :, m * 256:(m + 1) * 256].rearrange("p t (f c) -> p f t c", f=2),
                    PS[6 + m % 2][:].rearrange("p (f t c) -> p f t c", f=2, t=NT)).then_inc(x_kept, 1)

            def step_sizes(c):
                dve.wait_ge(w_used, U_XZ + 3)
                bias = ROWS[:, ROW["dt_bias"]:ROW["dt_bias"] + 32].unsqueeze(1).to_broadcast([P, NT, 32])
                tt(DT[:, 0, :].rearrange("p (t h) -> p t h", t=NT),
                   PS[5][:].rearrange("p (t c) -> p t c", t=NT)[:, :, 0:32], bias, ALU.add).then_inc(dt_raw, 1)
                dve.wait_ge(dt_raw, 1)
                stt(DT[:, 1, :], DT[:, 0, :], -1.0, DT[:, 0, :], ALU.mult, ALU.min).then_inc(dt_abs, 1)
                own.link(ts(DT[:, 0, :], DT[:, 0, :], 0.0, None, ALU.max))
                dve.wait_ge(lam_loaded, 16)
                lam = XDT[:, 0:256].rearrange("p (a b c) -> p a b c", a=2, b=2)
                T1L = T1[:, 0:128].rearrange("p (a c) -> p a c", a=2)
                own.link(tt(T1L, lam[:, :, 0, :], lam[:, :, 1, :], ALU.mult))
                nc.vector.tensor_reduce(SM[:, 36:38], T1L, AX.X, ALU.add).then_inc(lam_dot, 1)
                split_lo(c + 3)
                dve.wait_ge(dt_exp, 1)
                e, y, z, q = DT[:, 1, :], DT[:, 2, :], DT[:, 3, :], DT[:, 4, :]
                own.link(ts(y, e, 2.0, None, ALU.add))
                own.link(nc.vector.reciprocal(y, y))
                own.link(tt(y, y, e, ALU.mult))
                own.link(tt(z, y, y, ALU.mult))
                own.link(ts(q, z, 1.0 / 15, None, ALU.mult))
                for d in (13, 11, 9, 7, 5, 3):
                    own.link(stt(q, q, 1.0 / d, z, ALU.add, ALU.mult))
                own.link(stt(q, q, 1.0, y, ALU.add, ALU.mult))
                own.link(stt(DT[:, 2, :], q, 2.0, DT[:, 0, :], ALU.mult, ALU.add))
                stt(DT[:, 3, :].rearrange("p (t h) -> p t h", t=NT), DT[:, 2, :].rearrange("p (t h) -> p t h", t=NT), -1.0,
                    DT[:, 5, 0:32].unsqueeze(1).to_broadcast([P, NT, 32]), ALU.mult, ALU.mult).then_inc(a_ok, 1)
                dve.wait_ge(lam_exp, 1)
                own.link(tt(SM[:, 38:39], SM[:, 37:38], SM[:, 36:37], ALU.subtract))
                ts(SM[:, 39:40], SM[:, 38:39], -LAM_INIT, None, ALU.add).then_inc(lam_ok, 1)
                dve.wait_ge(lam_ok, 1)
                own.link(ts(ROWS[:, ROW["dt_bias"]:ROW["dt_bias"] + 8], ROWS[:, ROW["sinks"]:ROW["sinks"] + 8], -1.0, None, ALU.mult))

            for m, (kind, n) in enumerate(XZ):
                c = U_XZ + m
                if kind == "dt":
                    step_sizes(c)
                    continue
                if kind == "x":
                    dve.wait_ge(conv_1, n + 1)
                    for back in (1, 2, 3):
                        for f in range(2):
                            j = GC["conv_w"] + (CONV_K - 1 - back) * XBC_TILES + 2 * n + f
                            dst = CONV[:, f * TOK + back:(f + 1) * TOK]
                            ins = stt(dst, PS[4 + n % 2][:, f * TOK:(f + 1) * TOK - back], COLS[:, j:j + 1], dst,
                                      ALU.mult, ALU.add)
                            if back == 3 and f == 1:
                                ins.then_inc(conv_done, 1)
                            else:
                                own.inc(ins)
                        if back < 3:
                            own.wait()
                    if 1 <= n <= 8:
                        x_keep(n - 1)
                split_lo(c + 3)
            dve.wait_ge(x_turned, 9)
            nc.vector.tensor_copy(B0, PS[6][:]).then_inc(x_kept, 1)
            dve.wait_ge(cums, 1)
            ts(DT[:, 4, :].rearrange("p (t h) -> p t h", t=NT),
               PS[3][:, 0:64].rearrange("p (t h) -> p t h", t=NT), -1.0, None, ALU.mult).then_inc(cums_neg, 1)
            dve.wait_ge(cums_exp, 1)
            dve.wait_ge(gain_loaded, 32)

            def by_head(ap):
                return ap.rearrange("p (h c) -> p h c", h=HPG)

            def heads_bc(ap):
                return ap.unsqueeze(2).to_broadcast([P, HPG, SSD_P])

            split_lo(U_QKV + 3)
            u = U_QKV + 1
            for r in range(9):
                if r < 8:
                    g, c = divmod(r, 2)
                    xs = BUF1[:, c, g * GW:(g + 1) * GW]
                    hs = slice(c * 32 + g * HPG, c * 32 + (g + 1) * HPG)
                    if r:
                        dve.wait_ge(ssd_y, r)
                    own.link(tt(by_head(XDT), by_head(xs), heads_bc(DT[:, 2, hs]), ALU.mult))
                    if c == 0:
                        tt(by_head(XDEC), by_head(XDT), heads_bc(EX[:, 1, c, g * HPG:(g + 1) * HPG]),
                           ALU.mult).then_inc(xdec_ok, 1)
                if r:
                    n = r - 1
                    g, c = divmod(n, 2)
                    dve.wait_ge(skip_ok, r)
                    dve.wait_ge(ssd_y, r)
                    own.link(tt(Y, PS[3][:], Y, ALU.add))
                    if c:
                        dve.wait_ge(ssd_st, r)
                        own.link(tt(by_head(T1), by_head(PS[6][:]),
                                    heads_bc(EX[:, 0, c, g * HPG:(g + 1) * HPG]), ALU.mult))
                        own.link(tt(Y, Y, T1, ALU.add))
                    zs = BUF2[:, c, g * GW:(g + 1) * GW]
                    tt(Y, Y, zs, ALU.mult).then_inc(y_gated, 1)
                if r < 8:
                    dve.wait_ge(ssd_e, r + 1)
                    dve.wait_ge(ssd_cb, r + 1)
                    for b in range(2):
                        ins = tt(E[:, 4 * b:4 * b + 4, :], E[:, 4 * b:4 * b + 4, :],
                                 PS[2][:, 0:P].unsqueeze(1).to_broadcast([P, 4, P]), ALU.mult)
                    ins.then_inc(ssd_m, 1)
                if r:
                    dve.wait_ge(y_rms, r)
                    stt(zs, Y, RS[:, 4:5], GAIN[:, g0(n) * GW:(g0(n) + 1) * GW], ALU.mult, ALU.mult).then_inc(ys_ok, 1)
                else:
                    def g0(n):
                        return n // 2
                for _u in range(beside(r)):
                    split_lo(u + 3)
                    u += 1

            slopes = [2.0 ** (-8.0 * (h + 1) / DA_HEADS) for h in range(DA_HEADS)]

            def o_keep(h):
                dve.wait_ge(pv, h + 1)
                nc.vector.tensor_copy(XN[:, :, h * P:(h + 1) * P],
                                      PS[6][:, 0:256].rearrange("p (i c) -> p i c", i=NT)).then_inc(o_kept, 1)
            dve.wait_ge(ys_ok, 8)
            for h in range(9):
                if h < 8:
                    kt_lo(h)
                    dve.wait_ge(scores, h + 1)
                    if h:
                        own.wait()
                    f = -8.0 * slopes[h]
                    for m in range(2):
                        own.inc(stt(SMAP[:, m, :], tab("dist"), f, PS[4 + m][:, 0:384], ALU.mult, ALU.add))
                    own.wait()
                    own.inc(nc.vector.tensor_reduce(SM[:, 0:2], SMAP[:, :, 0:P], AX.X, ALU.max))
                    own.link(nc.vector.tensor_reduce(SM[:, 2:4], SMAP[:, :, P:3 * P], AX.X, ALU.max))
                    ts(SM[:, 4:8], SM[:, 0:4], -0.125, None, ALU.mult).then_inc(s_ready, 1)
                    split_lo(U_SSDW + h - 1 + 3)
                if h:
                    o_keep(h - 1)
                if h < 8:
                    dve.wait_ge(p_exp, 2 * (h + 1))
                    own.link(nc.vector.reciprocal(SM[:, 12:16], SM[:, 8:12]))
                    own.link(ts(SM[:, 16:20], SM[:, 12:16], SM[:, 39:40], None, ALU.mult))
                    if h:
                        dve.wait_ge(p_turned, h)
                    own.inc(ts(ATT[:, 0:P], SMAP[:, 0, 0:P], SM[:, 12:13], None, ALU.mult))
                    own.link(ts(ATT[:, P:3 * P], SMAP[:, 0, P:3 * P], SM[:, 14:15], None, ALU.mult))
                    own.inc(stt(ATT[:, 0:P], SMAP[:, 1, 0:P], SM[:, 17:18], ATT[:, 0:P], ALU.mult, ALU.add))
                    stt(ATT[:, P:3 * P], SMAP[:, 1, P:3 * P], SM[:, 19:20], ATT[:, P:3 * P], ALU.mult,
                        ALU.add).then_inc(attn_ok, 1)
                    dve.wait_ge(attn_ok, h + 1)
            split_lo(U_SSDW + 7 + 3)
            dve.wait_ge(o_rs, 1)
            o4 = XN[:].rearrange("p t (h c) -> p (t h) c", c=P)
            tt(o4, o4, RS[:].unsqueeze(2).to_broadcast([P, 16, P]), ALU.mult).then_inc(o_ok, 1)

            dve.wait_ge(gain_loaded, 48)

            def first_merge(gates, b, signal):
                t, cols = b // 2, slice((b % 2) * 512, (b % 2 + 1) * 512)
                tt(V[:, t, cols], PS[b][:], gates[:, t, cols], ALU.mult).then_inc(signal, 1)

            def second_merge(m, gates, unit):
                def product(b, c=slice(0, 512)):
                    g = slice(D + (b % 2) * 512 + c.start, D + (b % 2) * 512 + c.stop)
                    own.inc(tt(TB[:, b, c], PS[b][:, c], gates[:, b // 2, g], ALU.mult))

                def add(b, c=slice(0, 512)):
                    v = V[:, b // 2, (b % 2) * 512 + c.start:(b % 2) * 512 + c.stop]
                    tt(v, v, TB[:, b, c], ALU.add).then_inc(merged, 1)
                dve.wait_ge(branch_half, m + 1)
                product(0)
                product(1)
                own.wait()
                add(0)
                add(1)
                dve.wait_ge(w_used, unit + 1)
                left, right = slice(0, 256), slice(256, 512)
                product(2, left)
                own.wait()
                add(2, left)
                product(2, right)
                own.wait()
                add(2, right)
                product(3)
                own.wait()
                add(3)
            for n in range(8):
                if n == 7:
                    kt_lo(8, SUBLN)
                if n:
                    dve.wait_ge(w_used, gate_unit(n) + 1)
                else:
                    dve.wait_ge(gate0_kept, 1)
                cols = slice(n * 256, (n + 1) * 256)
                tt(BUF1[:, :, cols], PS[4 + n % 2][:].rearrange("p (t c) -> p t c", t=NT) if n else BUF1[:, :, cols],
                   GAIN[:, cols].unsqueeze(1).to_broadcast([P, NT, 256]), ALU.add).then_inc(g_logit, 1)
                if n:
                    split_lo(gate_unit(n) + 3)
                if n == 5:
                    dve.wait_ge(gates_ok, 4)
                    for b in range(4):
                        first_merge(BUF1, b, acc_read)
            products(8, U_DAW, 4, SUBLN, True)
            dve.wait_ge(acc_read, 4)
            dve.wait_ge(gates_ok, 8)
            second_merge(0, BUF1, U_DAW + 3)
            products(12, U_WOUT, 4)
            boundary(1, U_WOUT + 3, 4)
            ffn(1, U_FFN2)
            boundary(2, U_FFN2 + 3 * FF_STEPS - 1, 5)

            def rope(x, cos, sin, heads, half, signal):
                x1, x2 = x[:, :, :, 0:half], x[:, :, :, half:2 * half]
                cb = cos.rearrange("p (t c) -> p t c", t=NT).unsqueeze(2).to_broadcast([P, NT, heads, half])
                sbc = sin.rearrange("p (t c) -> p t c", t=NT).unsqueeze(2).to_broadcast([P, NT, heads, half])
                n = NT * heads * half
                t = [XN[:].rearrange("p t c -> p (t c)")[:, k * n:(k + 1) * n]
                     .rearrange("p (t h c) -> p t h c", t=NT, h=heads) for k in range(3)]
                own.wait()
                own.inc(tt(t[0], x1, cb, ALU.mult))
                own.inc(tt(t[1], x2, sbc, ALU.mult))
                own.link(tt(t[2], x2, cb, ALU.mult))
                own.link(tt(x2, x1, sbc, ALU.mult))
                own.inc(tt(x1, t[0], t[1], ALU.subtract))
                tt(x2, x2, t[2], ALU.add).then_inc(signal, 1)
            for q in range(6):
                split_lo(U_IN2 + q + 3)
                if q == 2:
                    dve.wait_ge(lat_rs, 1)
                    for t in range(NT):
                        own.inc(ts(PROJ[:, t, LAT0:LAT0 + Q_RANK], PROJ[:, t, LAT0:LAT0 + Q_RANK], RS[:, t:t + 1], None,
                                   ALU.mult))
                        ts(PROJ[:, t, LAT0 + Q_RANK:KR0], PROJ[:, t, LAT0 + Q_RANK:KR0], RS[:, 2 + t:3 + t], None,
                           ALU.mult).then_inc(lat_ok, 1)
            dve.wait_ge(lat_ok, 2)
            dve.wait_ge(proj_kept, 6)
            for j in range(3):
                dve.wait_ge(lat_hi, 1 + (j == 2))
                ins = stt(KTL[:, j * TOK:(j + 1) * TOK], PS[6 + j // 2][:, (j % 2) * TOK:(j % 2 + 1) * TOK],
                          COLS[:, GC["q_lat"] + j:GC["q_lat"] + j + 1], KTH[:, j * TOK:(j + 1) * TOK].bitcast(F32),
                          ALU.mult, ALU.subtract)
            ins.then_inc(lat_lo, 1)
            rope(PROJ[:, :, 0:640].rearrange("p t (h c) -> p t h c", c=HD), tab("cos_a"), tab("sin_a"), 10, HD // 2,
                 swa_roped)
            dve.wait_ge(swa_roped, 1)
            split_lo(U_GATE2A + 3)
            rope(PROJ[:, :, KR0:PJ].unsqueeze(2), tab("cos_b"), tab("sin_b"), 1, ROPE // 2, mla_roped)
            dve.wait_ge(mla_roped, 1)
            own.inc(nc.vector.tensor_copy(KM[:, :, :, NOPE:MLA_QK],
                                          PROJ[:, :, KR0:PJ].unsqueeze(2).to_broadcast([P, NT, MLA_HEADS, ROPE])))
            for n in range(2):
                split_lo(U_UQ + n + 3)
            dve.wait_ge(lat_hi, 3)
            for j in range(2):
                ins = stt(KTL[:, j * TOK:(j + 1) * TOK], PS[7][:, j * TOK:(j + 1) * TOK],
                          COLS[:, GC["kv_lat"] + j:GC["kv_lat"] + j + 1], KTH[:, j * TOK:(j + 1) * TOK].bitcast(F32),
                          ALU.mult, ALU.subtract)
            ins.then_inc(lat_lo, 1)
            dve.wait_ge(q_kept, 4)
            rope(QM[:, :, :, NOPE:MLA_QK], tab("cos_b"), tab("sin_b"), MLA_HEADS, ROPE // 2, mla_roped)
            dve.wait_ge(mla_roped, 2)
            split_lo(U_GATE2B + 3)
            split_lo(U_UKV + 3)
            dve.wait_ge(kv_kept, 4)
            nc.vector.tensor_copy(KM[:, :, :, 0:NOPE],
                                  V[:].rearrange("p t (h c) -> p t h c", h=MLA_HEADS)[:, :, :, 0:NOPE]).then_inc(kcat_ok, 1)
            nsinks = ROWS[:, ROW["dt_bias"]:ROW["dt_bias"] + 8]
            for r in range(9):
                if r == 8:
                    kt_lo(16)
                if r < 8:
                    for a in range(2):
                        dve.wait_ge(sc2, 2 * r + a + 1)
                        if r and a == 0:
                            dve.wait_ge(o2_kept, r - 1) if r > 1 else None
                        if r:
                            dve.wait_ge(p2_turned, 2 * (r - 1) + a + 1)
                        own.link(tt(SC[a], PS[2 + a][:, 0:384], tab(("swa", "mla")[a]), ALU.add))
                        for i in range(NT):
                            own.inc(nc.vector.tensor_reduce(SM[:, 20 + 2 * a + i:21 + 2 * a + i],
                                                            SC[a][:, i * P:i * P + P * (i + 1)], AX.X, ALU.max))
                        own.wait()
                        if a == 0:
                            if r:
                                dve.wait_ge(p2_exp, 2 * r)
                            ts(SM[:, 0:2], SM[:, 20:22], -HD ** -0.5, nsinks[:, r:r + 1], ALU.mult,
                               ALU.min).then_inc(s2_ready, 1)
                        else:
                            ts(SM[:, 2:4], SM[:, 22:24], -MLA_QK ** -0.5, None, ALU.mult).then_inc(s2_ready, 1)
                if r:
                    dve.wait_ge(pv2, r)
                    dst = XN[:].rearrange("p i (a h c) -> p a i h c", a=2, h=8)[:, :, :, r - 1, :]
                    tt(dst, PS[6][:, 0:256].rearrange("p (a i c) -> p a i c", a=2, i=NT),
                       SM[:, 28 + 0:32].rearrange("p (a i) -> p a i", a=2).unsqueeze(3).to_broadcast([P, 2, NT, 64]),
                       ALU.mult).then_inc(o2_kept, 1)
                    dve.wait_ge(o2_kept, r)
                if r < 6:
                    split_lo(g2_unit(2 + r) + 3)
                if r < 8:
                    dve.wait_ge(p2_exp, 2 * (r + 1))
                    own.link(tt(SM[:, 4:6], SM[:, 4:6], SM[:, 8:10], ALU.add))
                    own.link(nc.vector.reciprocal(SM[:, 28:32], SM[:, 4:8]))
            kt_lo(17)
            split_lo(U_OSWA + 3)
            kt_lo(18)
            dve.wait_ge(gates2, 2)
            dve.wait_ge(swa_half, 1)
            for b in range(4):
                if b == 2:
                    dve.wait_ge(w_used, U_OSWA + 2)
                first_merge(BUF2, b, acc_read)
            split_lo(U_OSWA + 1 + 3)
            kt_lo(19)
            dve.wait_ge(gates2, 4)
            dve.wait_ge(acc_read, 8)
            second_merge(1, BUF2, U_OMLA + 1)
            products(20, U_OUT2, 4)
            boundary(3, U_OUT2 + 3)
            ffn(2, U_FFN3)
            boundary(4, U_END - 1)
            dve.wait_ge(gain_loaded, 96)
            for t in range(NT):
                dve.wait_ge(rstd_ok, NT * 5 + t + 1)
                stt(XN[:, t, :], H[:, t, :], RS[:, t:t + 1], GAIN[:, 0:D], ALU.mult, ALU.mult).then_inc(out_ok, 1)

        @block.tensor
        def _(pe):
            mm = nc.tensor.matmul

            def norm(n, c, bank):
                def turn(t):
                    for q in range(2):
                        pe.wait_ge(xn_ok, 4 * n + 2 * t + q + 1)
                        if t:
                            pe.wait_ge(xt_lo, 4 * n + q + 1)
                        for k in range(4):
                            j = 4 * q + k
                            ins = nc.tensor.transpose(PS[6 + q][:, k * P:(k + 1) * P], XN[:, t, j * P:(j + 1) * P],
                                                      IDENT)
                        ins.then_inc(xn_turned, 1)
                turn(0)
                pe.wait_ge(xt_lo, 4 * n + 2)
                tokens(c, bank, only=0)
                turn(1)
                tokens(c + 1, bank + 1, only=0)
                pe.wait_ge(xt_lo, 4 * n + 4)
                tokens(c, bank, only=1)
                tokens(c + 1, bank + 1, only=1)

            def parts(ps, stat_hi, stat_lo, mov_hi, mov_lo, first, last):
                mm(ps, stat_hi, mov_hi, start=first, stop=False)
                mm(ps, stat_hi, mov_lo, start=False, stop=False)
                return mm(ps, stat_lo, mov_hi, start=False, stop=last)

            def channels(c, bank, i=0):
                s = slot(c)
                pe.wait_ge(w_lo, c + RING * i + 1)
                for f in range(2):
                    for k in range(KD):
                        ws = slice(k * 256 + f * P, k * 256 + (f + 1) * P)
                        ins = parts(PS[bank][:, f * TOK:(f + 1) * TOK], WH[:, s, ws], WL[:, s, ws],
                                    XTH[:, k, :], XTL[:, k, :], k == 0, k == KD - 1)
                ins.then_inc(w_used, 1)

            def tokens(c, bank, wide=256, only=None):
                s = slot(c)
                pe.wait_ge(w_lo, c + 1)
                for t in range(NT) if only is None else (only,):
                    for k in range(KD):
                        ws = slice(k * wide, (k + 1) * wide)
                        xs = slice(t * P, (t + 1) * P)
                        ins = parts(PS[bank][:, t * 256:t * 256 + wide], XTH[:, k, xs], XTL[:, k, xs],
                                    WH[:, s, ws], WL[:, s, ws], k == 0, k == KD - 1)
                if only != 0:
                    ins.then_inc(w_used, 1)

            def rows(c, first, last, i=0, banks=0, half=0, by_tile=None, tile_free=None):
                s = slot(c)
                pe.wait_ge(w_lo, c + RING * i + 1)
                order = [(k, t) for k in range(2) for t in range(NT)]
                if by_tile or tile_free:
                    order.sort(key=lambda kt: kt[1])
                for k, t in order:
                    if tile_free and k == 0:
                        tile_free(t)
                    a = slice(half * 512 + k * TOK + t * P, half * 512 + k * TOK + (t + 1) * P)
                    for h in range(2):
                        ws = slice(k * D + h * 512, k * D + (h + 1) * 512)
                        ins = parts(PS[banks + 2 * t + h][:], KTH[:, a], KTL[:, a], WH[:, s, ws], WL[:, s, ws],
                                    first and k == 0, last and k == 1)
                    if by_tile and (k, t) == (1, 0):
                        ins.then_inc(by_tile, 1)
                ins.then_inc(w_used, 1)

            def ffn(f, u0):
                n0 = FF_STEPS * f
                def step(c, j, i=0, first=False):
                    pe.wait_ge(gate_ok, j + n0)
                    channels(c, 4, i)
                    pe.wait_ge(h_ready, j + n0)
                    if first:
                        for k in range(2):
                            for t in range(NT):
                                h = HS[:, t * 256 + k * P:t * 256 + (k + 1) * P]
                                ins = nc.tensor.transpose(PS[7][:, k * TOK + t * P:k * TOK + (t + 1) * P], h, IDENT)
                        ins.then_inc(h0_turned, 1)
                    channels(c + 1, 5, i)
                    pe.wait_ge(hT_lo, j + n0)
                    rows(c + 2, first, False, i)
                step(u0 + 2, 1, 0, True)
                with pe.Fori(2, FF_STEPS) as i:
                    step(u0 - 1, i, i)
                pe.wait_ge(hT_lo, n0 + FF_STEPS)
                rows(u0 + 3 * FF_STEPS - 1, False, True, half=1, by_tile=acc_half)

            def turn_rows(n, src, k0):
                if n:
                    pe.wait_ge(k_lo, n)
                for k in range(2):
                    for t in range(NT):
                        ins = nc.tensor.transpose(PS[7][:, k * TOK + t * P:k * TOK + (t + 1) * P],
                                                  src[:, t, (k0 + k) * P:(k0 + k + 1) * P], IDENT)
                ins.then_inc(k_turned, 1)

            def products(n0, u0, n, src, k0=0, ready=None, by_tile=None, turned=False):
                def turn(j):
                    if ready:
                        ready(j)
                    turn_rows(n0 + j, src, k0 + 2 * j)
                if not turned:
                    turn(0)
                for j in range(n):
                    if j + 1 < n:
                        turn(j + 1)
                    pe.wait_ge(k_lo, n0 + j + 1)
                    rows(u0 + j, j == 0, j == n - 1, half=(n0 + j) % 2, by_tile=by_tile if j == n - 1 else None)

            pe.wait_ge(ident_loaded, 16)
            norm(0, U_FFN1, 4)
            ffn(0, U_FFN1)
            norm(1, U_XZ, 0)

            def turn_x(n):
                pe.wait_ge(conv_silu, n + 1)
                if n >= 2:
                    pe.wait_ge(x_kept, n - 1)
                for f in range(2):
                    for t in range(NT):
                        ins = nc.tensor.transpose(PS[6 + n % 2][:, f * TOK + t * P:f * TOK + (t + 1) * P],
                                                  XSIL[:, f * TOK + t * P:f * TOK + (t + 1) * P], IDENT)
                ins.then_inc(x_turned, 1)
            for m, (kind, n) in enumerate(XZ):
                c = U_XZ + m
                if kind == "x":
                    if n >= 2:
                        pe.wait_ge(conv_done, n - 1)
                    elif n == 1:
                        pe.wait_ge(dt_raw, 1)
                    channels(c, 4 + n % 2)
                    if 1 <= n <= 8:
                        turn_x(n - 1)
                elif kind == "dt":
                    tokens(c, 5, SSD_HEADS)
                elif n >= 2:
                    pe.wait_ge(z_kept, n - 1)
                    tokens(c, n % 2)
                if (kind, n) == ("z", 3):
                    pe.wait_ge(a_ok, 1)
                    for k, tri in enumerate((UPTO, AFTER)):
                        for v in range(NT):
                            ins = mm(PS[3][:, k * 64 + v * 32:k * 64 + (v + 1) * 32], tri, DT[:, 3, v * 32:(v + 1) * 32],
                                     start=True, stop=True)
                    ins.then_inc(cums, 1)
                if (kind, n) == ("x", 11):
                    pe.wait_ge(conv_silu, 10)
                    pe.wait_ge(x_kept, 7)
                    for g in range(SSD_GROUPS):
                        ins = nc.tensor.transpose(PS[6][:, g * P:(g + 1) * P], BT[:, g, 0:P], IDENT)
                    ins.then_inc(x_turned, 1)
            def qkv(u):
                n = u - U_QKV
                pe.wait_ge(conv_done, 12 - n) if n < 2 else pe.wait_ge(qkv_kept, n - 1)
                (channels if n < 8 else tokens)(u, 5 - n % 2)

            qkv(U_QKV)
            pe.wait_ge(consts16, 1)
            pe.wait_ge(conv_silu, 12)
            pe.wait_ge(z_kept, 8)
            u = U_QKV + 1
            for r in range(9):
                if r < 8:
                    g, c = divmod(r, 2)
                    if r:
                        pe.wait_ge(ssd_e, r)
                        pe.wait_ge(ssd_m, r)
                    mm(PS[2][:, 0:P], BT[:, g, c * P:(c + 1) * P], CT[:, g, c * P:(c + 1) * P], start=True,
                       stop=True).then_inc(ssd_cb, 1)
                    pe.wait_ge(ab_ok, r + 1)
                    for b in range(2):
                        mm(PS[b][:], ID16[:], MASK16[:].rearrange("p h l -> p (h l)"), start=True, stop=False)
                        for e in range(4):
                            ins = mm(PS[b][:, e * P:(e + 1) * P], AB[:, 4 * b + e, :], UPTO, start=False, stop=e == 3)
                    ins.then_inc(ssd_mm, 1)
                if r:
                    n = r - 1
                    g, c = divmod(n, 2)
                    if n:
                        pe.wait_ge(y_gated, n)
                    pe.wait_ge(cums_exp, 1)
                    pe.wait_ge(cums_neg, 1)
                    if c == 0:
                        pe.wait_ge(xdec_ok, n // 2 + 1)
                        mm(PS[6][:], B0[:, g * P:(g + 1) * P], XDEC, start=True, stop=True).then_inc(ssd_st, 1)
                    else:
                        pe.wait_ge(state_ok, n // 2 + 1)
                        mm(PS[6][:], CT[:, g, P:TOK], STATE, start=True, stop=True).then_inc(ssd_st, 1)
                    pe.wait_ge(ssd_m, r)
                    for e in range(HPG):
                        ins = mm(PS[3][:, e * SSD_P:(e + 1) * SSD_P], E[:, e, :], XDT[:, e * SSD_P:(e + 1) * SSD_P],
                                 start=True, stop=True)
                    ins.then_inc(ssd_y, 1)
                for _u in range(beside(r)):
                    qkv(u)
                    u += 1
            tokens(U_GATE0, 2)
            pe.wait_ge(ys_ok, 8)
            pe.wait_ge(qkv_kept, 12)
            for h in range(9):
                if h:
                    pe.wait_ge(attn_ok, h)
                    if h >= 2:
                        pe.wait_ge(o_kept, h - 1)
                    for b in range(3):
                        ins = nc.tensor.transpose(PS[6][:, b * P:(b + 1) * P], ATT[:, b * P:(b + 1) * P], IDENT)
                    ins.then_inc(p_turned, 1)
                if h < 8:
                    if h == 0:
                        turn_rows(0, BUF2, 0)
                    if h:
                        pe.wait_ge(s_ready, h)
                    for m in range(2):
                        ms = slice(m * 64, (m + 1) * 64)
                        mm(PS[4 + m][:, 0:P], QK[ms, h, 0, 0:P], QK[ms, h, 1, 0:P], start=True, stop=True)
                        ins = mm(PS[4 + m][:, P:3 * P], QK[ms, h, 0, P:TOK], QK[ms, h, 1, :], start=True, stop=True)
                    ins.then_inc(scores, 1)
                if h:
                    pe.wait_ge(p_kept, h)
                    vs = slice((h - 1) * P, h * P)
                    mm(PS[6][:, 0:P], PT[:, 0:P], V[:, 0, vs], start=True, stop=True)
                    mm(PS[6][:, P:2 * P], PT[:, P:2 * P], V[:, 0, vs], start=True, stop=False)
                    mm(PS[6][:, P:2 * P], PT[:, 2 * P:3 * P], V[:, 1, vs], start=False, stop=True).then_inc(pv, 1)
                if h < 8:
                    if h < 7:
                        turn_rows(h + 1, BUF2, 2 * (h + 1))
                    pe.wait_ge(k_lo, h + 1)
                    if h == 0:
                        pe.wait_ge(gate0_kept, 1)
                    rows(U_SSDW + h, h == 0, h == 7, half=h % 2)
            for n in range(1, 8):
                pe.wait_ge(s_ready, 8) if n < 3 else pe.wait_ge(g_logit, n - 1)
                if n == 7:
                    pe.wait_ge(o_ok, 1)
                    turn_rows(8, XN, 0)
                tokens(gate_unit(n), 4 + n % 2)
            pe.wait_ge(acc_read, 4)
            products(8, U_DAW, 4, XN, turned=True, by_tile=branch_half)
            products(12, U_WOUT, 4, V, ready=lambda j: pe.wait_ge(merged, min(3 + j, 5)), by_tile=acc_half)
            norm(2, U_FFN2, 4)
            ffn(1, U_FFN2)
            norm(3, U_IN2, 4)

            for q in range(2, 6):
                if q >= 4:
                    pe.wait_ge(proj_kept, q - 3)
                tokens(U_IN2 + q, (4, 5, 0, 1)[q % 4], min(256, PJ - 256 * IN2[q]))

            def turn_latent(bank, c0, tiles):
                for k in range(tiles):
                    for t in range(NT):
                        ins = nc.tensor.transpose(PS[bank][:, k * TOK + t * P:k * TOK + (t + 1) * P],
                                                  PROJ[:, t, c0 + k * P:c0 + (k + 1) * P], IDENT)
                ins.then_inc(lat_turned, 1)
            pe.wait_ge(lat_ok, 2)
            turn_latent(6, LAT0, 2)
            turn_latent(7, LAT0 + 2 * P, 1)
            pe.wait_ge(proj_kept, 4)
            tokens(g2_unit(0), 0)
            for n in range(2):
                c = U_UQ + n
                pe.wait_ge(w_lo, c + 1)
                if n == 0:
                    pe.wait_ge(lat_lo, 1)
                    pe.wait_ge(proj_kept, 6)
                for t in range(NT):
                    for k in range(3):
                        a = slice(k * TOK + t * P, k * TOK + (t + 1) * P)
                        ws = slice(k * 384, (k + 1) * 384)
                        ins = parts(PS[4 - 2 * n + t][:, 0:384], KTH[:, a], KTL[:, a], WH[:, slot(c), ws],
                                    WL[:, slot(c), ws], k == 0, k == 2)
                ins.then_inc(w_used, 1)
            turn_latent(7, LAT0 + Q_RANK, 2)

            def turn_queries(r, bank):
                for k in range(2):
                    for t in range(NT):
                        ins = nc.tensor.transpose(PS[bank][:, k * TOK + t * P:k * TOK + (t + 1) * P],
                                                  PROJ[:, t, (2 * r + k) * P:(2 * r + k + 1) * P], IDENT)
                ins.then_inc(swa_turned, 1)
            pe.wait_ge(swa_roped, 1)
            turn_queries(0, 6)
            tokens(g2_unit(1), 1)
            pe.wait_ge(g2_kept, 1)
            turn_queries(1, 0)
            pe.wait_ge(kdup_ok, 1)
            pe.wait_ge(swa_kept, 1)
            for k in range(SWA_KV):
                for t in range(NT):
                    ins = nc.tensor.transpose(PS[6][:, k * TOK + t * P:k * TOK + (t + 1) * P],
                                              KDUP[:, t, k, :, :].rearrange("p u c -> p (u c)"), IDENT)
            ins.then_inc(swa_turned, 1)
            pe.wait_ge(lat_lo, 2)
            pe.wait_ge(q_kept, 4)
            rows(U_UKV, True, True, banks=2)
            pe.wait_ge(swa_kept, 2)
            tokens(g2_unit(2), 0)
            pe.wait_ge(swa_kept, 3)
            pe.wait_ge(kcat_ok, 1)
            pe.wait_ge(kv_kept, 4)
            for r in range(9):
                if r < 8:
                    if r:
                        pe.wait_ge(mla_kept, r)
                    for a, src in enumerate((QM, KM)):
                        for t in range(NT):
                            ins = nc.tensor.transpose(PS[7][0:MLA_QK, a * TOK + t * P:a * TOK + (t + 1) * P],
                                                      src[:, t, r, :], IDENT)
                    ins.then_inc(mla_turned, 1)
                if r:
                    pe.wait_ge(p2_exp, 2 * r)
                    if r >= 2:
                        pe.wait_ge(p2_kept, 2 * (r - 1))
                    for a in range(2):
                        for b in range(3):
                            ins = nc.tensor.transpose(PS[4 + a][:, b * P:(b + 1) * P], SC[a][:, b * P:(b + 1) * P],
                                                      IDENT)
                        ins.then_inc(p2_turned, 1)

                def score(a, qt, kt, r):
                    if r:
                        pe.wait_ge(s2_ready, 2 * (r - 1) + a + 1)
                    mm(PS[2 + a][:, 0:P], qt[:, 0:P], kt[:, 0:P], start=True, stop=True)
                    mm(PS[2 + a][:, P:3 * P], qt[:, P:TOK], kt[:, :], start=True, stop=True).then_inc(sc2, 1)
                if r < 8:
                    ms = slice((r % 2) * 64, (r % 2 + 1) * 64)
                    score(0, SQT[ms, r // 2, :], SKT[ms, r // 4, :], r)
                if r == 8:
                    pe.wait_ge(k_lo, 17)
                    pe.wait_ge(s2_ready, 2 * r)
                    rows(U_OSWA, True, False)
                if r:
                    h = r - 1
                    if r >= 2:
                        pe.wait_ge(o2_kept, r - 1)
                    for a in range(2):
                        pe.wait_ge(p2_kept, 2 * h + a + 1)
                        if a == 0:
                            v = PROJ[:, :, 640 + (h // 4) * HD:640 + (h // 4 + 1) * HD]
                        else:
                            v = V[:, :, h * P + NOPE:(h + 1) * P]
                        mm(PS[6][:, a * P:a * P + 64], PT2[a][:, 0:P], v[:, 0, :], start=True, stop=True)
                        mm(PS[6][:, a * P + 64:(a + 1) * P], PT2[a][:, P:2 * P], v[:, 0, :], start=True, stop=False)
                        ins = mm(PS[6][:, a * P + 64:(a + 1) * P], PT2[a][:, 2 * P:3 * P], v[:, 1, :], start=False,
                                 stop=True)
                    ins.then_inc(pv2, 1)
                if r < 8:
                    pe.wait_ge(mla_kept, r + 1)
                    score(1, QK[0:MLA_QK, r, 0, :], QK[0:MLA_QK, r, 1, :], r)
                    if r < 5:
                        pe.wait_ge(g2_kept, r + 2)
                        tokens(g2_unit(3 + r), (3 + r) % 2)
                    if r == 7:
                        turn_rows(16, XN, 0)
            pe.wait_ge(g2_kept, 8)
            pe.wait_ge(o2_kept, 8)
            turn_rows(17, XN, 2)
            for j in range(1, 4):
                if j < 3:
                    turn_rows(17 + j, XN, 2 * j + 2)
                pe.wait_ge(k_lo, 17 + j)
                rows(U_OSWA + j, j % 2 == 0, j % 2 == 1, half=j % 2, by_tile=(None, swa_half, None, branch_half)[j],
                     tile_free=(lambda t: pe.wait_ge(acc_read, 6 + 2 * t)) if j == 2 else None)
            products(20, U_OUT2, 4, V, ready=lambda j: pe.wait_ge(merged, 5 + min(3 + j, 5)), by_tile=acc_half)
            norm(4, U_FFN3, 4)
            ffn(2, U_FFN3)


_SQUEEZED = ["ffn1_pre_g", "mix_pre_g", "ffn2_pre_g", "mix_norm_g_2", "ffn_norm_g_2",
             "ffn1_w_gate", "ffn1_w_up", "ffn1_w_down", "ffn1_post_g", "w_in", "gate_b", "ssd_norm_g", "ssd_w_branch",
             "da_w_branch", "w_out", "mix_post_g", "ffn2_w_gate", "ffn2_w_up", "ffn2_w_down", "ffn2_post_g",
             "w_in_2", "w_uq_2", "w_ukv_2", "w_o_swa_2", "w_o_mla_2", "w_out_2", "w_gate_2", "w_up_2", "w_down_2"]


def kernel(**inputs):
    import concourse.bacc as bacc
    from concourse.bass_utils import run_bass_kernel_spmd

    v = {k: np.asarray(a) for k, a in inputs.items()}

    def tiles(a):
        return a.reshape(-1, P).T
    cols = [tiles(v[k][0]) for k in ("q_norm_g_2", "kv_norm_g_2", "da_subln_g", "ssd_conv_b")]
    cols += [tiles(v["ssd_conv_w"][0][k]) for k in range(CONV_K)]
    rows = [v[k][0] for k in ("ssd_dt_bias", "ssd_A_log", "ssd_D", "swa_sinks_2")]
    lam = [v[f"da_lambda_{k}"][0] for k in ("q1", "k1", "q2", "k2")]
    host = {"x": v["x"], "cols": np.concatenate(cols, 1), "rows": np.concatenate(rows), "lam": np.concatenate(lam),
            "tables": TABLES,
            "final_norm_g_2": v["final_norm_g_2"]}
    host.update({k: v[k][0] for k in _SQUEEZED})
    nc = bacc.Bacc("TRN2", target_bir_lowering=False, num_devices=1)
    arrays, aps = {}, {}
    for name, a in host.items():
        a = np.ascontiguousarray(a)
        arrays[f"in_{name}"] = a
        aps[name] = nc.dram_tensor(f"in_{name}", a.shape, mybir.dt.from_np(a.dtype), kind="ExternalInput").ap()
    out = nc.dram_tensor("out_x", (1, TOK, D), F32, kind="ExternalOutput").ap()
    program(nc, aps, out)
    r = run_bass_kernel_spmd(nc, [arrays], core_ids=[0])
    return r.results[0]["out_x"]
```
